# Optimizing a Trainium2 kernel written in Bass

```python
import jax, jax.numpy as jnp
from jax import lax
import numpy as np

D_MODEL = 1024
BATCH = 1
SEQ = 1024
DEPTH = 2
DEC_BATCH = 8
DEC_SEQ = 4
PAST_LEN = 256
PAGE_SIZE = 128

HEAD_DIM = 64
RET_HEADS = 6
RET_WIDTH = RET_HEADS * HEAD_DIM
SB_HEADS = 6
SB_WIDTH = SB_HEADS * HEAD_DIM
CONV_WIDTH = 256
CONV_K = 31
MIX_WIDTH = RET_WIDTH + SB_WIDTH + CONV_WIDTH
IN_WIDTH = 4 * RET_WIDTH + 4 * SB_WIDTH + 3 * CONV_WIDTH
RET_CHUNK = 128
SB_BLOCK = 128
SB_BIAS_INIT = -5.0
ROPE_BASE = 10000.0
EPS = 1e-6

kernel_name = 'hybrid_retention_stickbreak_conformer_step'

def rmsnorm(x, w):
    xf = x.astype(jnp.float32)
    y = xf * lax.rsqrt(jnp.mean(xf * xf, axis=-1, keepdims=True) + EPS)
    return (y * w.astype(jnp.float32)).astype(x.dtype)

def layernorm(x, w, b):
    xf = x.astype(jnp.float32)
    mu = jnp.mean(xf, axis=-1, keepdims=True)
    var = jnp.mean(jnp.square(xf - mu), axis=-1, keepdims=True)
    y = (xf - mu) * lax.rsqrt(var + EPS) * w.astype(jnp.float32) + b.astype(jnp.float32)
    return y.astype(x.dtype)

def head_groupnorm(o, w):
    B, T, H, d = o.shape
    of = o.astype(jnp.float32)
    mu = jnp.mean(of, axis=-1, keepdims=True)
    var = jnp.mean(jnp.square(of - mu), axis=-1, keepdims=True)
    y = ((of - mu) * lax.rsqrt(var + EPS)).reshape(B, T, H * d) * w.astype(jnp.float32)
    return y.astype(o.dtype)

def rope(x, pos):
    half = HEAD_DIM // 2
    inv = jnp.power(ROPE_BASE, -2.0 * jnp.arange(half, dtype=jnp.float32) / HEAD_DIM)
    ang = pos.astype(jnp.float32)[:, None] * inv[None, :]
    cos = jnp.cos(ang)[None, :, None, :]
    sin = jnp.sin(ang)[None, :, None, :]
    xf = x.astype(jnp.float32)
    x1, x2 = xf[..., :half], xf[..., half:]
    return jnp.concatenate([x1 * cos - x2 * sin, x1 * sin + x2 * cos], axis=-1).astype(x.dtype)

def retention(q, k, v, S0):
    B, T, H, d = q.shape
    dt = q.dtype
    C = RET_CHUNK if T % RET_CHUNK == 0 else T
    N = T // C
    lg = jnp.log(1.0 - jnp.power(2.0, -5.0 - jnp.arange(H, dtype=jnp.float32)))
    c = jnp.arange(C, dtype=jnp.float32)
    diff = c[:, None] - c[None, :]
    D = jnp.where(diff[None] >= 0, jnp.exp(jnp.maximum(diff, 0.0)[None] * lg[:, None, None]), 0.0).astype(dt)
    q_dec = jnp.exp((c[:, None] + 1.0) * lg[None, :]).astype(dt)
    k_dec = jnp.exp((C - 1.0 - c)[:, None] * lg[None, :]).astype(dt)
    c_dec = jnp.exp(C * lg).astype(dt)

    def to_chunks(a):
        return a.reshape(B, N, C, H, a.shape[-1]).transpose(1, 0, 2, 3, 4)

    def step(S, xs):
        qc, kc, vc = xs
        att = jnp.einsum('bchd,bshd->bhcs', qc, kc) * D[None]
        o = (jnp.einsum('bhcs,bshe->bche', att, vc)
             + jnp.einsum('bchd,bhde->bche', qc * q_dec[None, :, :, None], S))
        S = S * c_dec[None, :, None, None] + jnp.einsum('bchd,bche->bhde', kc * k_dec[None, :, :, None], vc)
        return S, o

    S, o = lax.scan(step, S0.astype(dt), (to_chunks(q), to_chunks(k), to_chunks(v)))
    o = o.transpose(1, 0, 2, 3, 4).reshape(B, T, H, v.shape[-1])
    return o, S

def stickbreak(q, k, v, bias, n_past):
    B, Tq, H, d = q.shape
    scale = d ** -0.5
    bf = bias.astype(jnp.float32)[None, :, None, None]
    outs = []
    for start in range(0, Tq, SB_BLOCK):
        end = min(start + SB_BLOCK, Tq)
        nk = n_past + end
        qb, kb, vb = q[:, start:end], k[:, :nk], v[:, :nk]
        qpos = n_past + jnp.arange(start, end)
        kpos = jnp.arange(nk)
        mask = kpos[None, :] < qpos[:, None]
        z = jnp.einsum('bqhd,bkhd->bhqk', qb, kb).astype(jnp.float32) * scale + bf
        log_stop = jnp.where(mask, jax.nn.log_sigmoid(-z), 0.0)
        after = lax.cumsum(log_stop, axis=3, reverse=True) - log_stop
        A = jnp.where(mask, jnp.exp(jax.nn.log_sigmoid(z) + after), 0.0)
        outs.append(jnp.einsum('bhqk,bkhd->bqhd', A.astype(v.dtype), vb))
    return jnp.concatenate(outs, axis=1)

def conv_module(a, b, buf, dw_w, dw_b, ln_w, ln_b, pw_w):
    u = a * jax.nn.sigmoid(b)
    full = jnp.concatenate([buf.astype(u.dtype), u], axis=1)
    y = lax.conv_general_dilated(full, dw_w.astype(u.dtype)[:, None, :], (1,), 'VALID',
                                 dimension_numbers=('NWC', 'WIO', 'NWC'),
                                 feature_group_count=u.shape[-1]) + dw_b
    y = jax.nn.silu(layernorm(y, ln_w, ln_b)) @ pw_w
    return y, full[:, -(CONV_K - 1):]

def mixer_layer(x, pos, S0, k_past, v_past, buf, n_past,
                norm_pre, w_in, ret_gn_w, sb_bias, dw_w, dw_b, ln_w, ln_b, pw_w, w_out, norm_post):
    B, T, _ = x.shape
    h = rmsnorm(x, norm_pre)
    p = h @ w_in
    sizes = [RET_WIDTH] * 4 + [SB_WIDTH] * 4 + [CONV_WIDTH] * 3
    idx = np.cumsum(sizes)[:-1].tolist()
    rq, rk, rv, rg, sq, sk, sv, sg, ca, cb, cg = jnp.split(p, idx, axis=-1)

    def heads(t):
        return t.reshape(B, T, -1, HEAD_DIM)

    rq = rope(heads(rq), pos)
    rk = rope(heads(rk), pos) * (HEAD_DIM ** -0.5)
    o_r, S = retention(rq, rk, heads(rv), S0)
    o_r = head_groupnorm(o_r, ret_gn_w) * jax.nn.silu(rg)

    sk_h, sv_h = heads(sk), heads(sv)
    if k_past is None:
        k_all, v_all = sk_h, sv_h
    else:
        k_all = jnp.concatenate([k_past.astype(sk_h.dtype), sk_h], axis=1)
        v_all = jnp.concatenate([v_past.astype(sv_h.dtype), sv_h], axis=1)
    o_s = stickbreak(heads(sq), k_all, v_all, sb_bias, n_past).reshape(B, T, SB_WIDTH) * jax.nn.silu(sg)

    o_c, buf_new = conv_module(ca, cb, buf, dw_w, dw_b, ln_w, ln_b, pw_w)
    o_c = o_c * jax.nn.silu(cg)

    y = jnp.concatenate([o_r, o_s, o_c], axis=-1) @ w_out
    return x + rmsnorm(y, norm_post), S, sk_h, sv_h, buf_new

def setup_inputs(seed: int = 0) -> dict:
    key = jax.random.key(seed)
    ks = jax.random.split(key, 20)
    n_pages = PAST_LEN // PAGE_SIZE
    n_used = DEC_BATCH * n_pages
    n_pool = n_used + n_used // 4
    f32 = jnp.float32
    nrm = lambda k, s: jax.random.normal(k, s, f32)
    page_table = jax.random.permutation(ks[0], n_pool)[:n_used].reshape(DEC_BATCH, n_pages).astype(jnp.int32)
    return {
        'x_prompt': nrm(ks[1], (BATCH, SEQ, D_MODEL)),
        'x_sample': nrm(ks[2], (DEC_BATCH, DEC_SEQ, D_MODEL)),
        'state_ret': nrm(ks[3], (DEPTH, DEC_BATCH, RET_HEADS, HEAD_DIM, HEAD_DIM)),
        'cache_k': nrm(ks[4], (DEPTH, n_pool, PAGE_SIZE, SB_HEADS, HEAD_DIM)),
        'cache_v': nrm(ks[5], (DEPTH, n_pool, PAGE_SIZE, SB_HEADS, HEAD_DIM)),
        'state_conv': 0.5 * nrm(ks[6], (DEPTH, DEC_BATCH, CONV_K - 1, CONV_WIDTH)),
        'page_table': page_table,
        'norm_pre': 1.0 + 0.05 * nrm(ks[7], (DEPTH, D_MODEL)),
        'w_in': nrm(ks[8], (DEPTH, D_MODEL, IN_WIDTH)) * D_MODEL ** -0.5,
        'ret_gn_w': 1.0 + 0.05 * nrm(ks[9], (DEPTH, RET_WIDTH)),
        'sb_bias': SB_BIAS_INIT + 0.1 * nrm(ks[17], (DEPTH, SB_HEADS)),
        'conv_dw_w': nrm(ks[10], (DEPTH, CONV_K, CONV_WIDTH)) * CONV_K ** -0.5,
        'conv_dw_b': 0.01 * nrm(ks[11], (DEPTH, CONV_WIDTH)),
        'conv_ln_w': 1.0 + 0.05 * nrm(ks[12], (DEPTH, CONV_WIDTH)),
        'conv_ln_b': 0.01 * nrm(ks[13], (DEPTH, CONV_WIDTH)),
        'conv_pw_w': nrm(ks[14], (DEPTH, CONV_WIDTH, CONV_WIDTH)) * CONV_WIDTH ** -0.5,
        'w_out': nrm(ks[15], (DEPTH, MIX_WIDTH, D_MODEL)) * MIX_WIDTH ** -0.5,
        'norm_post': 1.0 + 0.05 * nrm(ks[16], (DEPTH, D_MODEL)),
    }

def reference(x_prompt, x_sample, state_ret, cache_k, cache_v, state_conv, page_table,
              norm_pre, w_in, ret_gn_w, sb_bias, conv_dw_w, conv_dw_b, conv_ln_w, conv_ln_b,
              conv_pw_w, w_out, norm_post):
    Bp, Tp, _ = x_prompt.shape
    Bs, Ts, _ = x_sample.shape
    n_pages = page_table.shape[1]
    past_len = n_pages * cache_k.shape[2]
    pos_p = jnp.arange(Tp)
    pos_s = past_len + jnp.arange(Ts)
    xp, xs = x_prompt, x_sample
    ret_p, ret_s, kp_l, vp_l, ks_l, vs_l, cp_l, cs_l = [], [], [], [], [], [], [], []
    for l in range(DEPTH):
        w = (norm_pre[l], w_in[l], ret_gn_w[l], sb_bias[l], conv_dw_w[l], conv_dw_b[l],
             conv_ln_w[l], conv_ln_b[l], conv_pw_w[l], w_out[l], norm_post[l])
        S0p = jnp.zeros((Bp, RET_HEADS, HEAD_DIM, HEAD_DIM), xp.dtype)
        buf0p = jnp.zeros((Bp, CONV_K - 1, CONV_WIDTH), xp.dtype)
        xp, Sp, kp, vp, bp = mixer_layer(xp, pos_p, S0p, None, None, buf0p, 0, *w)
        k_past = cache_k[l][page_table].reshape(Bs, past_len, SB_HEADS, HEAD_DIM)
        v_past = cache_v[l][page_table].reshape(Bs, past_len, SB_HEADS, HEAD_DIM)
        xs, Ss, ksn, vsn, bs = mixer_layer(xs, pos_s, state_ret[l], k_past, v_past,
                                           state_conv[l], past_len, *w)
        ret_p.append(Sp); ret_s.append(Ss)
        kp_l.append(kp); vp_l.append(vp); ks_l.append(ksn); vs_l.append(vsn)
        cp_l.append(bp); cs_l.append(bs)
    return (xp, xs, jnp.stack(ret_p), jnp.stack(ret_s), jnp.stack(kp_l), jnp.stack(vp_l),
            jnp.stack(ks_l), jnp.stack(vs_l), jnp.stack(cp_l), jnp.stack(cs_l))


_drawn_inputs = setup_inputs


def setup_inputs(seed=0):
    import zlib

    import numpy as np

    out = dict(_drawn_inputs(seed))
    spreads = {}
    factors = {'sb_bias': 8.0, 'conv_dw_b': 5.37, 'conv_ln_b': 8.0}
    for name, (base, spread) in spreads.items():
        noise = np.random.default_rng([zlib.crc32(name.encode()), seed]).standard_normal(out[name].shape)
        drawn = base * np.exp(spread * noise) if base else spread * noise
        out[name] = __import__('jax').numpy.asarray(drawn.astype(out[name].dtype))
    for name, factor in factors.items():
        out[name] = (out[name] * factor).astype(out[name].dtype)
    return out
```

```python
from contextlib import ExitStack

import numpy as np
import concourse.bass as bass
from concourse import mybir

F32 = mybir.dt.float32
F32R = mybir.dt.float32r
BF16 = mybir.dt.bfloat16
I32 = mybir.dt.int32
ALU = mybir.AluOpType
ACT = mybir.ActivationFunctionType

D_MODEL, SEQ, DEPTH = 1024, 1024, 2
DEC_BATCH, DEC_SEQ, PAST_LEN, PAGE = 8, 4, 256, 128
HEAD_DIM, HEADS, CONV_W, CONV_K = 64, 6, 256, 31
N_PAGES = PAST_LEN // PAGE
N_POOL = DEC_BATCH * N_PAGES * 5 // 4
ROPE_BASE, EPS = 10000.0, 1e-6

P = 128
KB = D_MODEL // P
NS = DEC_BATCH * DEC_SEQ
NT = SEQ + NS
CH = 3
CW = NT // CH
QB = SEQ // P
LAST = NT - P
PAIRS = HEADS // 2
CB = CONV_W // P
HIST = CONV_K - 1

PROJ = (
    [("rq", 0), ("rk", 0), ("rv", 0), ("ca", 0), ("cb", 0), ("ca", 1), ("cb", 1)]
    + [("sq", 0), ("sk", 0), ("sv", 0), ("rq", 1), ("rk", 1), ("rv", 1), ("rg", 0)]
    + [("sq", 1), ("sk", 1), ("sv", 1), ("rq", 2), ("rk", 2), ("rv", 2), ("rg", 1)]
    + [("sq", 2), ("sk", 2), ("sv", 2), ("rg", 2), ("cg", 0), ("cg", 1), ("sg", 0), ("sg", 1), ("sg", 2)]
)
OUT = [("out", f) for f in range(KB)]
BLOCKS = PROJ + OUT
FIRST_COLUMN = {"rq": 0, "rk": 3, "rv": 6, "rg": 9, "sq": 12, "sk": 15, "sv": 18, "sg": 21, "ca": 24, "cb": 26, "cg": 28}
MIX_SLOT = {"r": 0, "s": PAIRS, "c": 2 * PAIRS}
GLU_SLOT = [2, 5]

UNITS = []
for kb in range(QB):
    width = SEQ - kb * P
    parts = -(-width // 512)
    for i in range(parts):
        UNITS.append((kb, kb * P + i * (width // parts), width // parts))

NEVER = -(2.0 ** 100)
E_MAX = 2.0 ** 62

C_ID, C_TRI, C_ONE, C_BLK, C_CH, C_ROT, C_CAUSAL, C_CAUSAL9, C_BATCH9, C_EPS = 0, 128, 256, 384, 512, 640, 768, 896, 928, 936
C_NEG = 937
C_ALL = C_NEG + P
D_Q, D_K, D_STEP, D_Q9, D_K9, D_STEP9 = 0, 128, 256, 384, 416, 544
D_ALL = 672
V_PRE, V_POST, V_GN, V_BIAS, V_DW, V_DWB, V_LNW, V_LNB, V_PW = 0, 8, 16, 19, 25, 87, 89, 91, 93
V_ALL = 93 + CB * CONV_W


def shape_constants():
    f = np.float32
    c = np.zeros((P, C_ALL), f)
    i = np.arange(P)
    c[:, C_ID:C_ID + P] = np.eye(P)
    c[:, C_TRI:C_TRI + P] = -(i[:, None] >= i[None, :]).astype(f)
    c[:, C_ONE:C_ONE + P] = 1.0
    c[:, C_BLK:C_BLK + P] = (i[:, None] // HEAD_DIM == i[None, :] // HEAD_DIM) / HEAD_DIM
    c[:, C_CH:C_CH + P] = 1.0 / CONV_W
    half = HEAD_DIM // 2
    for m in range(P):
        if m % HEAD_DIM < half:
            c[m + half, C_ROT + m] = -1.0
        else:
            c[m - half, C_ROT + m] = 1.0
    c[:, C_CAUSAL:C_CAUSAL + P] = i[:, None] <= i[None, :]
    row = i - (P - NS)
    col = np.arange(NS)
    own = (row[:, None] >= 0) & (row[:, None] // DEC_SEQ == col[None, :] // DEC_SEQ)
    c[:, C_CAUSAL9:C_CAUSAL9 + NS] = own & (row[:, None] <= col[None, :])
    c[:, C_BATCH9:C_BATCH9 + DEC_BATCH] = (row[:, None] >= 0) & (row[:, None] // DEC_SEQ == np.arange(DEC_BATCH)[None, :])
    c[:, C_EPS] = EPS
    c[:, C_NEG:C_NEG + P] = -1.0

    masks = np.zeros((P, P + 2 * NS), f)
    masks[:, :P] = np.where(i[:, None] < i[None, :], 0.0, NEVER)
    ok = own & (row[:, None] < col[None, :])
    ok = np.repeat(ok.reshape(P, DEC_BATCH, 1, DEC_SEQ), 2, axis=2).reshape(P, 2 * NS)
    masks[:, P:] = np.where(ok, 0.0, NEVER)

    inv = np.power(f(ROPE_BASE), (-2.0 * np.arange(half, dtype=f) / HEAD_DIM).astype(f)).astype(f)
    pos = np.concatenate([np.arange(SEQ), PAST_LEN + np.arange(NS) % DEC_SEQ]).astype(f)
    angle = (inv[i % half][:, None] * pos[None, :]).astype(f).astype(np.float64)
    turn = np.stack([np.cos(angle), np.sin(angle)], 1).astype(f)

    d = np.zeros((PAIRS, P, D_ALL), f)
    for p in range(PAIRS):
        lg = np.log(1.0 - 2.0 ** (-5.0 - (2 * p + i // HEAD_DIM)))[:, None]
        t = np.arange(P)[None, :]
        d[p, :, D_Q:D_Q + P] = np.exp((t + 1) * lg)
        d[p, :, D_K:D_K + P] = np.exp(-(t + 1) * lg) * HEAD_DIM ** -0.5
        same = i[:, None] // HEAD_DIM == i[None, :] // HEAD_DIM
        d[p, :, D_STEP:D_STEP + P] = np.exp(P * lg) * same
        d[p, :, D_Q9:D_Q9 + NS] = np.exp((col[None, :] % DEC_SEQ + 1) * lg)
        d[p, :, D_K9 + P - NS:D_K9 + P] = np.exp(-(col[None, :] % DEC_SEQ + 1) * lg) * HEAD_DIM ** -0.5
        d[p, :, D_STEP9:D_STEP9 + P] = np.exp(DEC_SEQ * lg) * same
    return c, masks.astype(mybir.dt.np(BF16)), turn, d


class Signal:

    def __init__(self, sem, counts):
        self.sem, self.counts, self.n = sem, counts, 0

    def mark(self, event, by=1):
        self.n += by
        self.counts[event] = self.n
        return by

    def alias(self, event):
        self.counts[event] = self.n

    def at(self, event):
        return self.counts.get(event, 1)


def schedule():
    index = {b: n for n, b in enumerate(BLOCKS)}

    def project(name, j):
        return [("proj", index[(name, j)], c) for c in range(CH)]

    def turned(name, p):
        a = project(name, p)
        return [a[0], a[1], ("rot", name, p, 0), a[2], ("rot", name, p, 1), ("rot", name, p, 2)]

    def values(name, p):
        return project(name, p) + [("vtok", name, p, j) for j in range(CH)]

    def retention_blocks(p):
        return turned("rq", p) + turned("rk", p) + values("rv", p)

    def between(main, filler):
        out, done = [], 0
        for n, group in enumerate(main):
            out += group
            upto = (n + 1) * len(filler) // len(main)
            out += filler[done:upto]
            done = upto
        return out

    taps = [("taps", s, min(s + 3, CONV_K)) for s in range(1, CONV_K, 3)]
    steps = [("stat", 0), ("stat", 1), ("norm", 0), ("stat", 2), ("norm", 1), ("norm", 2)]
    steps += retention_blocks(0)
    for b in range(CB):
        steps += project("ca", b) + project("cb", b)
    steps += [("glu_rest",)]
    for p in range(PAIRS):
        main = [[("att", p, n)] * (n <= QB) + [("ro", p, n - 1)] * (n > 0) for n in range(QB + 2)]
        filler = project("sq", p) + project("sk", p) + values("sv", p)
        if p == 0:
            filler = between([[x] for x in filler], taps)
        steps += between(main, filler)
        filler = []
        if p < PAIRS - 1:
            filler += retention_blocks(p + 1)
        filler += [("gn_mean", p, 0), ("gn_mean", p, 1), ("gn_var", p, 0), ("gn_mean", p, 2), ("gn_var", p, 1), ("gn_var", p, 2)]
        filler += project("rg", p)
        if p == 1:
            for c in range(CH):
                filler += [("ln_mean", c), ("ln_var", c)]
            filler += [("pw", c) for c in range(CH)]
        if p == PAIRS - 1:
            filler += project("cg", 0) + project("cg", 1) + project("sg", 0) + project("sg", 1)
        n = len(UNITS)
        main = [[("score", p, 0)]]
        for u in range(n):
            main.append([("score", p, u + 1)] if u + 1 < n else [])
            main.append([("stop", p, u)])
            main.append([("weigh", p, u)])
        late = 3 if p < PAIRS - 1 else 4
        steps += between(main, filler[:-late]) + [("sample_z", p)] + filler[-late:] + [("sample", p)]
    steps += project("sg", PAIRS - 1)
    steps += [("split", c) for c in range(CH)]
    for f in range(KB):
        steps += project("out", f)
    steps += [("post", c) for c in range(CH)]
    return steps


def build(nc, io, counts):
    STEPS = schedule()
    ctx = ExitStack()
    with ctx:
        def sb(name, shape, dt=F32):
            return ctx.enter_context(nc.sbuf_tensor(name, shape, dt))

        def bank(name):
            return ctx.enter_context(nc.psum_tensor(name, [P, 512], F32))

        sems = []

        def sig(name):
            sems.append(ctx.enter_context(nc.semaphore(name)))
            return Signal(sems[-1], counts.setdefault(name, {}))

        H_hi = sb("H_hi", [P, KB, NT], F32R)
        H_lo = sb("H_lo", [P, KB, NT], F32R)
        MX = sb("MX", [P, KB, NT])
        w_raw = sb("w_raw", [P, KB * P])
        w_hi = sb("w_hi", [P, 2, KB * P], F32R)
        w_lo = sb("w_lo", [P, 2, KB * P], F32R)
        const = sb("const", [P, C_ALL])
        masks = sb("masks_sb", [P, P + 2 * NS], BF16)
        ident_b = sb("ident_b", [P, P], BF16)
        turn = sb("turn_sb", [P, 2, NT])
        decay = sb("decay_sb", [P, D_ALL])
        vec = sb("vec_sb", [P, V_ALL])
        pages = sb("pages", [1, DEC_BATCH * N_PAGES], I32)
        ret_q = sb("ret_q", [P, NT])
        ret_k = sb("ret_k", [P, NT])
        ret_v = sb("ret_v", [P, QB + 1, P])
        v_rows = sb("v_rows_sb", [P, NT])
        sb_k = sb("sb_k", [P, NT])
        sb_q = sb("sb_q", [P, 2, NT])
        sb_v = sb("sb_v", [P, QB + 1, P])
        raw_rot = sb("raw_rot", [P, 2, CW])
        rot_a = sb("rot_a", [P, 2, CW])
        squares = sb("squares", [P, 2, CW])
        sigmoids = sb("sigmoids", [P, 2, CW])
        hx = sb("hx", [P, 2, CW])
        gated = hx
        rstd = sb("rstd", [P, 1, CW])
        sumsq = sb_k[:].rearrange("p (c n) -> p c n", c=CH)
        state = sb("state", [P, P])
        state9 = sb("state9", [P, DEC_BATCH, P])
        qd = sb("qd", [P, 2, P])
        kd = sb("kd", [P, 2, P])
        kd_tok = sb("kd_tok", [P, 2, P])
        att = sb("att", [P, 2, 2, P])
        stop = sb("stop", [P, 4, 512])
        weight = sb("weight", [P, 2, 512])
        v_own = weight[:, 0, :].rearrange("p (b e) -> p b e", b=DEC_BATCH // 2)
        keep = sb("keep", [P, 512])
        stop9 = sb("stop9", [P, 3, 2 * NS])
        weight9 = sb("weight9", [P, 3, 2 * NS])
        page = sb("page", [P, DEC_BATCH * N_PAGES, P])
        glu9 = sb("glu9", [P, CB, DEC_BATCH, HIST + DEC_SEQ])

        ring = [bank("ring0"), bank("ring1")]
        Z = [bank(f"Z{i}") for i in range(4)]
        TOT, AV = bank("TOT"), bank("AV")
        A2, KT, RO, DS = [Z[0], Z[1]], Z[2], Z[3], TOT

        def cc(a, n=P):
            return const[:, a:a + n]

        ident, negtri, ones, blk, ch_mean, rotm = (cc(a) for a in (C_ID, C_TRI, C_ONE, C_BLK, C_CH, C_ROT))
        causal, causal9, batch9, eps, negones = cc(C_CAUSAL), cc(C_CAUSAL9, NS), cc(C_BATCH9, DEC_BATCH), cc(C_EPS, 1), cc(C_NEG)

        def vv(a, n=1):
            return vec[:, a:a + n]

        pw = vec[:, V_PW:V_PW + CB * CONV_W].rearrange("p (k n) -> p k n", k=CB)

        def cs(c):
            return slice(c * CW, (c + 1) * CW)

        xs = [MX[:, k, :] for k in range(KB)]
        glu = [xs[k] for k in GLU_SLOT]
        conv = [xs[6 + b] for b in range(CB)]
        stick = [xs[PAIRS + p] for p in range(PAIRS)]
        U = len(UNITS)
        z9 = Z[0][:, 0:6 * NS]

        def of_head(a, h):
            return a.rearrange("p (g h t) -> p g h t", h=2, t=DEC_SEQ)[:, :, h, :]

        s_vec = sig("s_vec")
        s_decay = sig("s_decay")
        s_w = sig("s_w")
        s_state9 = sig("s_state9")
        s_pagek = sig("s_pagek")
        s_pagev = sig("s_pagev")
        s_hist = sig("s_hist")
        s_x = [sig("s_x0"), sig("s_x1")]
        s_out = sig("s_out")
        s_stout = sig("s_stout")
        s_vout = sig("s_vout")
        s_whi = sig("s_whi")
        s_wlo = sig("s_wlo")
        s_full = sig("s_full")
        s_sqa, s_sqv = sig("s_sqa"), sig("s_sqv")
        s_sqm = sig("s_sqm")
        s_ln, s_rstd = sig("s_ln"), sig("s_rstd")
        s_hx = sig("s_hx")
        s_hhi, s_hlo = sig("s_hhi"), sig("s_hlo")
        s_copy = sig("s_copy")
        s_sqo = sig("s_sqo")
        s_q = sig("s_q")
        s_rota = sig("s_rota")
        s_rotb = sig("s_rotb")
        s_rope = sig("s_rope")
        s_sig = sig("s_sig")
        s_glu = sig("s_glu")
        s_tap = sig("s_tap")
        s_mid = sig("s_mid")
        s_mix = sig("s_mix")
        s_gate = sig("s_gate")
        s_dec = sig("s_dec")
        s_att = sig("s_att")
        s_attm = sig("s_attm")
        s_kd = sig("s_kd")
        s_ro = sig("s_ro")
        s_roc = sig("s_roc")
        s_ds = sig("s_ds")
        s_st = sig("s_st")
        s_own = sig("s_own")
        s_z = sig("s_z")
        s_e = sig("s_e")
        s_min = sig("s_min")
        s_l = sig("s_l")
        s_sp = sig("s_sp")
        s_za = sig("s_za")
        s_tot = sig("s_tot")
        s_a = sig("s_a")
        s_keepf = sig("s_keepf")
        s_av = sig("s_av")
        s_kept = sig("s_kept")
        s_o = sig("s_o")

        s_load = ctx.enter_context(nc.semaphore("s_load"))
        s_zero = ctx.enter_context(nc.semaphore("s_zero"))
        s_keep = ctx.enter_context(nc.semaphore("s_keep"))
        with nc.Block() as block:
            @block.sync
            def _(sp):
                sp.dma_start(const[:], io["const"]).then_inc(s_load, 16)
                sp.dma_start(masks[:], io["masks"]).then_inc(s_load, 16)
                sp.dma_start(turn[:], io["turn"]).then_inc(s_load, 16)
                sp.dma_start(pages[:], io["page_table"]).then_inc(s_load, 16)
                sp.dma_start(MX[:], io["xT"]).then_inc(s_load, 16)
                sp.dma_start(io["yT"], io["xT"]).then_inc(s_keep, 16)
                sp.wait_ge(s_load, 16 * 5)
                sp.wait_ge(s_keep, 16)

            @block.vector
            def _(dve):
                nc.vector.memset(sb_q[:], 0.0).then_inc(s_zero, 1)
                dve.wait_ge(s_load, 16 * 5)
                nc.vector.tensor_copy(ident_b[:], ident).then_inc(s_zero, 1)
                dve.wait_ge(s_zero, 2)

        loop = ExitStack()
        l = loop.enter_context(nc.Fori(0, DEPTH))

        def of_layer(name, *more):
            a = io[name][bass.ds(l, 1)]
            names = "abcdef"[:len(a.shape) - 1]
            a = a.rearrange(f"z {' '.join(names)} -> (z {names[0]}) {' '.join(names[1:])}")
            for i in more:
                a = a[i]
            return a

        jobs = {}
        for step in STEPS:
            if step[0] in ("stat", "proj", "rot", "vtok", "gn_mean", "gn_var", "ln_mean", "ln_var", "post"):
                jobs[step] = len(jobs)
            if step[0] == "pw":
                for b in range(CB):
                    jobs[("pw", b, step[1])] = len(jobs)
        in_order = list(jobs)

        def in_ring(job):
            return ring[jobs[job] % 2][:, 0:CW]

        def drained(job):
            kind = job[0]
            if kind == "stat":
                return s_ln.sem, s_ln.at(("norm", job[1]))
            if kind == "proj":
                name = BLOCKS[job[1]][0]
                s = {"sq": s_q, "cb": s_sig, "rg": s_gate, "sg": s_gate, "cg": s_gate, "out": s_sqo}.get(name, s_copy)
                return s.sem, s.at(job)
            if kind == "rot":
                return s_rotb.sem, s_rotb.at(job)
            if kind in ("vtok", "pw"):
                return s_copy.sem, s_copy.at(job)
            if kind in ("gn_mean", "ln_mean"):
                return s_mid.sem, s_mid.at(job)
            return s_ln.sem, s_ln.at(job)

        def job_of(name, j, c):
            return ("proj", BLOCKS.index((name, j)), c)

        rot_uses = [s for s in STEPS if s[0] == "rot"]
        sq_uses, root_uses, sig_uses = [], [], []
        for step in STEPS:
            if step[0] == "stat":
                sq_uses += [("stat", step[1], k) for k in range(0, KB, 2)]
            if step[0] == "gn_mean":
                sq_uses += [("gn_var", step[1], step[2])]
            if step[0] == "ln_mean":
                sq_uses += [("ln_var", step[1], b) for b in range(CB)]
            if step[0] in ("norm", "gn_var", "ln_var", "post"):
                root_uses.append(step)
            if step[0] == "proj" and BLOCKS[step[1]][0] in ("cb", "rg", "sg", "cg"):
                sig_uses.append(step)
            if step[0] == "pw":
                sig_uses += [("ln_act", step[1], b) for b in range(CB)]
        gate_uses = [s for s in sig_uses if s[0] == "proj" and BLOCKS[s[1]][0] != "cb"]
        v_uses = [s for s in STEPS if s[0] == "vtok" and s[3] == CH - 1]

        layer = ExitStack()
        block = layer.enter_context(nc.Block())

        @block.sync
        def _(sp):
            def load_weights(i):
                if i < len(BLOCKS):
                    if i > 0:
                        sp.wait_ge(s_wlo.sem, s_wlo.at(i - 1))
                    sp.dma_start(w_raw[:], of_layer("w", i)).then_inc(s_w.sem, s_w.mark(i, 16))

            def load_pair(p):
                if p > 0:
                    sp.wait_ge(s_st.sem, s_st.at((p - 1, QB, 1)))
                    sp.wait_ge(s_dec.sem, s_dec.at((p - 1, QB)))
                    sp.wait_ge(s_stout.sem, s_stout.at(p - 1))
                sp.dma_start(decay[:], io["decay"][p]).then_inc(s_decay.sem, s_decay.mark(p, 16))
                sp.dma_start(state9[:], of_layer("state_ret", p)).then_inc(s_state9.sem, s_state9.mark(p, 16))

            def load_pages(p, name, s):
                for i in range(DEC_BATCH * N_PAGES):
                    at = sp.value_load(pages[0:1, i:i + 1], min_val=0, max_val=N_POOL - 1)
                    a = io[name][bass.ds(l, 1), bass.ds(at, 1), p]
                    sp.dma_start(page[:, i, :], a.rearrange("z y p n -> (z y p) n")).then_inc(s.sem, s.mark(p, 16))

            def store_y(m):
                c, k = divmod(m, KB)
                sp.wait_ge(s_mix.sem, s_mix.at(("new", m)))
                sp.dma_start(io["yT"][:, k, cs(c)], MX[:, k, cs(c)]).then_inc(s_out.sem, s_out.mark("all", 16))

            sp.dma_start(vec[:], of_layer("vec")).then_inc(s_vec.sem, s_vec.mark("vec", 16))
            load_weights(0)
            load_pair(0)
            sp.dma_start(glu9[:, :, :, 0:HIST], of_layer("state_conv")).then_inc(s_hist.sem, s_hist.mark("hist", 16))
            load_pages(0, "cache_k", s_pagek)
            for step in STEPS:
                kind = step[0]
                if kind == "proj" and step[2] == 0:
                    load_weights(step[1] + 1)
                elif kind == "glu_rest":
                    sp.wait_ge(s_glu.sem, s_glu.at("rest"))
                    sp.wait_ge(s_hist.sem, s_hist.at("hist"))
                    for b in range(CB):
                        sp.dma_start(of_layer("conv_p")[:, b], glu[b][:, SEQ - HIST:SEQ]).then_inc(s_out.sem, s_out.mark("conv", 16))
                    sp.dma_start(of_layer("conv_s"), glu9[:, :, :, DEC_SEQ:]).then_inc(s_out.sem, s_out.mark("conv", 16))
                elif kind == "vtok" and step[1] == "sv" and step[3] == 0:
                    p = step[2]
                    sp.wait_ge(s_copy.sem, s_copy.at(job_of("sv", p, CH - 1)))
                    sp.dma_start(of_layer("k_rows", p), sb_k[:]).then_inc(s_vout.sem, s_vout.mark(p, 16))
                    sp.dma_start(of_layer("v_rows", p), v_rows[:]).then_inc(s_vout.sem, s_vout.mark(p, 16))
                elif kind == "stop" and step[2] == 0:
                    p = step[1]
                    sp.wait_ge(s_st.sem, s_st.at((p, QB, 1)))
                    sp.dma_start(of_layer("state_p", p), state[:]).then_inc(s_stout.sem, s_stout.mark(p, 16))
                    sp.dma_start(of_layer("state_s", p), state9[:]).then_inc(s_stout.sem, s_stout.mark(p, 16))
                elif kind == "stop" and step[2] == 2 and step[1] < PAIRS - 1:
                    load_pair(step[1] + 1)
                elif kind == "sample_z":
                    sp.wait_ge(s_z.sem, s_z.at((step[1], "sample")))
                    load_pages(step[1], "cache_v", s_pagev)
                elif kind == "sample" and step[1] < PAIRS - 1:
                    sp.wait_ge(s_av.sem, s_av.at((step[1], "sample")))
                    load_pages(step[1] + 1, "cache_k", s_pagek)
                elif kind == "post":
                    for k in range(KB):
                        n = step[1] * KB + k
                        if n >= 2:
                            sp.wait_ge(s_mix.sem, s_mix.at(("new", n - 2)))
                        else:
                            sp.wait_ge(s_mix.sem, s_mix.at(gate_uses[-1]))
                        sp.dma_start(hx[:, n % 2, :], io["yT"][:, k, cs(step[1])]).then_inc(
                            s_x[n % 2].sem, s_x[n % 2].mark(n, 16))
                        if n >= 1:
                            store_y(n - 1)
            store_y(CH * KB - 1)
            sp.wait_ge(s_out.sem, s_out.at("all"))
            sp.wait_ge(s_stout.sem, s_stout.at(PAIRS - 1))
            sp.wait_ge(s_vout.sem, s_vout.at(PAIRS - 1))

        @block.tensor
        def _(pe):
            def claim(job):
                if jobs[job] >= 2:
                    pe.wait_ge(*drained(in_order[jobs[job] - 2]))

            for step in STEPS:
                kind = step[0]
                if kind == "stat":
                    c = step[1]
                    claim(step)
                    for k in range(KB):
                        s, t = (s_sqa, squares) if k % 2 == 0 else (s_sqv, hx)
                        pe.wait_ge(s.sem, s.at(("stat", c, k)))
                        nc.tensor.matmul(in_ring(step), ones, t[:, k // 2 % 2, :], start=(k == 0), stop=(k == KB - 1)).then_inc(
                            s_sqm.sem, s_sqm.mark(("stat", c, k)))
                elif kind == "proj":
                    i, c = step[1:]
                    claim(step)
                    if c == 0:
                        pe.wait_ge(s_wlo.sem, s_wlo.at(i))
                    if i == 0 or i == len(PROJ):
                        src = "norm" if i == 0 else "split"
                        pe.wait_ge(s_hlo.sem, s_hlo.at((src, c, KB - 1)))
                    for k in range(KB):
                        a, b = w_hi[:, i % 2, k * P:(k + 1) * P], w_lo[:, i % 2, k * P:(k + 1) * P]
                        x, y = H_hi[:, k, cs(c)], H_lo[:, k, cs(c)]
                        nc.tensor.matmul(in_ring(step), a, x, start=(k == 0), stop=False)
                        nc.tensor.matmul(in_ring(step), a, y, start=False, stop=False)
                        last = nc.tensor.matmul(in_ring(step), b, x, start=False, stop=(k == KB - 1))
                    last.then_inc(s_full.sem, s_full.mark(step))
                elif kind == "rot":
                    _, name, p, c = step
                    claim(step)
                    pe.wait_ge(s_copy.sem, s_copy.at(job_of(name, p, c)))
                    nc.tensor.matmul(in_ring(step), rotm, raw_rot[:, rot_uses.index(step) % 2, :], start=True, stop=True).then_inc(
                        s_full.sem, s_full.mark(step))
                elif kind == "vtok":
                    _, name, p, j = step
                    claim(step)
                    if j == 0:
                        pe.wait_ge(s_copy.sem, s_copy.at(job_of(name, p, CH - 1)))
                    for n in range(3 * j, 3 * j + 3):
                        t0 = n * P if n < QB else LAST
                        last = nc.tensor.transpose(ring[jobs[step] % 2][:, (n - 3 * j) * P:(n - 3 * j + 1) * P],
                                                   v_rows[:, t0:t0 + P], ident)
                    last.then_inc(s_full.sem, s_full.mark(step))
                elif kind == "att":
                    p, n = step[1:]
                    w = P if n < QB else NS
                    pe.wait_ge(s_dec.sem, s_dec.at((p, n)))
                    if n > 0:
                        pe.wait_ge(s_attm.sem, s_attm.at((p, n - 1)))
                        pe.wait_ge(s_kd.sem, s_kd.at((p, n - 1)))
                    elif p > 0:
                        pe.wait_ge(s_a.sem, s_a.at((p - 1, "sample")))
                        pe.wait_ge(s_keepf.sem, s_keepf.at((p - 1, U - 1)))
                    for h in range(2):
                        r = slice(64 * h, 64 * h + 64)
                        nc.tensor.matmul(A2[h][:, 0:w], kd[r, n % 2, :], qd[r, n % 2, 0:w], start=True, stop=True)
                    nc.tensor.transpose(KT[:, 0:P], kd[:, n % 2, :], ident).then_inc(s_att.sem, s_att.mark((p, n)))
                elif kind == "ro":
                    p, n = step[1:]
                    w = P if n < QB else NS
                    if n == 0:
                        pe.wait_ge(s_copy.sem, s_copy.at(("vtok", "rv", p, CH - 1)))
                    else:
                        pe.wait_ge(s_roc.sem, s_roc.at((p, n - 1)))
                        pe.wait_ge(s_st.sem, s_st.at((p, n - 1)))
                    if 0 < n < QB:
                        nc.tensor.matmul(RO[:, 0:P], state[:], qd[:, n % 2, :], start=True, stop=False, skip_group_check=True)
                    pe.wait_ge(s_attm.sem, s_attm.at((p, n)))
                    for h in range(2):
                        r = slice(64 * h, 64 * h + 64)
                        last = nc.tensor.matmul(RO[r, 0:w], ret_v[:, n, r], att[:, n % 2, h, 0:w],
                                                start=(n == 0 or n == QB), stop=(n < QB), skip_group_check=True)
                    if n == QB:
                        pe.wait_ge(s_state9.sem, s_state9.at(p))
                        for b in range(DEC_BATCH):
                            q = slice(b * DEC_SEQ, (b + 1) * DEC_SEQ)
                            last = nc.tensor.matmul(RO[:, q], state9[:, b, :], qd[:, n % 2, q], start=False,
                                                    stop=(b == DEC_BATCH - 1), skip_group_check=True)
                    last.then_inc(s_ro.sem, s_ro.mark((p, n)))
                    pe.wait_ge(s_kd.sem, s_kd.at((p, n)))
                    if n < QB:
                        nc.tensor.matmul(DS[:, 0:P], kd_tok[:, n % 2, :], ret_v[:, n, :], start=True, stop=True).then_inc(
                            s_ds.sem, s_ds.mark((p, n)))
                    else:
                        for g in range(2):
                            pe.wait_ge(s_own.sem, s_own.at((p, g)))
                            if g == 1:
                                pe.wait_ge(s_st.sem, s_st.at((p, QB, 0)))
                            nc.tensor.matmul(DS[:, :], kd_tok[:, n % 2, :], v_own[:].rearrange("p b e -> p (b e)"),
                                             start=True, stop=True).then_inc(s_ds.sem, s_ds.mark((p, n, g)))
                elif kind in ("gn_mean", "gn_var"):
                    _, p, c = step
                    claim(step)
                    if kind == "gn_mean":
                        pe.wait_ge(s_roc.sem, s_roc.at((p, QB)))
                        rhs = xs[p][:, cs(c)]
                    else:
                        pe.wait_ge(s_sqa.sem, s_sqa.at(step))
                        rhs = squares[:, sq_uses.index(step) % 2, :]
                    nc.tensor.matmul(in_ring(step), blk, rhs, start=True, stop=True).then_inc(s_full.sem, s_full.mark(step))
                elif kind in ("ln_mean", "ln_var"):
                    c = step[1]
                    claim(step)
                    for b in range(CB):
                        if kind == "ln_mean":
                            pe.wait_ge(s_tap.sem, s_tap.at(CONV_K - 1))
                            rhs = conv[b][:, cs(c)]
                        else:
                            pe.wait_ge(s_sqa.sem, s_sqa.at(("ln_var", c, b)))
                            rhs = squares[:, sq_uses.index(("ln_var", c, b)) % 2, :]
                        last = nc.tensor.matmul(in_ring(step), ch_mean, rhs, start=(b == 0), stop=(b == CB - 1))
                    last.then_inc(s_full.sem, s_full.mark(step))
                elif kind == "pw":
                    c = step[1]
                    pe.wait_ge(s_mid.sem, s_mid.at(("ln_act", c, CB - 1)))
                    for b in range(CB):
                        job = ("pw", b, c)
                        claim(job)
                        for k in range(CB):
                            last = nc.tensor.matmul(in_ring(job), pw[:, k, b * P:(b + 1) * P], conv[k][:, cs(c)],
                                                    start=(k == 0), stop=(k == CB - 1))
                        last.then_inc(s_full.sem, s_full.mark(job))
                elif kind == "score":
                    p, u = step[1:]
                    kb, q0, n = UNITS[u]
                    for h in range(2):
                        if u >= 2:
                            pe.wait_ge(s_a.sem, s_a.at((p, u - 2, h)))
                        elif h == 0 and u == 0:
                            pe.wait_ge(s_roc.sem, s_roc.at((p, QB)))
                            pe.wait_ge(s_kd.sem, s_kd.at((p, QB)))
                            pe.wait_ge(s_st.sem, s_st.at((p, QB, 1)))
                            pe.wait_ge(s_q.sem, s_q.at(job_of("sq", p, CH - 1)))
                            pe.wait_ge(s_copy.sem, s_copy.at(job_of("sk", p, CH - 1)))
                        bk = Z[2 * (u % 2) + h]
                        diagonal = q0 == kb * P
                        last = nc.tensor.matmul(bk[:, 0:n], sb_k[:, kb * P:(kb + 1) * P], sb_q[:, h, q0:q0 + n],
                                                start=True, stop=not diagonal, skip_group_check=True)
                        if diagonal:
                            last = nc.tensor.matmul(bk[:, 0:P], ident_b[:], masks[:, 0:P], start=False, stop=True,
                                                    skip_group_check=True)
                        last.then_inc(s_z.sem, s_z.mark((p, u, h)))
                elif kind == "stop":
                    p, u = step[1:]
                    kb, q0, n = UNITS[u]
                    for h in range(2):
                        pe.wait_ge(s_sp.sem, s_sp.at((p, u, h)))
                        nc.tensor.matmul(Z[2 * (u % 2) + h][:, 0:n], negtri, stop[:, (2 * u + h) % 4, 0:n], start=False,
                                         stop=True, skip_group_check=True).then_inc(s_za.sem, s_za.mark((p, u, h)))
                    if kb > 0:
                        if UNITS[u - 1][0] > 0:
                            pe.wait_ge(s_keepf.sem, s_keepf.at((p, u - 1)))
                        for h in range(2):
                            last = nc.tensor.matmul(TOT[64 * h:64 * h + 64, 0:n], ones[:, 0:64], stop[:, (2 * u + h) % 4, 0:n],
                                                    start=True, stop=True, skip_group_check=True)
                        last.then_inc(s_tot.sem, s_tot.mark((p, u)))
                elif kind == "weigh":
                    p, u = step[1:]
                    kb, q0, n = UNITS[u]
                    if u == 0:
                        pe.wait_ge(s_copy.sem, s_copy.at(("vtok", "sv", p, CH - 1)))
                        if p > 0:
                            pe.wait_ge(s_o.sem, s_o.at((p - 1, "sample")))
                    else:
                        pe.wait_ge(s_o.sem, s_o.at((p, u - 1)))
                    for h in range(2):
                        pe.wait_ge(s_a.sem, s_a.at((p, u, h)))
                        last = nc.tensor.matmul(AV[64 * h:64 * h + 64, 0:n], sb_v[:, kb, 64 * h:64 * h + 64],
                                                weight[:, h, 0:n], start=True, stop=True, skip_group_check=True)
                    last.then_inc(s_av.sem, s_av.mark((p, u)))
                elif kind in ("sample_z", "sample"):
                    p = step[1]
                    w = 2 * NS
                    zs = z9.rearrange("p (g b n) -> p g b n", g=3, b=DEC_BATCH)
                    q9 = sb_q[:, :, SEQ:NT].rearrange("p h (b t) -> p b h t", b=DEC_BATCH)
                    if kind == "sample_z":
                        pe.wait_ge(s_a.sem, s_a.at((p, U - 1, 1)))
                        pe.wait_ge(s_pagek.sem, s_pagek.at(p))
                        nc.tensor.matmul(z9[:, 2 * w:3 * w], sb_k[:, LAST:NT], q9, start=True, stop=False, skip_group_check=True)
                        nc.tensor.matmul(z9[:, 2 * w:3 * w], ident_b[:], masks[:, P:P + w], start=False, stop=False, skip_group_check=True)
                        for b in range(DEC_BATCH):
                            for g in range(N_PAGES):
                                last = nc.tensor.matmul(zs[:, g, b], page[:, b * N_PAGES + g, :], q9[:, b], start=False,
                                                        stop=False, skip_group_check=True)
                        last.then_inc(s_z.sem, s_z.mark((p, "sample")))
                        continue
                    pe.wait_ge(s_sp.sem, s_sp.at((p, "sample")))
                    s9 = stop9[:].rearrange("p g n -> p (g n)")
                    nc.tensor.matmul(z9, negtri, s9, start=False, stop=False, skip_group_check=True)
                    nc.tensor.matmul(z9[:, 0:2 * w], negones, s9[:, w:3 * w], start=False, stop=False, skip_group_check=True)
                    nc.tensor.matmul(z9[:, 0:w], negones, s9[:, 2 * w:3 * w], start=False, stop=True,
                                     skip_group_check=True).then_inc(s_za.sem, s_za.mark((p, "sample")))
                    pe.wait_ge(s_a.sem, s_a.at((p, "sample")))
                    pe.wait_ge(s_pagev.sem, s_pagev.at(p))
                    pe.wait_ge(s_o.sem, s_o.at((p, U - 1)))
                    nc.tensor.matmul(AV[:, 0:w], sb_v[:, QB, :], weight9[:, 2, :], start=True, stop=False, skip_group_check=True)
                    for b in range(DEC_BATCH):
                        for g in range(N_PAGES):
                            q = slice(b * 2 * DEC_SEQ, (b + 1) * 2 * DEC_SEQ)
                            last = nc.tensor.matmul(AV[:, q], page[:, b * N_PAGES + g, :], weight9[:, g, q],
                                                    start=False, stop=(b == DEC_BATCH - 1 and g == N_PAGES - 1), skip_group_check=True)
                    last.then_inc(s_av.sem, s_av.mark((p, "sample")))
                elif kind == "post":
                    claim(step)
                    pe.wait_ge(s_mid.sem, s_mid.at(("sum", KB - 1, step[1])))
                    nc.tensor.matmul(in_ring(step), ones, sumsq[:, step[1], :], start=True, stop=True).then_inc(
                        s_full.sem, s_full.mark(step))

        @block.scalar
        def _(act):
            def weights_hi(i):
                if i < len(BLOCKS):
                    act.wait_ge(s_w.sem, s_w.at(i))
                    if i >= 2:
                        act.wait_ge(s_full.sem, s_full.at(("proj", i - 2, CH - 1)))
                    nc.scalar.activation(w_hi[:, i % 2, :], w_raw[:], ACT.Copy).then_inc(s_whi.sem, s_whi.mark(i))

            def root(src, scale, use):
                n = root_uses.index(use)
                if n >= 1:
                    old = root_uses[n - 1]
                    if old[0] == "norm":
                        act.wait_ge(s_hx.sem, s_hx.at((old[1], KB - 1)))
                    else:
                        act.wait_ge(s_mid.sem, s_mid.at(("root", n - 1)))
                nc.scalar.activation(rstd[:, 0, :], src, ACT.Ln, bias=eps, scale=scale).then_inc(s_ln.sem, s_ln.mark(use))
                act.wait_ge(s_ln.sem, s_ln.at(use))
                nc.scalar.activation(rstd[:, 0, :], rstd[:, 0, :], ACT.Exp, scale=-0.5).then_inc(
                    s_rstd.sem, s_rstd.mark(use))

            def square(src, use):
                n = sq_uses.index(use)
                if n >= 2:
                    old = sq_uses[n - 2]
                    if old[0] == "stat":
                        act.wait_ge(s_sqm.sem, s_sqm.at(old))
                    else:
                        act.wait_ge(s_full.sem, s_full.at(old if old[0] == "gn_var" else old[:2]))
                nc.scalar.activation(squares[:, n % 2, :], src, ACT.Square).then_inc(s_sqa.sem, s_sqa.mark(use))

            def sigmoid(src, use, **affine):
                n = sig_uses.index(use)
                if n >= 2:
                    old = sig_uses[n - 2]
                    s = s_mid if old[0] == "ln_act" else (s_gate if BLOCKS[old[1]][0] != "cb" else s_glu)
                    act.wait_ge(s.sem, s.at(old))
                nc.scalar.activation(sigmoids[:, n % 2, :], src, ACT.Sigmoid, **affine).then_inc(s_sig.sem, s_sig.mark(use))

            def exp_scores(p, u):
                kb, q0, n = UNITS[u]
                if u >= 2:
                    act.wait_ge(s_za.sem, s_za.at((p, u - 2, 1)))
                    if UNITS[u - 2][0] > 0:
                        act.wait_ge(s_tot.sem, s_tot.at((p, u - 2)))
                elif p > 0:
                    act.wait_ge(s_tot.sem, s_tot.at((p - 1, U - 1)))
                for h in range(2):
                    act.wait_ge(s_z.sem, s_z.at((p, u, h)))
                    nc.scalar.activation(stop[:, (2 * u + h) % 4, 0:n], Z[2 * (u % 2) + h][:, 0:n], ACT.Exp,
                                         bias=vv(V_BIAS + 2 * p + h)).then_inc(s_e.sem, s_e.mark((p, u, h)))

            def ln_scores(p, u):
                n = UNITS[u][2]
                for h in range(2):
                    s = stop[:, (2 * u + h) % 4, 0:n]
                    act.wait_ge(s_min.sem, s_min.at((p, u, h)))
                    nc.scalar.activation(s, s, ACT.Ln, bias=1.0).then_inc(s_l.sem, s_l.mark((p, u, h)))

            act.wait_ge(s_vec.sem, s_vec.at("vec"))
            weights_hi(0)
            for step in STEPS:
                kind = step[0]
                if kind == "stat":
                    for k in range(0, KB, 2):
                        square(xs[k][:, cs(step[1])], ("stat", step[1], k))
                elif kind == "norm":
                    c = step[1]
                    act.wait_ge(s_sqm.sem, s_sqm.at(("stat", c, KB - 1)))
                    root(in_ring(("stat", c)), 1.0 / D_MODEL, step)
                    for k in range(KB):
                        act.wait_ge(s_hx.sem, s_hx.at((c, k)))
                        nc.scalar.activation(H_hi[:, k, cs(c)], hx[:, k % 2, :], ACT.Copy, scale=vv(V_PRE + k)).then_inc(
                            s_hhi.sem, s_hhi.mark(("norm", c, k)))
                elif kind == "proj":
                    i, c = step[1:]
                    name, j = BLOCKS[i]
                    if c == 0:
                        weights_hi(i + 1)
                    act.wait_ge(s_full.sem, s_full.at(step))
                    src = in_ring(step)
                    if name in ("rq", "rk"):
                        n = rot_uses.index(("rot", name, j, c))
                        if n >= 2:
                            act.wait_ge(s_rope.sem, s_rope.at(rot_uses[n - 2]))
                        nc.scalar.activation(raw_rot[:, n % 2, :], src, ACT.Copy).then_inc(s_copy.sem, s_copy.mark(step))
                    elif name in ("rv", "sv"):
                        n = v_uses.index(("vtok", name, j, CH - 1))
                        if c == 0 and n > 0:
                            act.wait_ge(s_full.sem, s_full.at(v_uses[n - 1]))
                            if name == "rv":
                                act.wait_ge(s_vout.sem, s_vout.at(j - 1))
                        nc.scalar.activation(v_rows[:, cs(c)], src, ACT.Copy).then_inc(s_copy.sem, s_copy.mark(step))
                    elif name == "sk":
                        if j > 0 and c == 0:
                            act.wait_ge(s_z.sem, s_z.at((j - 1, "sample")))
                            act.wait_ge(s_vout.sem, s_vout.at(j - 1))
                        nc.scalar.activation(sb_k[:, cs(c)], src, ACT.Copy).then_inc(s_copy.sem, s_copy.mark(step))
                    elif name == "ca":
                        act.wait_ge(s_hx.sem, s_hx.at((CH - 1, KB - 1)))
                        nc.scalar.activation(glu[j][:, cs(c)], src, ACT.Copy).then_inc(s_copy.sem, s_copy.mark(step))
                    elif name in ("cb", "rg", "sg", "cg"):
                        sigmoid(src, step)
                    elif name == "out":
                        nc.scalar.activation(xs[j][:, cs(c)], src, ACT.Copy).then_inc(s_copy.sem, s_copy.mark(step))
                        if 3 * j + c >= 2:
                            a, b = divmod(3 * j + c - 2, 3)
                            act.wait_ge(s_mid.sem, s_mid.at(("sum", a, b)))
                        else:
                            act.wait_ge(s_gate.sem, s_gate.at(job_of("sg", PAIRS - 1, CH - 1)))
                        nc.scalar.activation(squares[:, (3 * j + c) % 2, :], src, ACT.Square).then_inc(
                            s_sqo.sem, s_sqo.mark(step))
                elif kind == "vtok":
                    _, name, p, j = step
                    if p > 0 and j == 0:
                        if name == "rv":
                            act.wait_ge(s_ds.sem, s_ds.at((p - 1, QB, 1)))
                        else:
                            act.wait_ge(s_av.sem, s_av.at((p - 1, "sample")))
                    to = ret_v if name == "rv" else sb_v
                    act.wait_ge(s_full.sem, s_full.at(step))
                    nc.scalar.activation(to[:, 3 * j:3 * j + 3, :],
                                         ring[jobs[step] % 2][:, 0:3 * P].rearrange("p (n e) -> p n e", n=3),
                                         ACT.Copy).then_inc(s_copy.sem, s_copy.mark(step))
                elif kind == "att":
                    p, n = step[1:]
                    act.wait_ge(s_att.sem, s_att.at((p, n)))
                    if n >= 2:
                        act.wait_ge(s_ds.sem, s_ds.at((p, n - 2)))
                    elif p > 0:
                        act.wait_ge(s_ds.sem, s_ds.at((p - 1, QB, 1)))
                    nc.scalar.activation(kd_tok[:, n % 2, :], KT[:, 0:P], ACT.Copy).then_inc(s_kd.sem, s_kd.mark((p, n)))
                elif kind == "ro":
                    p, n = step[1:]
                    t0, w = (n * P, P) if n < QB else (SEQ, NS)
                    if p == GLU_SLOT[0]:
                        act.wait_ge(s_tap.sem, s_tap.at(CONV_K - 1))
                    act.wait_ge(s_hx.sem, s_hx.at((CH - 1, KB - 1)))
                    act.wait_ge(s_ro.sem, s_ro.at((p, n)))
                    nc.scalar.activation(xs[p][:, t0:t0 + w], RO[:, 0:w], ACT.Copy).then_inc(s_roc.sem, s_roc.mark((p, n)))
                elif kind == "gn_mean":
                    act.wait_ge(s_mid.sem, s_mid.at(step))
                    square(xs[step[1]][:, cs(step[2])], ("gn_var", step[1], step[2]))
                elif kind == "gn_var":
                    act.wait_ge(s_full.sem, s_full.at(step))
                    root(in_ring(step), 1.0, step)
                elif kind == "ln_mean":
                    for b in range(CB):
                        act.wait_ge(s_mid.sem, s_mid.at(step))
                        square(conv[b][:, cs(step[1])], ("ln_var", step[1], b))
                elif kind == "ln_var":
                    act.wait_ge(s_full.sem, s_full.at(step))
                    root(in_ring(step), 1.0, step)
                elif kind == "pw":
                    c = step[1]
                    for b in range(CB):
                        act.wait_ge(s_mid.sem, s_mid.at(("ln_n", c, b)))
                        sigmoid(conv[b][:, cs(c)], ("ln_act", c, b), scale=vv(V_LNW + b), bias=vv(V_LNB + b))
                    act.wait_ge(s_full.sem, s_full.at(("pw", CB - 1, c)))
                    for b in range(CB):
                        nc.scalar.activation(conv[b][:, cs(c)], in_ring(("pw", b, c)), ACT.Copy).then_inc(
                            s_copy.sem, s_copy.mark(("pw", b, c)))
                elif kind == "score":
                    p, u = step[1:]
                    exp_scores(p, u)
                    if u == 0:
                        ln_scores(p, u)
                elif kind == "weigh":
                    p, u = step[1:]
                    kb, q0, n = UNITS[u]
                    if u >= 1:
                        act.wait_ge(s_av.sem, s_av.at((p, u - 1)))
                    elif p > 0:
                        act.wait_ge(s_av.sem, s_av.at((p - 1, U - 1)))
                    for h in range(2):
                        act.wait_ge(s_za.sem, s_za.at((p, u, h)))
                        nc.scalar.activation(weight[:, h, 0:n], Z[2 * (u % 2) + h][:, 0:n], ACT.Exp,
                                             bias=vv(V_BIAS + 2 * p + h)).then_inc(s_a.sem, s_a.mark((p, u, h)))
                    if kb > 0:
                        act.wait_ge(s_tot.sem, s_tot.at((p, u)))
                        act.wait_ge(s_o.sem, s_o.at((p, u - 1)))
                        nc.scalar.activation(keep[:, 0:n], TOT[:, 0:n], ACT.Exp, scale=-1.0).then_inc(
                            s_keepf.sem, s_keepf.mark((p, u)))
                    if u + 1 < U:
                        ln_scores(p, u + 1)
                elif kind in ("sample_z", "sample"):
                    p = step[1]
                    name, to, ready, done = ("e", stop9, s_z, s_e) if kind == "sample_z" else ("a", weight9, s_za, s_a)
                    act.wait_ge(ready.sem, ready.at((p, "sample")))
                    if p > 0 and name == "a":
                        act.wait_ge(s_av.sem, s_av.at((p - 1, "sample")))
                    for h in range(2):
                        last = nc.scalar.activation(of_head(to[:].rearrange("p g n -> p (g n)"), h), of_head(z9, h), ACT.Exp,
                                                    bias=vv(V_BIAS + 2 * p + h))
                    last.then_inc(done.sem, done.mark((p, "sample")))
                    if name == "e":
                        act.wait_ge(s_min.sem, s_min.at((p, "sample")))
                        nc.scalar.activation(stop9[:], stop9[:], ACT.Ln, bias=1.0).then_inc(s_l.sem, s_l.mark((p, "sample")))
                elif kind == "split":
                    c = step[1]
                    act.wait_ge(s_full.sem, s_full.at(job_of("sg", PAIRS - 1, CH - 1)))
                    for k in range(KB):
                        g = job_of("rg", k, c) if k < PAIRS else (job_of("sg", k - PAIRS, c) if k < 2 * PAIRS else job_of("cg", k - 2 * PAIRS, c))
                        act.wait_ge(s_mix.sem, s_mix.at(g))
                        nc.scalar.activation(H_hi[:, k, cs(c)], xs[k][:, cs(c)], ACT.Copy).then_inc(
                            s_hhi.sem, s_hhi.mark(("split", c, k)))
                elif kind == "post":
                    act.wait_ge(s_full.sem, s_full.at(step))
                    root(in_ring(step), 1.0 / D_MODEL, step)

        @block.vector
        def _(dve):
            def softplus(p, u):
                n = UNITS[u][2]
                for h in range(2):
                    s = stop[:, (2 * u + h) % 4, 0:n]
                    dve.wait_ge(s_l.sem, s_l.at((p, u, h)))
                    nc.vector.scalar_tensor_tensor(out=s, in0=Z[2 * (u % 2) + h][:, 0:n], scalar=vv(V_BIAS + 2 * p + h), in1=s,
                                                   op0=ALU.add, op1=ALU.max).then_inc(s_sp.sem, s_sp.mark((p, u, h)))

            dve.wait_ge(s_vec.sem, s_vec.at("vec"))
            for step in STEPS:
                kind = step[0]
                if kind == "stat":
                    c = step[1]
                    if c == 2:
                        dve.wait_ge(s_hlo.sem, s_hlo.at(("norm", 0, KB - 1)))
                    for k in range(1, KB, 2):
                        if k >= 5 or c > 0:
                            old = (c, k - 4) if k >= 5 else (c - 1, k + 4)
                            dve.wait_ge(s_sqm.sem, s_sqm.at(("stat", *old)))
                        x = xs[k][:, cs(c)]
                        nc.vector.tensor_tensor(hx[:, k // 2 % 2, :], x, x, ALU.mult).then_inc(s_sqv.sem, s_sqv.mark(("stat", c, k)))
                elif kind == "norm":
                    c = step[1]
                    n = root_uses.index(step)
                    dve.wait_ge(s_rstd.sem, s_rstd.at(step))
                    if c == 0:
                        dve.wait_ge(s_sqm.sem, s_sqm.at(("stat", 1, KB - 1)))
                    for k in range(KB + 1):
                        if k < KB:
                            if k >= 2:
                                dve.wait_ge(s_hlo.sem, s_hlo.at(("norm", c, k - 2)))
                            elif c == 1:
                                dve.wait_ge(s_sqm.sem, s_sqm.at(("stat", 2, KB - 1)))
                            elif c > 0:
                                dve.wait_ge(s_hlo.sem, s_hlo.at(("norm", c - 1, k + 6)))
                            nc.vector.tensor_tensor(hx[:, k % 2, :], xs[k][:, cs(c)], rstd[:, 0, :], ALU.mult).then_inc(
                                s_hx.sem, s_hx.mark((c, k)))
                        if k > 0:
                            m = k - 1
                            dve.wait_ge(s_hhi.sem, s_hhi.at(("norm", c, m)))
                            nc.vector.scalar_tensor_tensor(out=H_lo[:, m, cs(c)], in0=hx[:, m % 2, :], scalar=vv(V_PRE + m),
                                                           in1=H_hi[:, m, cs(c)].bitcast(F32), op0=ALU.mult,
                                                           op1=ALU.subtract).then_inc(s_hlo.sem, s_hlo.mark(("norm", c, m)))
                elif kind == "proj":
                    i, c = step[1:]
                    name, j = BLOCKS[i]
                    src = in_ring(step)
                    if name == "sq":
                        if j > 0 and c == 0:
                            dve.wait_ge(s_z.sem, s_z.at((j - 1, "sample")))
                        dve.wait_ge(s_full.sem, s_full.at(step))
                        for h in range(2):
                            r = slice(64 * h, 64 * h + 64)
                            last = nc.vector.tensor_scalar(sb_q[r, h, cs(c)], src[r], HEAD_DIM ** -0.5, None, ALU.mult)
                        last.then_inc(s_q.sem, s_q.mark(step))
                    elif name == "cb":
                        dve.wait_ge(s_sig.sem, s_sig.at(step))
                        n = sig_uses.index(step)
                        nc.vector.tensor_tensor(glu[j][:, cs(c)], glu[j][:, cs(c)], sigmoids[:, n % 2, :], ALU.mult).then_inc(
                            s_glu.sem, s_glu.mark(step))
                    elif name in ("rg", "sg", "cg"):
                        dve.wait_ge(s_sig.sem, s_sig.at(step))
                        n, m = sig_uses.index(step), gate_uses.index(step)
                        if m >= 2:
                            dve.wait_ge(s_mix.sem, s_mix.at(gate_uses[m - 2]))
                        nc.vector.tensor_tensor(gated[:, m % 2, :], src, sigmoids[:, n % 2, :], ALU.mult).then_inc(
                            s_gate.sem, s_gate.mark(step))
                        dve.wait_ge(s_gate.sem, s_gate.at(step))
                        k = j + {"rg": 0, "sg": PAIRS, "cg": 2 * PAIRS}[name]
                        x = xs[k][:, cs(c)]
                        if name == "rg":
                            dve.wait_ge(s_mid.sem, s_mid.at(("gn_n", j, c)))
                            nc.vector.scalar_tensor_tensor(out=x, in0=x, scalar=vv(V_GN + j), in1=gated[:, m % 2, :],
                                                           op0=ALU.mult, op1=ALU.mult).then_inc(s_mix.sem, s_mix.mark(step))
                        else:
                            if name == "sg":
                                dve.wait_ge(s_o.sem, s_o.at((j, "sample")))
                            else:
                                dve.wait_ge(s_copy.sem, s_copy.at(("pw", j, c)))
                            nc.vector.tensor_tensor(x, x, gated[:, m % 2, :], ALU.mult).then_inc(s_mix.sem, s_mix.mark(step))
                    elif name == "out":
                        dve.wait_ge(s_sqo.sem, s_sqo.at(step))
                        s = squares[:, (3 * j + c) % 2, :]
                        if j == 0:
                            dve.wait_ge(s_z.sem, s_z.at((PAIRS - 1, "sample")))
                            dve.wait_ge(s_vout.sem, s_vout.at(PAIRS - 1))
                            nc.vector.tensor_copy(sumsq[:, c, :], s).then_inc(s_mid.sem, s_mid.mark(("sum", j, c)))
                        else:
                            dve.wait_ge(s_mid.sem, s_mid.at(("sum", j - 1, c)))
                            nc.vector.tensor_tensor(sumsq[:, c, :], sumsq[:, c, :], s, ALU.add).then_inc(
                                s_mid.sem, s_mid.mark(("sum", j, c)))
                elif kind == "rot":
                    _, name, p, c = step
                    n = rot_uses.index(step)
                    dve.wait_ge(s_full.sem, s_full.at(step))
                    dve.wait_ge(s_rota.sem, s_rota.at(step))
                    nc.vector.tensor_tensor(raw_rot[:, n % 2, :], in_ring(step), turn[:, 1, cs(c)], ALU.mult).then_inc(
                        s_rotb.sem, s_rotb.mark(step))
                    dve.wait_ge(s_rotb.sem, s_rotb.at(step))
                    if p > 0 and c == 0:
                        dve.wait_ge(s_dec.sem, s_dec.at((p - 1, QB)))
                    to = ret_q if name == "rq" else ret_k
                    nc.vector.tensor_tensor(to[:, cs(c)], rot_a[:, n % 2, :], raw_rot[:, n % 2, :], ALU.add).then_inc(
                        s_rope.sem, s_rope.mark(step))
                elif kind == "glu_rest":
                    dve.wait_ge(s_glu.sem, s_glu.at(job_of("cb", CB - 1, CH - 1)))
                    for b in range(CB):
                        last = nc.vector.tensor_copy(glu9[:, b, :, HIST:], glu[b][:, SEQ:NT].rearrange("p (b t) -> p b t", b=DEC_BATCH))
                    last.then_inc(s_glu.sem, s_glu.mark("rest"))
                    dve.wait_ge(s_glu.sem, s_glu.at("rest"))
                    for b in range(CB):
                        w = vv(V_DW + b * CONV_K + CONV_K - 1)
                        nc.vector.tensor_scalar(conv[b][:, 0:SEQ], glu[b][:, 0:SEQ], w, vv(V_DWB + b), ALU.mult, ALU.add)
                        last = nc.vector.tensor_scalar(conv[b][:, SEQ:NT].rearrange("p (b t) -> p b t", b=DEC_BATCH),
                                                       glu9[:, b, :, HIST:], w, vv(V_DWB + b), ALU.mult, ALU.add)
                        last.then_inc(s_tap.sem, s_tap.mark((0, b)))
                    dve.wait_ge(s_hist.sem, s_hist.at("hist"))
                elif kind == "taps":
                    for s in range(step[1], step[2]):
                        for b in range(CB):
                            w = vv(V_DW + b * CONV_K + CONV_K - 1 - s)
                            dve.wait_ge(s_tap.sem, s_tap.at((s - 1, b)))
                            y, y9 = conv[b][:, s:SEQ], conv[b][:, SEQ:NT].rearrange("p (b t) -> p b t", b=DEC_BATCH)
                            nc.vector.scalar_tensor_tensor(out=y, in0=glu[b][:, 0:SEQ - s], scalar=w, in1=y, op0=ALU.mult, op1=ALU.add)
                            last = nc.vector.scalar_tensor_tensor(out=y9, in0=glu9[:, b, :, HIST - s:HIST - s + DEC_SEQ], scalar=w,
                                                                  in1=y9, op0=ALU.mult, op1=ALU.add)
                            last.then_inc(s_tap.sem, s_tap.mark((s, b)))
                    if step[2] == CONV_K:
                        s_tap.alias(CONV_K - 1)
                elif kind == "att":
                    p, n = step[1:]
                    w = P if n < QB else NS
                    dve.wait_ge(s_att.sem, s_att.at((p, n)))
                    if n >= 2:
                        dve.wait_ge(s_ro.sem, s_ro.at((p, n - 2)))
                    elif p > 0:
                        dve.wait_ge(s_ro.sem, s_ro.at((p - 1, QB)))
                    for h in range(2):
                        last = nc.vector.tensor_tensor(att[:, n % 2, h, 0:w], A2[h][:, 0:w], causal if n < QB else causal9, ALU.mult)
                    last.then_inc(s_attm.sem, s_attm.mark((p, n)))
                elif kind == "ro":
                    p, n = step[1:]
                    if n == 0:
                        dve.wait_ge(s_decay.sem, s_decay.at(p))
                        if p > 0:
                            dve.wait_ge(s_stout.sem, s_stout.at(p - 1))
                        dve.wait_ge(s_ds.sem, s_ds.at((p, n)))
                        nc.vector.tensor_tensor(state[:], DS[:, 0:P], decay[:, D_STEP:D_STEP + P], ALU.mult).then_inc(
                            s_st.sem, s_st.mark((p, n)))
                    elif n < QB:
                        dve.wait_ge(s_ds.sem, s_ds.at((p, n)))
                        nc.vector.tensor_tensor(state[:], state[:], DS[:, 0:P], ALU.add).then_inc(s_st.sem, s_st.mark((p, n, "sum")))
                        dve.wait_ge(s_st.sem, s_st.at((p, n, "sum")))
                        nc.vector.tensor_tensor(state[:], state[:], decay[:, D_STEP:D_STEP + P], ALU.mult).then_inc(
                            s_st.sem, s_st.mark((p, n)))
                    else:
                        for g in range(2):
                            s = state9[:, 4 * g:4 * g + 4, :]
                            dve.wait_ge(s_ds.sem, s_ds.at((p, n, g)))
                            nc.vector.tensor_tensor(s, s, DS[:, :].rearrange("p (b e) -> p b e", b=4), ALU.add).then_inc(
                                s_st.sem, s_st.mark((p, n, g, "sum")))
                            dve.wait_ge(s_st.sem, s_st.at((p, n, g, "sum")))
                            step9 = decay[:, D_STEP9:D_STEP9 + P].unsqueeze(1).to_broadcast([P, 4, P])
                            nc.vector.tensor_tensor(s, s, step9, ALU.mult).then_inc(s_st.sem, s_st.mark((p, n, g)))
                elif kind == "gn_mean":
                    _, p, c = step
                    dve.wait_ge(s_full.sem, s_full.at(step))
                    nc.vector.tensor_tensor(xs[p][:, cs(c)], xs[p][:, cs(c)], in_ring(step), ALU.subtract).then_inc(
                        s_mid.sem, s_mid.mark(step))
                elif kind == "gn_var":
                    _, p, c = step
                    n = root_uses.index(step)
                    dve.wait_ge(s_rstd.sem, s_rstd.at(step))
                    dve.wait_ge(s_mid.sem, s_mid.at(("gn_mean", p, c)))
                    nc.vector.tensor_tensor(xs[p][:, cs(c)], xs[p][:, cs(c)], rstd[:, 0, :], ALU.mult).then_inc(
                        s_mid.sem, s_mid.mark(("gn_n", p, c)))
                    s_mid.alias(("root", n))
                elif kind == "ln_mean":
                    c = step[1]
                    dve.wait_ge(s_full.sem, s_full.at(step))
                    for b in range(CB):
                        last = nc.vector.tensor_tensor(conv[b][:, cs(c)], conv[b][:, cs(c)], in_ring(step), ALU.subtract)
                    last.then_inc(s_mid.sem, s_mid.mark(step))
                elif kind == "ln_var":
                    c = step[1]
                    n = root_uses.index(step)
                    dve.wait_ge(s_rstd.sem, s_rstd.at(step))
                    dve.wait_ge(s_mid.sem, s_mid.at(("ln_mean", c)))
                    for b in range(CB):
                        nc.vector.tensor_tensor(conv[b][:, cs(c)], conv[b][:, cs(c)], rstd[:, 0, :], ALU.mult).then_inc(
                            s_mid.sem, s_mid.mark(("ln_n", c, b)))
                    s_mid.alias(("root", n))
                elif kind == "pw":
                    c = step[1]
                    for b in range(CB):
                        x = conv[b][:, cs(c)]
                        dve.wait_ge(s_sig.sem, s_sig.at(("ln_act", c, b)))
                        nc.vector.tensor_scalar(x, x, vv(V_LNW + b), vv(V_LNB + b), ALU.mult, ALU.add).then_inc(
                            s_mid.sem, s_mid.mark(("ln_l", c, b)))
                        dve.wait_ge(s_mid.sem, s_mid.at(("ln_l", c, b)))
                        nc.vector.tensor_tensor(x, x, sigmoids[:, sig_uses.index(("ln_act", c, b)) % 2, :], ALU.mult).then_inc(
                            s_mid.sem, s_mid.mark(("ln_act", c, b)))
                elif kind == "score":
                    if step[2] == 0:
                        softplus(*step[1:])
                elif kind == "weigh":
                    p, u = step[1:]
                    kb, q0, n = UNITS[u]
                    if u + 1 < U:
                        softplus(p, u + 1)
                    o = stick[p][:, q0:q0 + n]
                    dve.wait_ge(s_av.sem, s_av.at((p, u)))
                    if kb == 0:
                        if p == 2:
                            dve.wait_ge(s_tap.sem, s_tap.at(CONV_K - 1))
                            dve.wait_ge(s_out.sem, s_out.at("conv"))
                        nc.vector.tensor_copy(o, AV[:, 0:n]).then_inc(s_o.sem, s_o.mark((p, u)))
                    else:
                        dve.wait_ge(s_keepf.sem, s_keepf.at((p, u)))
                        dve.wait_ge(s_o.sem, s_o.at((p, u - 1)))
                        nc.vector.tensor_tensor(o, o, keep[:, 0:n], ALU.mult).then_inc(s_kept.sem, s_kept.mark((p, u)))
                        dve.wait_ge(s_kept.sem, s_kept.at((p, u)))
                        nc.vector.tensor_tensor(o, o, AV[:, 0:n], ALU.add).then_inc(s_o.sem, s_o.mark((p, u)))
                elif kind == "sample_z":
                    p = step[1]
                    dve.wait_ge(s_l.sem, s_l.at((p, "sample")))
                    s9 = stop9[:].rearrange("p g n -> p (g n)")
                    for h in range(2):
                        last = nc.vector.scalar_tensor_tensor(out=of_head(s9, h), in0=of_head(z9, h), scalar=vv(V_BIAS + 2 * p + h),
                                                              in1=of_head(s9, h), op0=ALU.add, op1=ALU.max)
                    last.then_inc(s_sp.sem, s_sp.mark((p, "sample")))
                elif kind == "sample":
                    p = step[1]
                    dve.wait_ge(s_av.sem, s_av.at((p, "sample")))
                    for h in range(2):
                        r = slice(64 * h, 64 * h + 64)
                        last = nc.vector.tensor_copy(stick[p][r, SEQ:NT].rearrange("p (b t) -> p b t", b=DEC_BATCH),
                                                     of_head(AV[r, 0:2 * NS], h))
                    last.then_inc(s_o.sem, s_o.mark((p, "sample")))
                elif kind == "split":
                    c = step[1]
                    for k in range(KB):
                        dve.wait_ge(s_hhi.sem, s_hhi.at(("split", c, k)))
                        nc.vector.tensor_tensor(H_lo[:, k, cs(c)], xs[k][:, cs(c)], H_hi[:, k, cs(c)].bitcast(F32),
                                                ALU.subtract).then_inc(s_hlo.sem, s_hlo.mark(("split", c, k)))
                elif kind == "post":
                    c = step[1]
                    n = root_uses.index(step)
                    dve.wait_ge(s_rstd.sem, s_rstd.at(step))
                    for k in range(KB):
                        m = c * KB + k
                        x = xs[k][:, cs(c)]
                        nc.vector.scalar_tensor_tensor(out=x, in0=x, scalar=vv(V_POST + k), in1=rstd[:, 0, :], op0=ALU.mult,
                                                       op1=ALU.mult).then_inc(s_mid.sem, s_mid.mark(("post", c, k)))
                        dve.wait_ge(s_mid.sem, s_mid.at(("post", c, k)))
                        dve.wait_ge(s_x[m % 2].sem, s_x[m % 2].at(m))
                        nc.vector.tensor_tensor(x, x, hx[:, m % 2, :], ALU.add).then_inc(s_mix.sem, s_mix.mark(("new", m)))
                    s_mid.alias(("root", n))

        @block.gpsimd
        def _(pool):
            def weights_lo(i):
                if i < len(BLOCKS):
                    pool.wait_ge(s_whi.sem, s_whi.at(i))
                    if i >= 2:
                        pool.wait_ge(s_full.sem, s_full.at(("proj", i - 2, CH - 1)))
                    nc.gpsimd.tensor_tensor(w_lo[:, i % 2, :], w_raw[:], w_hi[:, i % 2, :].bitcast(F32), ALU.subtract).then_inc(
                        s_wlo.sem, s_wlo.mark(i))

            def decays(p, n):
                if n > QB:
                    return
                if n >= 2:
                    pool.wait_ge(s_ro.sem, s_ro.at((p, n - 2)))
                elif p > 0:
                    pool.wait_ge(s_ro.sem, s_ro.at((p - 1, QB)))
                a, b, w = (n * P, n * P, P) if n < QB else (SEQ, LAST, NS)
                dq, dk = (D_Q, D_K) if n < QB else (D_Q9, D_K9)
                nc.gpsimd.tensor_tensor(qd[:, n % 2, 0:w], ret_q[:, a:a + w], decay[:, dq:dq + w], ALU.mult)
                nc.gpsimd.tensor_tensor(kd[:, n % 2, :], ret_k[:, b:b + P], decay[:, dk:dk + P], ALU.mult).then_inc(
                    s_dec.sem, s_dec.mark((p, n)))

            weights_lo(0)
            for step in STEPS:
                kind = step[0]
                if kind == "proj":
                    i, c = step[1:]
                    name, j = BLOCKS[i]
                    if c == 0:
                        weights_lo(i + 1)
                    if name in ("rq", "rk"):
                        use = ("rot", name, j, c)
                        n = rot_uses.index(use)
                        if n >= 2:
                            pool.wait_ge(s_rope.sem, s_rope.at(rot_uses[n - 2]))
                        pool.wait_ge(s_copy.sem, s_copy.at(step))
                        nc.gpsimd.tensor_tensor(rot_a[:, n % 2, :], raw_rot[:, n % 2, :], turn[:, 0, cs(c)], ALU.mult).then_inc(
                            s_rota.sem, s_rota.mark(use))
                elif kind == "att":
                    p, n = step[1:]
                    if n == 0:
                        pool.wait_ge(s_decay.sem, s_decay.at(p))
                        pool.wait_ge(s_rope.sem, s_rope.at(("rot", "rk", p, CH - 1)))
                        decays(p, 0)
                    decays(p, n + 1)
                elif kind == "ro" and step[2] == QB:
                    p = step[1]
                    pool.wait_ge(s_copy.sem, s_copy.at(("vtok", "rv", p, CH - 1)))
                    for g in range(2):
                        if g == 0 and p > 0:
                            pool.wait_ge(s_av.sem, s_av.at((p - 1, U - 1)))
                        if g == 1:
                            pool.wait_ge(s_ds.sem, s_ds.at((p, QB, 0)))
                        elif p > 0:
                            pool.wait_ge(s_ds.sem, s_ds.at((p - 1, QB, 1)))
                        nc.gpsimd.tensor_tensor(v_own[:], ret_v[:, QB, :].unsqueeze(1).to_broadcast([P, 4, P]),
                                                batch9[:, 4 * g:4 * g + 4].unsqueeze(2).to_broadcast([P, 4, P]),
                                                ALU.mult).then_inc(s_own.sem, s_own.mark((p, g)))
                elif kind == "score":
                    p, u = step[1:]
                    n = UNITS[u][2]
                    for h in range(2):
                        s = stop[:, (2 * u + h) % 4, 0:n]
                        pool.wait_ge(s_e.sem, s_e.at((p, u, h)))
                        nc.gpsimd.tensor_scalar(s, s, E_MAX, None, ALU.min).then_inc(s_min.sem, s_min.mark((p, u, h)))
                elif kind == "sample_z":
                    p = step[1]
                    pool.wait_ge(s_e.sem, s_e.at((p, "sample")))
                    nc.gpsimd.tensor_scalar(stop9[:], stop9[:], E_MAX, None, ALU.min).then_inc(s_min.sem, s_min.mark((p, "sample")))

        layer.close()
        nums = [x.num for x in sems]
        assert sorted(nums) == list(range(min(nums), max(nums) + 1))
        nc.sync.sem_clear(range(min(nums), max(nums) + 1))
        nc.all_engine_barrier()
        loop.close()


def kernel(x_prompt, x_sample, state_ret, cache_k, cache_v, state_conv, page_table,
           norm_pre, w_in, ret_gn_w, sb_bias, conv_dw_w, conv_dw_b, conv_ln_w, conv_ln_b,
           conv_pw_w, w_out, norm_post):
    import concourse.bacc as bacc
    from concourse.bass_utils import run_bass_kernel_spmd

    L, B, D = DEPTH, DEC_BATCH, HEAD_DIM
    (x_prompt, x_sample, state_ret, cache_k, cache_v, state_conv, page_table, norm_pre, w_in, ret_gn_w, sb_bias,
     conv_dw_w, conv_dw_b, conv_ln_w, conv_ln_b, conv_pw_w, w_out, norm_post) = map(np.asarray, (
         x_prompt, x_sample, state_ret, cache_k, cache_v, state_conv, page_table, norm_pre, w_in, ret_gn_w, sb_bias,
         conv_dw_w, conv_dw_b, conv_ln_w, conv_ln_b, conv_pw_w, w_out, norm_post))

    def by_partition(a):
        return a.reshape(L, -1, P).transpose(0, 2, 1)

    x = np.concatenate([x_prompt.reshape(SEQ, D_MODEL), x_sample.reshape(NS, D_MODEL)])
    columns = [FIRST_COLUMN[name] + j for name, j in PROJ]
    w = np.concatenate([w_in.reshape(L, KB, P, -1, P)[:, :, :, columns], w_out.reshape(L, KB, P, KB, P)], 3)
    w = w.transpose(0, 3, 2, 1, 4).reshape(L, len(BLOCKS), P, KB * P)
    states = np.zeros((L, PAIRS, 2, D, B, 2, D), np.float32)
    s = state_ret.reshape(L, B, PAIRS, 2, D, D)
    for h in range(2):
        states[:, :, h, :, :, h, :] = s[:, :, :, h].transpose(0, 2, 3, 1, 4)
    vec = np.concatenate([
        by_partition(norm_pre), by_partition(norm_post), by_partition(ret_gn_w),
        np.broadcast_to(sb_bias[:, None, :], (L, P, HEADS)),
        conv_dw_w.reshape(L, CONV_K, CB, P).transpose(0, 3, 2, 1).reshape(L, P, CB * CONV_K),
        by_partition(conv_dw_b), by_partition(conv_ln_w), by_partition(conv_ln_b),
        conv_pw_w.reshape(L, CB, P, CONV_W).transpose(0, 2, 1, 3).reshape(L, P, CB * CONV_W),
    ], 2)
    const, masks, turn, decay = shape_constants()
    ins = {
        "xT": x.reshape(NT, KB, P).transpose(2, 1, 0),
        "w": w,
        "vec": vec,
        "state_ret": states.reshape(L, PAIRS, P, B, P),
        "state_conv": state_conv.reshape(L, B, HIST, CB, P).transpose(0, 4, 3, 1, 2),
        "cache_k": cache_k.reshape(L, N_POOL, PAGE, PAIRS, P).transpose(0, 1, 3, 4, 2),
        "cache_v": cache_v.reshape(L, N_POOL, PAGE, PAIRS, P).transpose(0, 1, 3, 2, 4),
        "page_table": page_table.reshape(1, B * N_PAGES),
        "const": const, "masks": masks, "turn": turn, "decay": decay,
    }
    ins = {k: np.ascontiguousarray(v) for k, v in ins.items()}
    outs = {
        "yT": (P, KB, NT), "state_p": (L, PAIRS, P, P), "state_s": (L, PAIRS, P, B, P),
        "k_rows": (L, PAIRS, P, NT), "v_rows": (L, PAIRS, P, NT),
        "conv_p": (L, P, CB, HIST), "conv_s": (L, P, CB, B, HIST),
    }

    def assemble(counts):
        nc = bacc.Bacc("TRN2", target_bir_lowering=False, num_devices=1, dynamic_dma_scratch_size=1024)
        io = {k: nc.dram_tensor(f"in_{k}", v.shape, mybir.dt.from_np(v.dtype), kind="ExternalInput").ap() for k, v in ins.items()}
        io |= {k: nc.dram_tensor(f"out_{k}", v, F32, kind="ExternalOutput").ap() for k, v in outs.items()}
        build(nc, io, counts)
        return nc

    counts = {}
    assemble(counts)
    nc = assemble(counts)
    r = run_bass_kernel_spmd(nc, [{f"in_{k}": v for k, v in ins.items()}], core_ids=[0]).results[0]
    got = {k: np.asarray(r[f"out_{k}"]) for k in outs}

    y = got["yT"].transpose(2, 1, 0).reshape(NT, D_MODEL)
    sp = got["state_p"].reshape(L, PAIRS, 2, D, 2, D)
    sp = np.stack([sp[:, :, h, :, h, :] for h in range(2)], 2).reshape(L, 1, HEADS, D, D)
    ss = got["state_s"].reshape(L, PAIRS, 2, D, B, 2, D)
    ss = np.stack([ss[:, :, h, :, :, h, :] for h in range(2)], 2)
    ss = ss.transpose(0, 4, 1, 2, 3, 5).reshape(L, B, HEADS, D, D)

    def rows(a):
        a = a.transpose(0, 3, 1, 2).reshape(L, NT, HEADS, D)
        return a[:, :SEQ].reshape(L, 1, SEQ, HEADS, D), a[:, SEQ:].reshape(L, B, DEC_SEQ, HEADS, D)

    kp, ks = rows(got["k_rows"])
    vp, vs = rows(got["v_rows"])
    cp = got["conv_p"].transpose(0, 3, 2, 1).reshape(L, 1, HIST, CONV_W)
    cv = got["conv_s"].transpose(0, 3, 4, 2, 1).reshape(L, B, HIST, CONV_W)
    return (y[:SEQ].reshape(1, SEQ, D_MODEL), y[SEQ:].reshape(B, DEC_SEQ, D_MODEL), sp, ss, kp, vp, ks, vs, cp, cv)
```

```python
from contextlib import ExitStack

import numpy as np
import concourse.bass as bass
from concourse import mybir

F32 = mybir.dt.float32
F32R = mybir.dt.float32r
BF16 = mybir.dt.bfloat16
I32 = mybir.dt.int32
ALU = mybir.AluOpType
ACT = mybir.ActivationFunctionType

D_MODEL, SEQ, DEPTH = 1024, 1024, 2
DEC_BATCH, DEC_SEQ, PAST_LEN, PAGE = 8, 4, 256, 128
HEAD_DIM, HEADS, CONV_W, CONV_K = 64, 6, 256, 31
N_PAGES = PAST_LEN // PAGE
N_POOL = DEC_BATCH * N_PAGES * 5 // 4
ROPE_BASE, EPS = 10000.0, 1e-6

P = 128
KB = D_MODEL // P
NS = DEC_BATCH * DEC_SEQ
NT = SEQ + NS
CH = 3
CW = NT // CH
QB = SEQ // P
LAST = NT - P
PAIRS = HEADS // 2
CB = CONV_W // P
HIST = CONV_K - 1

PROJ = [
    ("sq", 0), ("sk", 0), ("sv", 0), ("ca", 0), ("cb", 0), ("ca", 1), ("cb", 1), ("rq", 0), ("rk", 0), ("rv", 0),
    ("sq", 1), ("sk", 1), ("sv", 1), ("rq", 1), ("rk", 1), ("rv", 1), ("rg", 0), ("sg", 0), ("rg", 1),
    ("sq", 2), ("sk", 2), ("sv", 2), ("rq", 2), ("rk", 2), ("rv", 2), ("cg", 0), ("cg", 1), ("sg", 1), ("rg", 2), ("sg", 2),
]
OUT = [("out", f) for f in range(KB)]
BLOCKS = PROJ + OUT
FIRST_COLUMN = {"rq": 0, "rk": 3, "rv": 6, "rg": 9, "sq": 12, "sk": 15, "sv": 18, "sg": 21, "ca": 24, "cb": 26, "cg": 28}
MIX_SLOT = {"r": 0, "s": PAIRS, "c": 2 * PAIRS}
GLU_SLOT = [2, 5]

UNITS = []
for kb in range(QB):
    width = SEQ - kb * P
    parts = -(-width // 512)
    for i in range(parts):
        UNITS.append((kb, kb * P + i * (width // parts), width // parts))

NEVER = -(2.0 ** 100)
E_MAX = 2.0 ** 62

EXP_LN = "natural_log_exp_and_others"

C_ID, C_TRI, C_ONE, C_BLK, C_CH, C_ROT, C_CAUSAL, C_CAUSAL9, C_BATCH9, C_EPS = 0, 128, 256, 384, 512, 640, 768, 896, 928, 936
C_NEG = 937
C_ALL = C_NEG + P
D_Q, D_K, D_Q9, D_BOTH9, D_K9, D_STEP, D_STEP9 = 0, 256, 384, 448, 480, 608, 609
D_ALL = 610
V_PRE, V_POST, V_GN, V_BIAS, V_DW, V_DWB, V_LNW, V_LNB, V_PW = 0, 8, 16, 19, 25, 87, 89, 91, 93
V_ALL = 93 + CB * CONV_W


def shape_constants():
    f = np.float32
    c = np.zeros((P, C_ALL), f)
    i = np.arange(P)
    c[:, C_ID:C_ID + P] = np.eye(P)
    c[:, C_TRI:C_TRI + P] = -(i[:, None] >= i[None, :]).astype(f)
    c[:, C_ONE:C_ONE + P] = 1.0
    c[:, C_BLK:C_BLK + P] = (i[:, None] // HEAD_DIM == i[None, :] // HEAD_DIM) / HEAD_DIM
    c[:, C_CH:C_CH + P] = 1.0 / CONV_W
    half = HEAD_DIM // 2
    for m in range(P):
        if m % HEAD_DIM < half:
            c[m + half, C_ROT + m] = -1.0
        else:
            c[m - half, C_ROT + m] = 1.0
    c[:, C_CAUSAL:C_CAUSAL + P] = i[:, None] <= i[None, :]
    row = i - (P - NS)
    col = np.arange(NS)
    own = (row[:, None] >= 0) & (row[:, None] // DEC_SEQ == col[None, :] // DEC_SEQ)
    c[:, C_CAUSAL9:C_CAUSAL9 + NS] = own & (row[:, None] <= col[None, :])
    c[:, C_BATCH9:C_BATCH9 + DEC_BATCH] = (row[:, None] >= 0) & (row[:, None] // DEC_SEQ == np.arange(DEC_BATCH)[None, :])
    c[:, C_EPS] = EPS
    c[:, C_NEG:C_NEG + P] = -1.0

    masks = np.zeros((P, P + 2 * NS), f)
    masks[:, :P] = np.where(i[:, None] < i[None, :], 0.0, NEVER)
    ok = own & (row[:, None] < col[None, :])
    ok = np.repeat(ok.reshape(P, DEC_BATCH, 1, DEC_SEQ), 2, axis=2).reshape(P, 2 * NS)
    masks[:, P:] = np.where(ok, 0.0, NEVER)

    inv = np.power(f(ROPE_BASE), (-2.0 * np.arange(half, dtype=f) / HEAD_DIM).astype(f)).astype(f)
    pos = np.concatenate([np.arange(SEQ), PAST_LEN + np.arange(NS) % DEC_SEQ]).astype(f)
    angle = (inv[i % half][:, None] * pos[None, :]).astype(f).astype(np.float64)
    turn = np.stack([np.cos(angle), np.sin(angle)], 1).astype(f)

    d = np.zeros((PAIRS, P, D_ALL), f)
    for p in range(PAIRS):
        lg = np.log(1.0 - 2.0 ** (-5.0 - (2 * p + i // HEAD_DIM)))[:, None]
        t = np.arange(P)[None, :]
        q = np.exp((t + 1) * lg)
        q9 = np.exp((col[None, :] % DEC_SEQ + 1) * lg)
        for h in range(2):
            mine = i[:, None] // HEAD_DIM == h
            d[p, :, D_Q + h * P:D_Q + (h + 1) * P] = q * mine
            d[p, :, D_Q9 + h * NS:D_Q9 + (h + 1) * NS] = q9 * mine
        d[p, :, D_BOTH9:D_BOTH9 + NS] = q9
        d[p, :, D_K:D_K + P] = np.exp(-(t + 1) * lg) * HEAD_DIM ** -0.5
        d[p, :, D_K9 + P - NS:D_K9 + P] = np.exp(-(col[None, :] % DEC_SEQ + 1) * lg) * HEAD_DIM ** -0.5
        d[p, :, D_STEP] = np.exp(P * lg[:, 0]) * HEAD_DIM
        d[p, :, D_STEP9] = np.exp(DEC_SEQ * lg[:, 0]) * HEAD_DIM
    return c, masks.astype(mybir.dt.np(BF16)), turn, d


class Signal:

    def __init__(self, sem, counts, complete):
        self.sem, self.counts, self.complete, self.n = sem, counts, complete, 0

    def mark(self, event, by=1):
        self.n += by
        self.counts[event] = self.n
        return by

    def alias(self, event):
        self.counts[event] = self.n

    def at(self, event):
        return self.counts[event] if self.complete else 1


def schedule():
    index = {b: n for n, b in enumerate(BLOCKS)}

    def project(name, j):
        return [("proj", index[(name, j)], c) for c in range(CH)]

    def turned(name, p):
        a = project(name, p)
        return [a[0], a[1], ("rot", name, p, 0), a[2], ("rot", name, p, 1), ("rot", name, p, 2)]

    def values(name, p):
        return project(name, p) + [("vtok", name, p, j) for j in range(CH)]

    def retention_blocks(p):
        return turned("rq", p) + turned("rk", p) + values("rv", p)

    def stick_blocks(p):
        return project("sq", p) + project("sk", p) + values("sv", p)

    def retention(p):
        main = [[("att", p, n)] * (n <= QB) + [("ro", p, n - 1)] * (n > 0) for n in range(QB + 2)]
        return main + [[("ds9", p, 0)], [("ds9", p, 1)]]

    def group_norm(p):
        return [("gn_mean", p, 0), ("gn_mean", p, 1), ("gn_var", p, 0), ("gn_mean", p, 2), ("gn_var", p, 1), ("gn_var", p, 2)]

    def cost(step):
        return {"proj": 8, "taps": 2}.get(step[0], 1)

    def between(main, filler, weights=None):
        weights = weights or [1] * len(main)
        whole, out, done, spent, passed = sum(map(cost, filler)), [], 0, 0, 0
        for group, weight in zip(main, weights):
            out += group
            passed += weight
            while done < len(filler) and (spent + cost(filler[done]) / 2) * sum(weights) <= whole * passed:
                spent += cost(filler[done])
                out.append(filler[done])
                done += 1
        return out + filler[done:]

    taps = [("taps", s) for s in range(1, CONV_K)]
    conv_norm = []
    for c in range(CH):
        conv_norm += [("ln_mean", c), ("ln_var", c)]
    conv_norm += [("ln_act", b) for b in range(CB)] + [("pw", c) for c in range(CH)]

    fill = [
        project("ca", 0) + project("cb", 0) + project("ca", 1) + project("cb", 1) + [("glu_rest",)]
        + between([[x] for x in retention_blocks(0)], taps[:10]),
        between([[x] for x in retention_blocks(1)], taps[18:])
        + between(retention(1), group_norm(0) + project("rg", 0) + project("sg", 0)) + group_norm(1) + project("rg", 1),
        between([[x] for x in retention_blocks(2)], conv_norm)
        + between(retention(2), project("cg", 0) + project("cg", 1) + project("sg", 1)) + group_norm(2) + project("rg", 2),
    ]
    ahead = [[], between(retention(0), taps[10:18]), []]
    steps = [("norm", c) for c in range(CH)]
    for p in range(PAIRS):
        steps += between([[x] for x in stick_blocks(p)], ahead[p])
        main, weights = [[("score", p, 0)]], [2]
        for u, (_, _, width) in enumerate(UNITS):
            main.append([("score", p, u + 1)] if u + 1 < len(UNITS) else [])
            main.append([("stop", p, u)])
            main.append([("weigh", p, u)])
            weights += [2 + width / 256] * 3
        n = len(fill[p]) - (6 if p == 0 else 3)
        late = fill[p][n:]
        steps += between(main, fill[p][:n], weights)
        steps += [("sample_z", p)] + late[:2] + [("sample_t", p)] + late[2:3] + [("sample_v", p)] + late[3:]
    steps += project("sg", PAIRS - 1)
    steps += [("split", c) for c in range(CH)]
    for f in range(KB):
        steps += project("out", f)
    steps += [("post", c) for c in range(CH)]
    return steps


def build(nc, io, counts):
    complete = bool(counts)
    STEPS = schedule()
    ctx = ExitStack()
    with ctx:
        def sb(name, shape, dt=F32):
            return ctx.enter_context(nc.sbuf_tensor(name, shape, dt))

        def bank(name):
            return ctx.enter_context(nc.psum_tensor(name, [P, 512], F32))

        sems = []

        def sig(name):
            sems.append(ctx.enter_context(nc.semaphore(name)))
            return Signal(sems[-1], counts.setdefault(name, {}), complete)

        H_hi = sb("H_hi", [P, KB, NT], F32R)
        H_lo = sb("H_lo", [P, KB, NT], F32R)
        MX = sb("MX", [P, KB, NT])
        w_raw = sb("w_raw", [P, KB * P])
        w_hi = sb("w_hi", [P, 2, KB * P], F32R)
        w_lo = sb("w_lo", [P, 2, KB * P], F32R)
        const = sb("const", [P, C_ALL])
        masks = sb("masks_sb", [P, P + 2 * NS], BF16)
        ident_b = sb("ident_b", [P, P], BF16)
        turn = sb("turn_sb", [P, 2, NT])
        decay = sb("decay_sb", [P, D_ALL])
        vec = sb("vec_sb", [P, V_ALL])
        pages = sb("pages", [1, DEC_BATCH * N_PAGES], I32)
        ret_q = sb("ret_q", [P, NT])
        ret_k = sb("ret_k", [P, NT])
        ret_v = sb("ret_v", [P, QB + 1, P])
        v_rows = sb("v_rows_sb", [P, NT])
        sb_k = sb("sb_k", [P, NT])
        sb_q = sb("sb_q", [P, 2, NT])
        sb_v = sb("sb_v", [P, QB + 1, P])
        raw_rot = sb("raw_rot", [P, 2, CW])
        rot_a = sb("rot_a", [P, 2, CW])
        squares = sb("squares", [P, 2, CW])
        gate = sb("gate", [P, NT])
        hx = sb("hx", [P, 2, CW])
        rstd = sb("rstd", [P, 1, CW])
        sumsq = sb_k[:].rearrange("p (c n) -> p c n", c=CH)
        xsq = ret_q[:].rearrange("p (c n) -> p c n", c=CH)
        state = sb("state", [P, P])
        state9 = sb("state9", [P, DEC_BATCH, P])
        qd = sb("qd", [P, 2, 2, P])
        kd = sb("kd", [P, 2, P])
        kd_tok = sb("kd_tok", [P, 2, P])
        att = sb("att", [P, 2, 2, P])
        qd9 = att[:, QB % 2, 0, P - NS:P]
        stop = sb("stop", [P, 4, 512])
        weight = sb("weight", [P, 2, 512])
        v_own = hx[:].rearrange("p a n -> p (a n)")[:, 0:512].rearrange("p (b e) -> p b e", b=DEC_BATCH // 2)
        keep = sb("keep", [P, 512])
        stop9 = sb("stop9", [P, 3, 2 * NS])
        weight9 = stop9
        page = sb("page", [P, DEC_BATCH * N_PAGES, P])
        glu9 = sb("glu9", [P, CB, DEC_BATCH, HIST + DEC_SEQ])

        ring = [bank("ring0"), bank("ring1")]
        Z = [bank(f"Z{i}") for i in range(4)]
        TOT, AV = bank("TOT"), bank("AV")

        def cc(a, n=P):
            return const[:, a:a + n]

        ident, negtri, ones, blk, ch_mean, rotm = (cc(a) for a in (C_ID, C_TRI, C_ONE, C_BLK, C_CH, C_ROT))
        causal, causal9, batch9, eps, negones = cc(C_CAUSAL), cc(C_CAUSAL9, NS), cc(C_BATCH9, DEC_BATCH), cc(C_EPS, 1), cc(C_NEG)

        def vv(a, n=1):
            return vec[:, a:a + n]

        pw = vec[:, V_PW:V_PW + CB * CONV_W].rearrange("p (k n) -> p k n", k=CB)

        def cs(c):
            return slice(c * CW, (c + 1) * CW)

        xs = [MX[:, k, :] for k in range(KB)]
        glu = [xs[k] for k in GLU_SLOT]
        conv = [xs[6 + b] for b in range(CB)]
        stick = [xs[PAIRS + p] for p in range(PAIRS)]
        U = len(UNITS)
        z9 = Z[0][:, 0:6 * NS]

        def of_head(a, h):
            return a.rearrange("p (g h t) -> p g h t", h=2, t=DEC_SEQ)[:, :, h, :]

        s_vec = sig("s_vec")
        s_decay = sig("s_decay")
        s_w = sig("s_w")
        s_state9 = sig("s_state9")
        s_pagek = sig("s_pagek")
        s_pagev = sig("s_pagev")
        s_hist = sig("s_hist")
        s_x = [sig("s_x0"), sig("s_x1")]
        s_out = sig("s_out")
        s_stout = sig("s_stout")
        s_vout = sig("s_vout")
        s_whi = sig("s_whi")
        s_wlo = sig("s_wlo")
        s_full = sig("s_full")
        s_sqa = sig("s_sqa")
        s_xsq = sig("s_xsq")
        s_ln, s_rstd = sig("s_ln"), sig("s_rstd")
        s_hx = sig("s_hx")
        s_hhi, s_hlo = sig("s_hhi"), sig("s_hlo")
        s_scaled = sig("s_scaled")
        s_new = sig("s_new")
        s_copy = sig("s_copy")
        s_sqo = sig("s_sqo")
        s_q = sig("s_q")
        s_rota = sig("s_rota")
        s_rotb = sig("s_rotb")
        s_rope = sig("s_rope")
        s_sig = sig("s_sig")
        s_glu = sig("s_glu")
        s_tap = sig("s_tap")
        s_mid = sig("s_mid")
        s_mix = sig("s_mix")
        s_gate = sig("s_gate")
        s_dec = sig("s_dec")
        s_att = sig("s_att")
        s_attm = sig("s_attm")
        s_kd = sig("s_kd")
        s_ro = sig("s_ro")
        s_roc = sig("s_roc")
        s_ds = sig("s_ds")
        s_st = sig("s_st")
        s_own = sig("s_own")
        s_z = sig("s_z")
        s_e = sig("s_e")
        s_min = sig("s_min")
        s_l = sig("s_l")
        s_sp = sig("s_sp")
        s_za = sig("s_za")
        s_tot = sig("s_tot")
        s_a = sig("s_a")
        s_keepf = sig("s_keepf")
        s_av = sig("s_av")
        s_kept = sig("s_kept")
        s_o = sig("s_o")

        s_load = ctx.enter_context(nc.semaphore("s_load"))
        s_zero = ctx.enter_context(nc.semaphore("s_zero"))
        s_keep = ctx.enter_context(nc.semaphore("s_keep"))
        s_chunk = [ctx.enter_context(nc.semaphore(f"s_chunk{c}")) for c in range(CH)]
        s_first_square = ctx.enter_context(nc.semaphore("s_first_square"))
        s_first_sum = ctx.enter_context(nc.semaphore("s_first_sum"))
        with nc.Block() as block:
            @block.sync
            def _(sp):
                for c in range(CH):
                    sp.dma_start(MX[:, :, cs(c)], io["xT"][:, :, cs(c)]).then_inc(s_chunk[c], 16)
                sp.dma_start(const[:], io["const"]).then_inc(s_load, 16)
                sp.dma_start(masks[:], io["masks"]).then_inc(s_load, 16)
                sp.dma_start(turn[:], io["turn"]).then_inc(s_load, 16)
                sp.dma_start(pages[:], io["page_table"]).then_inc(s_load, 16)
                sp.dma_start(io["yT"], io["xT"]).then_inc(s_keep, 16)
                sp.wait_ge(s_load, 16 * 4)
                sp.wait_ge(s_keep, 16)

            @block.scalar
            def _(act):
                nc.scalar.preload_act_table_set(EXP_LN)
                for n in range(CH * KB):
                    c, k = divmod(n, KB)
                    if k == 0:
                        act.wait_ge(s_chunk[c], 16)
                    if n >= 2:
                        act.wait_ge(s_first_sum, n - 1)
                    nc.scalar.activation(squares[:, n % 2, :], xs[k][:, cs(c)], ACT.Square).then_inc(s_first_square, 1)

            @block.vector
            def _(dve):
                nc.vector.memset(sb_q[:], 0.0).then_inc(s_zero, 1)
                for n in range(CH * KB):
                    c, k = divmod(n, KB)
                    s = squares[:, n % 2, :]
                    dve.wait_ge(s_first_square, n + 1)
                    if k == 0:
                        nc.vector.tensor_copy(xsq[:, c, :], s).then_inc(s_first_sum, 1)
                    else:
                        dve.wait_ge(s_first_sum, n)
                        nc.vector.tensor_tensor(xsq[:, c, :], xsq[:, c, :], s, ALU.add).then_inc(s_first_sum, 1)
                dve.wait_ge(s_load, 16 * 4)
                nc.vector.tensor_copy(ident_b[:], ident).then_inc(s_zero, 1)
                dve.wait_ge(s_zero, 2)
                dve.wait_ge(s_first_sum, CH * KB)

        loop = ExitStack()
        l = loop.enter_context(nc.Fori(0, DEPTH))

        def of_layer(name, *more):
            a = io[name][bass.ds(l, 1)]
            names = "abcdef"[:len(a.shape) - 1]
            a = a.rearrange(f"z {' '.join(names)} -> (z {names[0]}) {' '.join(names[1:])}")
            for i in more:
                a = a[i]
            return a

        jobs = {}
        for step in STEPS:
            if step[0] in ("norm", "proj", "rot", "vtok", "att", "ro", "ds9", "gn_mean", "gn_var", "ln_mean", "ln_var", "post"):
                jobs[step] = len(jobs)
            if step[0] == "pw":
                for b in range(CB):
                    jobs[("pw", b, step[1])] = len(jobs)
        in_order = list(jobs)

        def in_ring(job):
            return ring[jobs[job] % 2][:, 0:CW]

        def bank_of(job):
            return ring[jobs[job] % 2]

        def scores_of(p, n, w):
            return bank_of(("att", p, n))[:, 0:2 * P].rearrange("p (h w) -> p h w", h=2)[:, :, 0:w]

        def turned_keys(p, n):
            return bank_of(("att", p, n))[:, 2 * P:3 * P]

        def outputs_of(p, n):
            return bank_of(("ro", p, n))[:, 0:P]

        def increment(p, n):
            return bank_of(("ro", p, n))[:, P:2 * P]

        def drained(job):
            kind = job[0]
            if kind == "norm":
                s = s_ln
            elif kind == "proj":
                name = BLOCKS[job[1]][0]
                s = {"sq": s_q, "rg": s_gate, "sg": s_gate, "cg": s_gate, "out": s_sqo}.get(name, s_copy)
            elif kind == "rot":
                s = s_rotb
            elif kind in ("vtok", "pw"):
                s = s_copy
            elif kind == "att":
                s, job = s_kd, job[1:]
            elif kind == "ro":
                s, job = s_roc, job[1:]
            elif kind == "ds9":
                s, job = s_st, (job[1], QB, job[2], "sum")
            elif kind in ("gn_mean", "ln_mean"):
                s = s_mid
            else:
                s = s_ln
            return s.sem, s.at(job)

        def job_of(name, j, c):
            return ("proj", BLOCKS.index((name, j)), c)

        rot_uses = [s for s in STEPS if s[0] == "rot"]
        sq_uses, root_uses, gate_uses = [], [], []
        for step in STEPS:
            if step[0] == "gn_mean":
                sq_uses += [("gn_var", step[1], step[2])]
            if step[0] == "ln_mean":
                sq_uses += [("ln_var", step[1], b) for b in range(CB)]
            if step[0] in ("norm", "gn_var", "ln_var", "post"):
                root_uses.append(step)
            if step[0] == "proj" and BLOCKS[step[1]][0] in ("cb", "rg", "sg", "cg") and step[2] == CH - 1:
                gate_uses.append(BLOCKS[step[1]])
            if step[0] == "ln_act":
                gate_uses.append(step)
        v_uses = [s for s in STEPS if s[0] == "vtok" and s[3] == CH - 1]

        layer = ExitStack()
        block = layer.enter_context(nc.Block())

        @block.sync
        def _(sp):
            def load_pair(p):
                if p > 0:
                    sp.wait_ge(s_st.sem, s_st.at((p - 1, QB, 1)))
                    sp.wait_ge(s_dec.sem, s_dec.at((p - 1, QB)))
                    sp.wait_ge(s_stout.sem, s_stout.at(p - 1))
                sp.dma_start(decay[:], io["decay"][p]).then_inc(s_decay.sem, s_decay.mark(p, 16))
                sp.dma_start(state9[:], of_layer("state_ret", p)).then_inc(s_state9.sem, s_state9.mark(p, 16))

            def load_pages(p, name, s):
                for i in range(DEC_BATCH * N_PAGES):
                    a = io[name][bass.ds(l, 1), bass.ds(page_ids[i], 1), p]
                    sp.dma_start(page[:, i, :], a.rearrange("z y p n -> (z y p) n")).then_inc(s.sem, s.mark(p, 16))

            def store_y(m):
                c, k = divmod(m, KB)
                sp.wait_ge(s_new.sem, s_new.at(m))
                sp.dma_start(io["yT"][:, k, cs(c)], MX[:, k, cs(c)]).then_inc(s_out.sem, s_out.mark("all", 16))

            sp.dma_start(vec[:], of_layer("vec")).then_inc(s_vec.sem, s_vec.mark("vec", 16))
            load_pair(0)
            page_ids = [sp.value_load(pages[0:1, i:i + 1], min_val=0, max_val=N_POOL - 1) for i in range(DEC_BATCH * N_PAGES)]
            sp.dma_start(glu9[:, :, :, 0:HIST], of_layer("state_conv")).then_inc(s_hist.sem, s_hist.mark("hist", 16))
            load_pages(0, "cache_k", s_pagek)
            for step in STEPS:
                kind = step[0]
                if kind == "glu_rest":
                    sp.wait_ge(s_glu.sem, s_glu.at("rest"))
                    sp.wait_ge(s_hist.sem, s_hist.at("hist"))
                    for b in range(CB):
                        sp.dma_start(of_layer("conv_p")[:, b], glu[b][:, SEQ - HIST:SEQ]).then_inc(s_out.sem, s_out.mark("conv", 16))
                    sp.dma_start(of_layer("conv_s"), glu9[:, :, :, DEC_SEQ:]).then_inc(s_out.sem, s_out.mark("conv", 16))
                elif kind == "vtok" and step[1] == "sv" and step[3] == 0:
                    p = step[2]
                    sp.wait_ge(s_copy.sem, s_copy.at(job_of("sv", p, CH - 1)))
                    sp.dma_start(of_layer("k_rows", p), sb_k[:]).then_inc(s_vout.sem, s_vout.mark(p, 16))
                    sp.dma_start(of_layer("v_rows", p), v_rows[:]).then_inc(s_vout.sem, s_vout.mark(p, 16))
                elif kind == "ds9" and step[2] == 1:
                    p = step[1]
                    sp.wait_ge(s_st.sem, s_st.at((p, QB, 1)))
                    sp.dma_start(of_layer("state_p", p), state[:]).then_inc(s_stout.sem, s_stout.mark(p, 16))
                    sp.dma_start(of_layer("state_s", p), state9[:]).then_inc(s_stout.sem, s_stout.mark(p, 16))
                    if p < PAIRS - 1:
                        load_pair(p + 1)
                elif kind == "sample_z":
                    sp.wait_ge(s_z.sem, s_z.at((step[1], "sample")))
                    load_pages(step[1], "cache_v", s_pagev)
                elif kind == "sample_v" and step[1] < PAIRS - 1:
                    sp.wait_ge(s_av.sem, s_av.at((step[1], "sample")))
                    load_pages(step[1] + 1, "cache_k", s_pagek)
                elif kind == "post":
                    for k in range(KB):
                        n = step[1] * KB + k
                        if n >= 2:
                            sp.wait_ge(s_new.sem, s_new.at(n - 2))
                        else:
                            sp.wait_ge(s_ds.sem, s_ds.at((PAIRS - 1, QB, 1)))
                        sp.dma_start(hx[:, n % 2, :], io["yT"][:, k, cs(step[1])]).then_inc(
                            s_x[n % 2].sem, s_x[n % 2].mark(n, 16))
                        if n >= 1:
                            store_y(n - 1)
            store_y(CH * KB - 1)
            sp.wait_ge(s_out.sem, s_out.at("all"))
            sp.wait_ge(s_stout.sem, s_stout.at(PAIRS - 1))
            sp.wait_ge(s_vout.sem, s_vout.at(PAIRS - 1))

        @block.tensor
        def _(pe):
            def claim(job):
                if jobs[job] >= 2:
                    pe.wait_ge(*drained(in_order[jobs[job] - 2]))

            for step in STEPS:
                kind = step[0]
                if kind == "norm":
                    claim(step)
                    nc.tensor.matmul(in_ring(step), ones, xsq[:, step[1], :], start=True, stop=True).then_inc(
                        s_full.sem, s_full.mark(step))
                elif kind == "proj":
                    i, c = step[1:]
                    claim(step)
                    if c == 0:
                        pe.wait_ge(s_wlo.sem, s_wlo.at(i))
                    if i == 0 or i == len(PROJ):
                        src = "norm" if i == 0 else "split"
                        pe.wait_ge(s_hlo.sem, s_hlo.at((src, c, KB - 1)))
                    for k in range(KB):
                        a, b = w_hi[:, i % 2, k * P:(k + 1) * P], w_lo[:, i % 2, k * P:(k + 1) * P]
                        x, y = H_hi[:, k, cs(c)], H_lo[:, k, cs(c)]
                        nc.tensor.matmul(in_ring(step), a, x, start=(k == 0), stop=False)
                        nc.tensor.matmul(in_ring(step), a, y, start=False, stop=False)
                        last = nc.tensor.matmul(in_ring(step), b, x, start=False, stop=(k == KB - 1))
                    last.then_inc(s_full.sem, s_full.mark(step))
                elif kind == "rot":
                    _, name, p, c = step
                    claim(step)
                    pe.wait_ge(s_copy.sem, s_copy.at(job_of(name, p, c)))
                    nc.tensor.matmul(in_ring(step), rotm, raw_rot[:, rot_uses.index(step) % 2, :], start=True, stop=True).then_inc(
                        s_full.sem, s_full.mark(step))
                elif kind == "vtok":
                    _, name, p, j = step
                    claim(step)
                    if j == 0:
                        pe.wait_ge(s_copy.sem, s_copy.at(job_of(name, p, CH - 1)))
                    for n in range(3 * j, 3 * j + 3):
                        t0 = n * P if n < QB else LAST
                        last = nc.tensor.transpose(ring[jobs[step] % 2][:, (n - 3 * j) * P:(n - 3 * j + 1) * P],
                                                   v_rows[:, t0:t0 + P], ident)
                    last.then_inc(s_full.sem, s_full.mark(step))
                elif kind == "att":
                    p, n = step[1:]
                    w = P if n < QB else NS
                    claim(step)
                    pe.wait_ge(s_dec.sem, s_dec.at((p, n)))
                    nc.tensor.matmul(scores_of(p, n, w), kd[:, n % 2, :], qd[:, n % 2, :, 0:w], start=True, stop=True,
                                     skip_group_check=True)
                    nc.tensor.transpose(turned_keys(p, n), kd[:, n % 2, :], ident).then_inc(s_att.sem, s_att.mark((p, n)))
                elif kind == "ro":
                    p, n = step[1:]
                    w = P if n < QB else NS
                    claim(step)
                    if n == 0:
                        pe.wait_ge(s_copy.sem, s_copy.at(("vtok", "rv", p, CH - 1)))
                    else:
                        pe.wait_ge(s_st.sem, s_st.at((p, n - 1)))
                    out = outputs_of(p, n)
                    if 0 < n < QB:
                        for h in range(2):
                            nc.tensor.matmul(out, state[:], qd[:, n % 2, h, :], start=(h == 0), stop=False, skip_group_check=True)
                    pe.wait_ge(s_attm.sem, s_attm.at((p, n)))
                    for h in range(2):
                        r = slice(64 * h, 64 * h + 64)
                        last = nc.tensor.matmul(out[r, 0:w], ret_v[:, n, r], att[:, n % 2, h, 0:w],
                                                start=(n == 0 or n == QB), stop=(n < QB), skip_group_check=True)
                    if n == QB:
                        pe.wait_ge(s_state9.sem, s_state9.at(p))
                        for b in range(DEC_BATCH):
                            q = slice(b * DEC_SEQ, (b + 1) * DEC_SEQ)
                            last = nc.tensor.matmul(out[:, q], state9[:, b, :], qd9[:, q], start=False,
                                                    stop=(b == DEC_BATCH - 1), skip_group_check=True)
                    last.then_inc(s_ro.sem, s_ro.mark((p, n)))
                    if n < QB:
                        pe.wait_ge(s_kd.sem, s_kd.at((p, n)))
                        nc.tensor.matmul(increment(p, n), kd_tok[:, n % 2, :], ret_v[:, n, :], start=True, stop=True,
                                         skip_group_check=True).then_inc(s_ds.sem, s_ds.mark((p, n)))
                elif kind == "ds9":
                    _, p, g = step
                    claim(step)
                    pe.wait_ge(s_kd.sem, s_kd.at((p, QB)))
                    pe.wait_ge(s_own.sem, s_own.at((p, g)))
                    nc.tensor.matmul(bank_of(step)[:, :], kd_tok[:, QB % 2, :], v_own[:].rearrange("p b e -> p (b e)"),
                                     start=True, stop=True).then_inc(s_ds.sem, s_ds.mark((p, QB, g)))
                elif kind in ("gn_mean", "gn_var"):
                    _, p, c = step
                    claim(step)
                    if kind == "gn_mean":
                        pe.wait_ge(s_roc.sem, s_roc.at((p, QB)))
                        rhs = xs[p][:, cs(c)]
                    else:
                        pe.wait_ge(s_sqa.sem, s_sqa.at(step))
                        rhs = squares[:, sq_uses.index(step) % 2, :]
                    nc.tensor.matmul(in_ring(step), blk, rhs, start=True, stop=True).then_inc(s_full.sem, s_full.mark(step))
                elif kind in ("ln_mean", "ln_var"):
                    c = step[1]
                    claim(step)
                    for b in range(CB):
                        if kind == "ln_mean":
                            pe.wait_ge(s_tap.sem, s_tap.at(CONV_K - 1))
                            rhs = conv[b][:, cs(c)]
                        else:
                            pe.wait_ge(s_sqa.sem, s_sqa.at(("ln_var", c, b)))
                            rhs = squares[:, sq_uses.index(("ln_var", c, b)) % 2, :]
                        last = nc.tensor.matmul(in_ring(step), ch_mean, rhs, start=(b == 0), stop=(b == CB - 1))
                    last.then_inc(s_full.sem, s_full.mark(step))
                elif kind == "pw":
                    c = step[1]
                    pe.wait_ge(s_mid.sem, s_mid.at(("ln_act", CB - 1)))
                    for b in range(CB):
                        job = ("pw", b, c)
                        claim(job)
                        for k in range(CB):
                            last = nc.tensor.matmul(in_ring(job), pw[:, k, b * P:(b + 1) * P], conv[k][:, cs(c)],
                                                    start=(k == 0), stop=(k == CB - 1))
                        last.then_inc(s_full.sem, s_full.mark(job))
                elif kind == "score":
                    p, u = step[1:]
                    kb, q0, n = UNITS[u]
                    for h in range(2):
                        if u >= 2:
                            pe.wait_ge(s_a.sem, s_a.at((p, u - 2, h)))
                        elif h == 0 and u == 0:
                            if p > 0:
                                pe.wait_ge(s_a.sem, s_a.at((p - 1, "sample")))
                            pe.wait_ge(s_q.sem, s_q.at(job_of("sq", p, CH - 1)))
                            pe.wait_ge(s_copy.sem, s_copy.at(job_of("sk", p, CH - 1)))
                        bk = Z[2 * (u % 2) + h]
                        diagonal = q0 == kb * P
                        last = nc.tensor.matmul(bk[:, 0:n], sb_k[:, kb * P:(kb + 1) * P], sb_q[:, h, q0:q0 + n],
                                                start=True, stop=not diagonal, skip_group_check=True)
                        if diagonal:
                            last = nc.tensor.matmul(bk[:, 0:P], ident_b[:], masks[:, 0:P], start=False, stop=True,
                                                    skip_group_check=True)
                        last.then_inc(s_z.sem, s_z.mark((p, u, h)))
                elif kind == "stop":
                    p, u = step[1:]
                    kb, q0, n = UNITS[u]
                    for h in range(2):
                        pe.wait_ge(s_sp.sem, s_sp.at((p, u, h)))
                        nc.tensor.matmul(Z[2 * (u % 2) + h][:, 0:n], negtri, stop[:, (2 * u + h) % 4, 0:n], start=False,
                                         stop=True, skip_group_check=True).then_inc(s_za.sem, s_za.mark((p, u, h)))
                    if kb > 0:
                        if UNITS[u - 1][0] > 0:
                            pe.wait_ge(s_keepf.sem, s_keepf.at((p, u - 1)))
                        elif p > 0:
                            pe.wait_ge(s_keepf.sem, s_keepf.at((p - 1, U - 1)))
                        for h in range(2):
                            last = nc.tensor.matmul(TOT[64 * h:64 * h + 64, 0:n], ones[:, 0:64], stop[:, (2 * u + h) % 4, 0:n],
                                                    start=True, stop=True, skip_group_check=True)
                        last.then_inc(s_tot.sem, s_tot.mark((p, u)))
                elif kind == "weigh":
                    p, u = step[1:]
                    kb, q0, n = UNITS[u]
                    if u == 0:
                        pe.wait_ge(s_copy.sem, s_copy.at(("vtok", "sv", p, CH - 1)))
                        if p > 0:
                            pe.wait_ge(s_o.sem, s_o.at((p - 1, "sample")))
                    else:
                        pe.wait_ge(s_o.sem, s_o.at((p, u - 1)))
                    for h in range(2):
                        pe.wait_ge(s_a.sem, s_a.at((p, u, h)))
                        last = nc.tensor.matmul(AV[64 * h:64 * h + 64, 0:n], sb_v[:, kb, 64 * h:64 * h + 64],
                                                weight[:, h, 0:n], start=True, stop=True, skip_group_check=True)
                    last.then_inc(s_av.sem, s_av.mark((p, u)))
                elif kind == "sample_z":
                    p = step[1]
                    w = 2 * NS
                    zs = z9.rearrange("p (g b n) -> p g b n", g=3, b=DEC_BATCH)
                    q9 = sb_q[:, :, SEQ:NT].rearrange("p h (b t) -> p b h t", b=DEC_BATCH)
                    pe.wait_ge(s_a.sem, s_a.at((p, U - 1, 1)))
                    pe.wait_ge(s_pagek.sem, s_pagek.at(p))
                    nc.tensor.matmul(z9[:, 2 * w:3 * w], sb_k[:, LAST:NT], q9, start=True, stop=False, skip_group_check=True)
                    nc.tensor.matmul(z9[:, 2 * w:3 * w], ident_b[:], masks[:, P:P + w], start=False, stop=False, skip_group_check=True)
                    for b in range(DEC_BATCH):
                        for g in range(N_PAGES):
                            last = nc.tensor.matmul(zs[:, g, b], page[:, b * N_PAGES + g, :], q9[:, b], start=False,
                                                    stop=False, skip_group_check=True)
                    last.then_inc(s_z.sem, s_z.mark((p, "sample")))
                elif kind == "sample_t":
                    p = step[1]
                    w = 2 * NS
                    pe.wait_ge(s_sp.sem, s_sp.at((p, "sample")))
                    s9 = stop9[:].rearrange("p g n -> p (g n)")
                    nc.tensor.matmul(z9, negtri, s9, start=False, stop=False, skip_group_check=True)
                    nc.tensor.matmul(z9[:, 0:2 * w], negones, s9[:, w:3 * w], start=False, stop=False, skip_group_check=True)
                    nc.tensor.matmul(z9[:, 0:w], negones, s9[:, 2 * w:3 * w], start=False, stop=True,
                                     skip_group_check=True).then_inc(s_za.sem, s_za.mark((p, "sample")))
                elif kind == "sample_v":
                    p = step[1]
                    w = 2 * NS
                    pe.wait_ge(s_a.sem, s_a.at((p, "sample")))
                    pe.wait_ge(s_pagev.sem, s_pagev.at(p))
                    pe.wait_ge(s_o.sem, s_o.at((p, U - 1)))
                    nc.tensor.matmul(AV[:, 0:w], sb_v[:, QB, :], weight9[:, 2, :], start=True, stop=False, skip_group_check=True)
                    for b in range(DEC_BATCH):
                        for g in range(N_PAGES):
                            q = slice(b * 2 * DEC_SEQ, (b + 1) * 2 * DEC_SEQ)
                            last = nc.tensor.matmul(AV[:, q], page[:, b * N_PAGES + g, :], weight9[:, g, q],
                                                    start=False, stop=(b == DEC_BATCH - 1 and g == N_PAGES - 1), skip_group_check=True)
                    last.then_inc(s_av.sem, s_av.mark((p, "sample")))
                elif kind == "post":
                    claim(step)
                    pe.wait_ge(s_mid.sem, s_mid.at(("sum", KB - 1, step[1])))
                    nc.tensor.matmul(in_ring(step), ones, sumsq[:, step[1], :], start=True, stop=True).then_inc(
                        s_full.sem, s_full.mark(step))

        @block.scalar
        def _(act):
            def load_weights(i):
                if i < len(BLOCKS):
                    if i > 0:
                        act.wait_ge(s_wlo.sem, s_wlo.at(i - 1))
                    act.dma_start(w_raw[:], of_layer("w", i)).then_inc(s_w.sem, s_w.mark(i, 16))

            def weights_hi(i):
                if i < len(BLOCKS):
                    act.wait_ge(s_w.sem, s_w.at(i))
                    if i >= 2:
                        act.wait_ge(s_full.sem, s_full.at(("proj", i - 2, CH - 1)))
                    nc.scalar.activation(w_hi[:, i % 2, :], w_raw[:], ACT.Copy).then_inc(s_whi.sem, s_whi.mark(i))

            def root(src, scale, use):
                n = root_uses.index(use)
                if n >= 1:
                    old = root_uses[n - 1]
                    if old[0] == "norm":
                        act.wait_ge(s_hx.sem, s_hx.at((old[1], KB - 1)))
                    elif old[0] == "post":
                        act.wait_ge(s_scaled.sem, s_scaled.at((old[1], KB - 1)))
                    else:
                        act.wait_ge(s_mid.sem, s_mid.at(("root", n - 1)))
                nc.scalar.activation(rstd[:, 0, :], src, ACT.Ln, bias=eps, scale=scale).then_inc(s_ln.sem, s_ln.mark(use))
                act.wait_ge(s_ln.sem, s_ln.at(use))
                nc.scalar.activation(rstd[:, 0, :], rstd[:, 0, :], ACT.Exp, scale=-0.5).then_inc(
                    s_rstd.sem, s_rstd.mark(use))

            def square(src, use):
                n = sq_uses.index(use)
                if n >= 2:
                    old = sq_uses[n - 2]
                    act.wait_ge(s_full.sem, s_full.at(old if old[0] == "gn_var" else old[:2]))
                nc.scalar.activation(squares[:, n % 2, :], src, ACT.Square).then_inc(s_sqa.sem, s_sqa.mark(use))

            def gate_free(use):
                n = gate_uses.index(use)
                if n >= 1:
                    old = gate_uses[n - 1]
                    s = s_mid if old[0] == "ln_act" else (s_glu if old[0] == "cb" else s_mix)
                    act.wait_ge(s.sem, s.at(old))

            def sigmoid(src, use, **affine):
                nc.scalar.activation(gate[:], src, ACT.Sigmoid, **affine).then_inc(s_sig.sem, s_sig.mark(use))
                nc.scalar.preload_act_table_set(EXP_LN)

            def exp_scores(p, u):
                kb, q0, n = UNITS[u]
                if u >= 2:
                    act.wait_ge(s_za.sem, s_za.at((p, u - 2, 1)))
                    if UNITS[u - 2][0] > 0:
                        act.wait_ge(s_tot.sem, s_tot.at((p, u - 2)))
                elif p > 0:
                    act.wait_ge(s_tot.sem, s_tot.at((p - 1, U - 1)))
                for h in range(2):
                    act.wait_ge(s_z.sem, s_z.at((p, u, h)))
                    nc.scalar.activation(stop[:, (2 * u + h) % 4, 0:n], Z[2 * (u % 2) + h][:, 0:n], ACT.Exp,
                                         bias=vv(V_BIAS + 2 * p + h)).then_inc(s_e.sem, s_e.mark((p, u, h)))

            def ln_scores(p, u):
                n = UNITS[u][2]
                for h in range(2):
                    s = stop[:, (2 * u + h) % 4, 0:n]
                    act.wait_ge(s_min.sem, s_min.at((p, u, h)))
                    nc.scalar.activation(s, s, ACT.Ln, bias=1.0).then_inc(s_l.sem, s_l.mark((p, u, h)))

            load_weights(0)
            act.wait_ge(s_vec.sem, s_vec.at("vec"))
            weights_hi(0)
            load_weights(1)
            for step in STEPS:
                kind = step[0]
                if kind == "norm":
                    c = step[1]
                    act.wait_ge(s_full.sem, s_full.at(step))
                    root(in_ring(step), 1.0 / D_MODEL, step)
                    for k in range(KB):
                        act.wait_ge(s_hx.sem, s_hx.at((c, k)))
                        nc.scalar.activation(H_hi[:, k, cs(c)], hx[:, k % 2, :], ACT.Copy).then_inc(
                            s_hhi.sem, s_hhi.mark(("norm", c, k)))
                elif kind == "proj":
                    i, c = step[1:]
                    name, j = BLOCKS[i]
                    if c == 0:
                        weights_hi(i + 1)
                    elif c == 2:
                        load_weights(i + 2)
                    act.wait_ge(s_full.sem, s_full.at(step))
                    src = in_ring(step)
                    if name in ("rq", "rk"):
                        n = rot_uses.index(("rot", name, j, c))
                        if n >= 2:
                            act.wait_ge(s_rope.sem, s_rope.at(rot_uses[n - 2]))
                        nc.scalar.activation(raw_rot[:, n % 2, :], src, ACT.Copy).then_inc(s_copy.sem, s_copy.mark(step))
                    elif name in ("rv", "sv"):
                        n = v_uses.index(("vtok", name, j, CH - 1))
                        if c == 0 and n > 0:
                            act.wait_ge(s_full.sem, s_full.at(v_uses[n - 1]))
                            if name == "rv":
                                act.wait_ge(s_vout.sem, s_vout.at(j))
                        nc.scalar.activation(v_rows[:, cs(c)], src, ACT.Copy).then_inc(s_copy.sem, s_copy.mark(step))
                    elif name == "sk":
                        if j > 0 and c == 0:
                            act.wait_ge(s_z.sem, s_z.at((j - 1, "sample")))
                            act.wait_ge(s_vout.sem, s_vout.at(j - 1))
                        nc.scalar.activation(sb_k[:, cs(c)], src, ACT.Copy).then_inc(s_copy.sem, s_copy.mark(step))
                    elif name == "ca":
                        act.wait_ge(s_hx.sem, s_hx.at((CH - 1, KB - 1)))
                        nc.scalar.activation(glu[j][:, cs(c)], src, ACT.Copy).then_inc(s_copy.sem, s_copy.mark(step))
                    elif name in ("cb", "rg", "sg", "cg"):
                        if c == 0:
                            gate_free((name, j))
                        nc.scalar.activation(gate[:, cs(c)], src, ACT.Copy).then_inc(s_copy.sem, s_copy.mark(step))
                        if c == CH - 1:
                            act.wait_ge(s_copy.sem, s_copy.at(step))
                            sigmoid(gate[:], (name, j))
                    elif name == "out":
                        nc.scalar.activation(xs[j][:, cs(c)], src, ACT.Copy).then_inc(s_copy.sem, s_copy.mark(step))
                        if 3 * j + c >= 2:
                            a, b = divmod(3 * j + c - 2, 3)
                            act.wait_ge(s_mid.sem, s_mid.at(("sum", a, b)))
                        else:
                            act.wait_ge(s_full.sem, s_full.at(("gn_var", PAIRS - 1, CH - 1)))
                        nc.scalar.activation(squares[:, (3 * j + c) % 2, :], src, ACT.Square).then_inc(
                            s_sqo.sem, s_sqo.mark(step))
                elif kind == "vtok":
                    _, name, p, j = step
                    if p > 0 and j == 0:
                        if name == "rv":
                            act.wait_ge(s_ds.sem, s_ds.at((p - 1, QB, 1)))
                        else:
                            act.wait_ge(s_av.sem, s_av.at((p - 1, "sample")))
                    to = ret_v if name == "rv" else sb_v
                    act.wait_ge(s_full.sem, s_full.at(step))
                    nc.scalar.activation(to[:, 3 * j:3 * j + 3, :],
                                         ring[jobs[step] % 2][:, 0:3 * P].rearrange("p (n e) -> p n e", n=3),
                                         ACT.Copy).then_inc(s_copy.sem, s_copy.mark(step))
                elif kind == "att":
                    p, n = step[1:]
                    act.wait_ge(s_attm.sem, s_attm.at((p, n)))
                    if n >= 2:
                        act.wait_ge(s_ds.sem, s_ds.at((p, n - 2)))
                    elif p > 0:
                        act.wait_ge(s_ds.sem, s_ds.at((p - 1, QB, 1)))
                    nc.scalar.activation(kd_tok[:, n % 2, :], turned_keys(p, n), ACT.Copy).then_inc(s_kd.sem, s_kd.mark((p, n)))
                elif kind == "ro":
                    p, n = step[1:]
                    t0, w = (n * P, P) if n < QB else (SEQ, NS)
                    if p == GLU_SLOT[0]:
                        act.wait_ge(s_tap.sem, s_tap.at(CONV_K - 1))
                        act.wait_ge(s_out.sem, s_out.at("conv"))
                    act.wait_ge(s_hx.sem, s_hx.at((CH - 1, KB - 1)))
                    if n < QB:
                        act.wait_ge(s_st.sem, s_st.at((p, n, "sum")))
                    act.wait_ge(s_ro.sem, s_ro.at((p, n)))
                    nc.scalar.activation(xs[p][:, t0:t0 + w], outputs_of(p, n)[:, 0:w], ACT.Copy).then_inc(s_roc.sem, s_roc.mark((p, n)))
                elif kind == "gn_mean":
                    act.wait_ge(s_mid.sem, s_mid.at(step))
                    square(xs[step[1]][:, cs(step[2])], ("gn_var", step[1], step[2]))
                elif kind == "gn_var":
                    act.wait_ge(s_full.sem, s_full.at(step))
                    root(in_ring(step), 1.0, step)
                elif kind == "ln_mean":
                    for b in range(CB):
                        act.wait_ge(s_mid.sem, s_mid.at(step))
                        square(conv[b][:, cs(step[1])], ("ln_var", step[1], b))
                elif kind == "ln_var":
                    act.wait_ge(s_full.sem, s_full.at(step))
                    root(in_ring(step), 1.0, step)
                elif kind == "ln_act":
                    b = step[1]
                    gate_free(step)
                    act.wait_ge(s_mid.sem, s_mid.at(("ln_n", CH - 1, CB - 1)))
                    sigmoid(conv[b], step, scale=vv(V_LNW + b), bias=vv(V_LNB + b))
                elif kind == "pw":
                    c = step[1]
                    act.wait_ge(s_full.sem, s_full.at(("pw", CB - 1, c)))
                    for b in range(CB):
                        nc.scalar.activation(conv[b][:, cs(c)], in_ring(("pw", b, c)), ACT.Copy).then_inc(
                            s_copy.sem, s_copy.mark(("pw", b, c)))
                elif kind == "score":
                    p, u = step[1:]
                    exp_scores(p, u)
                    if u == 0:
                        ln_scores(p, u)
                elif kind == "weigh":
                    p, u = step[1:]
                    kb, q0, n = UNITS[u]
                    if u >= 1:
                        act.wait_ge(s_av.sem, s_av.at((p, u - 1)))
                    elif p > 0:
                        act.wait_ge(s_av.sem, s_av.at((p - 1, U - 1)))
                    for h in range(2):
                        act.wait_ge(s_za.sem, s_za.at((p, u, h)))
                        nc.scalar.activation(weight[:, h, 0:n], Z[2 * (u % 2) + h][:, 0:n], ACT.Exp,
                                             bias=vv(V_BIAS + 2 * p + h)).then_inc(s_a.sem, s_a.mark((p, u, h)))
                    if kb > 0:
                        act.wait_ge(s_tot.sem, s_tot.at((p, u)))
                        act.wait_ge(s_o.sem, s_o.at((p, u - 1)))
                        nc.scalar.activation(keep[:, 0:n], TOT[:, 0:n], ACT.Exp, scale=-1.0).then_inc(
                            s_keepf.sem, s_keepf.mark((p, u)))
                    if u + 1 < U:
                        ln_scores(p, u + 1)
                elif kind in ("sample_z", "sample_t"):
                    p = step[1]
                    name, to, ready, done = ("e", stop9, s_z, s_e) if kind == "sample_z" else ("a", weight9, s_za, s_a)
                    act.wait_ge(ready.sem, ready.at((p, "sample")))
                    if p > 0 and name == "e":
                        act.wait_ge(s_av.sem, s_av.at((p - 1, "sample")))
                    for h in range(2):
                        last = nc.scalar.activation(of_head(to[:].rearrange("p g n -> p (g n)"), h), of_head(z9, h), ACT.Exp,
                                                    bias=vv(V_BIAS + 2 * p + h))
                    last.then_inc(done.sem, done.mark((p, "sample")))
                    if name == "e":
                        act.wait_ge(s_min.sem, s_min.at((p, "sample")))
                        nc.scalar.activation(stop9[:], stop9[:], ACT.Ln, bias=1.0).then_inc(s_l.sem, s_l.mark((p, "sample")))
                elif kind == "split":
                    c = step[1]
                    act.wait_ge(s_full.sem, s_full.at(job_of("sg", PAIRS - 1, c)))
                    for k in range(KB):
                        act.wait_ge(s_mix.sem, s_mix.at(("rg", k) if k < PAIRS else ("sg", k - PAIRS) if k < 2 * PAIRS else ("cg", k - 2 * PAIRS)))
                        nc.scalar.activation(H_hi[:, k, cs(c)], xs[k][:, cs(c)], ACT.Copy).then_inc(
                            s_hhi.sem, s_hhi.mark(("split", c, k)))
                elif kind == "post":
                    c = step[1]
                    act.wait_ge(s_full.sem, s_full.at(step))
                    root(in_ring(step), 1.0 / D_MODEL, step)
                    for k in range(KB):
                        m = c * KB + k
                        act.wait_ge(s_new.sem, s_new.at(m))
                        if m >= 2:
                            act.wait_ge(s_xsq.sem, s_xsq.at(m - 2))
                        else:
                            act.wait_ge(s_mid.sem, s_mid.at(("sum", KB - 1, CH - 1)))
                        nc.scalar.activation(squares[:, m % 2, :], xs[k][:, cs(c)], ACT.Square).then_inc(
                            s_sqa.sem, s_sqa.mark(("post", m)))

        @block.vector
        def _(dve):
            def softplus(p, u):
                n = UNITS[u][2]
                for h in range(2):
                    s = stop[:, (2 * u + h) % 4, 0:n]
                    dve.wait_ge(s_l.sem, s_l.at((p, u, h)))
                    nc.vector.scalar_tensor_tensor(out=s, in0=Z[2 * (u % 2) + h][:, 0:n], scalar=vv(V_BIAS + 2 * p + h), in1=s,
                                                   op0=ALU.add, op1=ALU.max).then_inc(s_sp.sem, s_sp.mark((p, u, h)))

            dve.wait_ge(s_vec.sem, s_vec.at("vec"))
            for step in STEPS:
                kind = step[0]
                if kind == "norm":
                    c = step[1]
                    dve.wait_ge(s_rstd.sem, s_rstd.at(step))
                    for k in range(KB + 1):
                        if k < KB:
                            if k >= 2:
                                dve.wait_ge(s_hlo.sem, s_hlo.at(("norm", c, k - 2)))
                            elif c > 0:
                                dve.wait_ge(s_hlo.sem, s_hlo.at(("norm", c - 1, k + KB - 2)))
                            nc.vector.scalar_tensor_tensor(out=hx[:, k % 2, :], in0=xs[k][:, cs(c)], scalar=vv(V_PRE + k),
                                                           in1=rstd[:, 0, :], op0=ALU.mult, op1=ALU.mult).then_inc(
                                s_hx.sem, s_hx.mark((c, k)))
                        if k > 0:
                            m = k - 1
                            dve.wait_ge(s_hhi.sem, s_hhi.at(("norm", c, m)))
                            nc.vector.tensor_tensor(H_lo[:, m, cs(c)], hx[:, m % 2, :], H_hi[:, m, cs(c)].bitcast(F32),
                                                    ALU.subtract).then_inc(s_hlo.sem, s_hlo.mark(("norm", c, m)))
                elif kind == "proj":
                    i, c = step[1:]
                    name, j = BLOCKS[i]
                    src = in_ring(step)
                    if name == "sq":
                        if j > 0 and c == 0:
                            dve.wait_ge(s_z.sem, s_z.at((j - 1, "sample")))
                        dve.wait_ge(s_full.sem, s_full.at(step))
                        for h in range(2):
                            r = slice(64 * h, 64 * h + 64)
                            last = nc.vector.tensor_scalar(sb_q[r, h, cs(c)], src[r], HEAD_DIM ** -0.5, None, ALU.mult)
                        last.then_inc(s_q.sem, s_q.mark(step))
                    elif name == "cb" and c == CH - 1:
                        dve.wait_ge(s_sig.sem, s_sig.at((name, j)))
                        nc.vector.tensor_tensor(glu[j], glu[j], gate[:], ALU.mult).then_inc(s_glu.sem, s_glu.mark((name, j)))
                    elif name in ("rg", "sg", "cg"):
                        k = j + {"rg": 0, "sg": PAIRS, "cg": 2 * PAIRS}[name]
                        x = xs[k][:, cs(c)]
                        if name == "rg":
                            dve.wait_ge(s_mid.sem, s_mid.at(("gn_n", j, c)))
                        elif name == "sg":
                            dve.wait_ge(s_o.sem, s_o.at((j, "sample")))
                        else:
                            dve.wait_ge(s_copy.sem, s_copy.at(("pw", j, c)))
                        dve.wait_ge(s_copy.sem, s_copy.at(step))
                        if name == "rg":
                            last = nc.vector.scalar_tensor_tensor(out=x, in0=x, scalar=vv(V_GN + j), in1=src, op0=ALU.mult, op1=ALU.mult)
                        else:
                            last = nc.vector.tensor_tensor(x, x, src, ALU.mult)
                        last.then_inc(s_gate.sem, s_gate.mark(step))
                        if c == CH - 1:
                            dve.wait_ge(s_gate.sem, s_gate.at(step))
                            dve.wait_ge(s_sig.sem, s_sig.at((name, j)))
                            nc.vector.tensor_tensor(xs[k], xs[k], gate[:], ALU.mult).then_inc(s_mix.sem, s_mix.mark((name, j)))
                    elif name == "out":
                        dve.wait_ge(s_sqo.sem, s_sqo.at(step))
                        s = squares[:, (3 * j + c) % 2, :]
                        if j == 0:
                            dve.wait_ge(s_z.sem, s_z.at((PAIRS - 1, "sample")))
                            dve.wait_ge(s_vout.sem, s_vout.at(PAIRS - 1))
                            nc.vector.tensor_copy(sumsq[:, c, :], s).then_inc(s_mid.sem, s_mid.mark(("sum", j, c)))
                        else:
                            dve.wait_ge(s_mid.sem, s_mid.at(("sum", j - 1, c)))
                            nc.vector.tensor_tensor(sumsq[:, c, :], sumsq[:, c, :], s, ALU.add).then_inc(
                                s_mid.sem, s_mid.mark(("sum", j, c)))
                elif kind == "rot":
                    _, name, p, c = step
                    n = rot_uses.index(step)
                    dve.wait_ge(s_full.sem, s_full.at(step))
                    dve.wait_ge(s_rota.sem, s_rota.at(step))
                    nc.vector.tensor_tensor(raw_rot[:, n % 2, :], in_ring(step), turn[:, 1, cs(c)], ALU.mult).then_inc(
                        s_rotb.sem, s_rotb.mark(step))
                    dve.wait_ge(s_rotb.sem, s_rotb.at(step))
                    if p > 0 and c == 0:
                        dve.wait_ge(s_dec.sem, s_dec.at((p - 1, QB)))
                    to = ret_q if name == "rq" else ret_k
                    nc.vector.tensor_tensor(to[:, cs(c)], rot_a[:, n % 2, :], raw_rot[:, n % 2, :], ALU.add).then_inc(
                        s_rope.sem, s_rope.mark(step))
                elif kind == "glu_rest":
                    dve.wait_ge(s_glu.sem, s_glu.at(("cb", CB - 1)))
                    for b in range(CB):
                        last = nc.vector.tensor_copy(glu9[:, b, :, HIST:], glu[b][:, SEQ:NT].rearrange("p (b t) -> p b t", b=DEC_BATCH))
                    last.then_inc(s_glu.sem, s_glu.mark("rest"))
                    dve.wait_ge(s_glu.sem, s_glu.at("rest"))
                    for b in range(CB):
                        w = vv(V_DW + b * CONV_K + CONV_K - 1)
                        nc.vector.tensor_scalar(conv[b][:, 0:SEQ], glu[b][:, 0:SEQ], w, vv(V_DWB + b), ALU.mult, ALU.add)
                        last = nc.vector.tensor_scalar(conv[b][:, SEQ:NT].rearrange("p (b t) -> p b t", b=DEC_BATCH),
                                                       glu9[:, b, :, HIST:], w, vv(V_DWB + b), ALU.mult, ALU.add)
                        last.then_inc(s_tap.sem, s_tap.mark((0, b)))
                    dve.wait_ge(s_hist.sem, s_hist.at("hist"))
                elif kind == "taps":
                    for s in range(step[1], step[1] + 1):
                        for b in range(CB):
                            w = vv(V_DW + b * CONV_K + CONV_K - 1 - s)
                            dve.wait_ge(s_tap.sem, s_tap.at((s - 1, b)))
                            y, y9 = conv[b][:, s:SEQ], conv[b][:, SEQ:NT].rearrange("p (b t) -> p b t", b=DEC_BATCH)
                            nc.vector.scalar_tensor_tensor(out=y, in0=glu[b][:, 0:SEQ - s], scalar=w, in1=y, op0=ALU.mult, op1=ALU.add)
                            last = nc.vector.scalar_tensor_tensor(out=y9, in0=glu9[:, b, :, HIST - s:HIST - s + DEC_SEQ], scalar=w,
                                                                  in1=y9, op0=ALU.mult, op1=ALU.add)
                            last.then_inc(s_tap.sem, s_tap.mark((s, b)))
                    if step[1] == CONV_K - 1:
                        s_tap.alias(CONV_K - 1)
                elif kind == "att":
                    p, n = step[1:]
                    w = P if n < QB else NS
                    dve.wait_ge(s_att.sem, s_att.at((p, n)))
                    if n >= 2:
                        dve.wait_ge(s_ro.sem, s_ro.at((p, n - 2)))
                    elif p > 0:
                        dve.wait_ge(s_ro.sem, s_ro.at((p - 1, QB)))
                    ok = (causal if n < QB else causal9).unsqueeze(1).to_broadcast([P, 2, w])
                    last = nc.vector.tensor_tensor(att[:, n % 2, :, 0:w], scores_of(p, n, w), ok, ALU.mult)
                    last.then_inc(s_attm.sem, s_attm.mark((p, n)))
                elif kind == "ro" and step[2] < QB:
                    p, n = step[1:]
                    if n == 0:
                        dve.wait_ge(s_decay.sem, s_decay.at(p))
                        if p > 0:
                            dve.wait_ge(s_stout.sem, s_stout.at(p - 1))
                        dve.wait_ge(s_ds.sem, s_ds.at((p, n)))
                        nc.vector.scalar_tensor_tensor(out=state[:], in0=increment(p, n), scalar=decay[:, D_STEP:D_STEP + 1], in1=blk,
                                                       op0=ALU.mult, op1=ALU.mult).then_inc(
                            s_st.sem, s_st.mark((p, n)))
                        s_st.alias((p, n, "sum"))
                    else:
                        dve.wait_ge(s_ds.sem, s_ds.at((p, n)))
                        dve.wait_ge(s_st.sem, s_st.at((p, n - 1)))
                        nc.vector.tensor_tensor(state[:], state[:], increment(p, n), ALU.add).then_inc(s_st.sem, s_st.mark((p, n, "sum")))
                        dve.wait_ge(s_st.sem, s_st.at((p, n, "sum")))
                        nc.vector.scalar_tensor_tensor(out=state[:], in0=state[:], scalar=decay[:, D_STEP:D_STEP + 1], in1=blk,
                                                       op0=ALU.mult, op1=ALU.mult).then_inc(
                            s_st.sem, s_st.mark((p, n)))
                elif kind == "ds9":
                    _, p, g = step
                    x = state9[:, 4 * g:4 * g + 4, :]
                    dve.wait_ge(s_ro.sem, s_ro.at((p, QB)))
                    dve.wait_ge(s_ds.sem, s_ds.at((p, QB, g)))
                    nc.vector.tensor_tensor(x, x, bank_of(step)[:, :].rearrange("p (b e) -> p b e", b=4), ALU.add).then_inc(
                        s_st.sem, s_st.mark((p, QB, g, "sum")))
                    dve.wait_ge(s_st.sem, s_st.at((p, QB, g, "sum")))
                    nc.vector.scalar_tensor_tensor(out=x, in0=x, scalar=decay[:, D_STEP9:D_STEP9 + 1], in1=blk.unsqueeze(1).to_broadcast([P, 4, P]),
                                                   op0=ALU.mult, op1=ALU.mult).then_inc(s_st.sem, s_st.mark((p, QB, g)))
                elif kind == "gn_mean":
                    _, p, c = step
                    dve.wait_ge(s_full.sem, s_full.at(step))
                    nc.vector.tensor_tensor(xs[p][:, cs(c)], xs[p][:, cs(c)], in_ring(step), ALU.subtract).then_inc(
                        s_mid.sem, s_mid.mark(step))
                elif kind == "gn_var":
                    _, p, c = step
                    n = root_uses.index(step)
                    dve.wait_ge(s_rstd.sem, s_rstd.at(step))
                    dve.wait_ge(s_mid.sem, s_mid.at(("gn_mean", p, c)))
                    nc.vector.tensor_tensor(xs[p][:, cs(c)], xs[p][:, cs(c)], rstd[:, 0, :], ALU.mult).then_inc(
                        s_mid.sem, s_mid.mark(("gn_n", p, c)))
                    s_mid.alias(("root", n))
                elif kind == "ln_mean":
                    c = step[1]
                    dve.wait_ge(s_full.sem, s_full.at(step))
                    for b in range(CB):
                        last = nc.vector.tensor_tensor(conv[b][:, cs(c)], conv[b][:, cs(c)], in_ring(step), ALU.subtract)
                    last.then_inc(s_mid.sem, s_mid.mark(step))
                elif kind == "ln_var":
                    c = step[1]
                    n = root_uses.index(step)
                    dve.wait_ge(s_rstd.sem, s_rstd.at(step))
                    dve.wait_ge(s_mid.sem, s_mid.at(("ln_mean", c)))
                    for b in range(CB):
                        nc.vector.tensor_tensor(conv[b][:, cs(c)], conv[b][:, cs(c)], rstd[:, 0, :], ALU.mult).then_inc(
                            s_mid.sem, s_mid.mark(("ln_n", c, b)))
                    s_mid.alias(("root", n))
                elif kind == "ln_act":
                    b = step[1]
                    dve.wait_ge(s_sig.sem, s_sig.at(step))
                    nc.vector.tensor_scalar(conv[b], conv[b], vv(V_LNW + b), vv(V_LNB + b), ALU.mult, ALU.add).then_inc(
                        s_mid.sem, s_mid.mark(("ln_l", b)))
                    dve.wait_ge(s_mid.sem, s_mid.at(("ln_l", b)))
                    nc.vector.tensor_tensor(conv[b], conv[b], gate[:], ALU.mult).then_inc(s_mid.sem, s_mid.mark(step))
                elif kind == "score":
                    if step[2] == 0:
                        softplus(*step[1:])
                elif kind == "weigh":
                    p, u = step[1:]
                    kb, q0, n = UNITS[u]
                    if u + 1 < U:
                        softplus(p, u + 1)
                    o = stick[p][:, q0:q0 + n]
                    dve.wait_ge(s_av.sem, s_av.at((p, u)))
                    if kb == 0:
                        if p == 2:
                            dve.wait_ge(s_tap.sem, s_tap.at(CONV_K - 1))
                            dve.wait_ge(s_out.sem, s_out.at("conv"))
                        nc.vector.tensor_copy(o, AV[:, 0:n]).then_inc(s_o.sem, s_o.mark((p, u)))
                    else:
                        dve.wait_ge(s_keepf.sem, s_keepf.at((p, u)))
                        dve.wait_ge(s_o.sem, s_o.at((p, u - 1)))
                        nc.vector.tensor_tensor(o, o, keep[:, 0:n], ALU.mult).then_inc(s_kept.sem, s_kept.mark((p, u)))
                        dve.wait_ge(s_kept.sem, s_kept.at((p, u)))
                        nc.vector.tensor_tensor(o, o, AV[:, 0:n], ALU.add).then_inc(s_o.sem, s_o.mark((p, u)))
                elif kind == "sample_z":
                    p = step[1]
                    dve.wait_ge(s_l.sem, s_l.at((p, "sample")))
                    s9 = stop9[:].rearrange("p g n -> p (g n)")
                    for h in range(2):
                        last = nc.vector.scalar_tensor_tensor(out=of_head(s9, h), in0=of_head(z9, h), scalar=vv(V_BIAS + 2 * p + h),
                                                              in1=of_head(s9, h), op0=ALU.add, op1=ALU.max)
                    last.then_inc(s_sp.sem, s_sp.mark((p, "sample")))
                elif kind == "sample_v":
                    p = step[1]
                    dve.wait_ge(s_av.sem, s_av.at((p, "sample")))
                    for h in range(2):
                        r = slice(64 * h, 64 * h + 64)
                        last = nc.vector.tensor_copy(stick[p][r, SEQ:NT].rearrange("p (b t) -> p b t", b=DEC_BATCH),
                                                     of_head(AV[r, 0:2 * NS], h))
                    last.then_inc(s_o.sem, s_o.mark((p, "sample")))
                elif kind == "split":
                    c = step[1]
                    for k in range(KB):
                        dve.wait_ge(s_hhi.sem, s_hhi.at(("split", c, k)))
                        nc.vector.tensor_tensor(H_lo[:, k, cs(c)], xs[k][:, cs(c)], H_hi[:, k, cs(c)].bitcast(F32),
                                                ALU.subtract).then_inc(s_hlo.sem, s_hlo.mark(("split", c, k)))
                elif kind == "post":
                    c = step[1]
                    dve.wait_ge(s_rstd.sem, s_rstd.at(step))
                    for k in range(KB):
                        x = xs[k][:, cs(c)]
                        nc.vector.scalar_tensor_tensor(out=x, in0=x, scalar=vv(V_POST + k), in1=rstd[:, 0, :], op0=ALU.mult,
                                                       op1=ALU.mult).then_inc(s_scaled.sem, s_scaled.mark((c, k)))
                    for k in range(KB):
                        m = c * KB + k
                        x = squares[:, m % 2, :]
                        dve.wait_ge(s_sqa.sem, s_sqa.at(("post", m)))
                        if k == 0:
                            if c == 0:
                                dve.wait_ge(s_dec.sem, s_dec.at((PAIRS - 1, QB)))
                            nc.vector.tensor_copy(xsq[:, c, :], x).then_inc(s_xsq.sem, s_xsq.mark(m))
                        else:
                            dve.wait_ge(s_xsq.sem, s_xsq.at(m - 1))
                            nc.vector.tensor_tensor(xsq[:, c, :], xsq[:, c, :], x, ALU.add).then_inc(s_xsq.sem, s_xsq.mark(m))

        @block.gpsimd
        def _(pool):
            def weights_lo(i):
                if i < len(BLOCKS):
                    pool.wait_ge(s_whi.sem, s_whi.at(i))
                    if i >= 2:
                        pool.wait_ge(s_full.sem, s_full.at(("proj", i - 2, CH - 1)))
                    nc.gpsimd.tensor_tensor(w_lo[:, i % 2, :], w_raw[:], w_hi[:, i % 2, :].bitcast(F32), ALU.subtract).then_inc(
                        s_wlo.sem, s_wlo.mark(i))

            def decays(p, n):
                if n > QB:
                    return
                if n >= 2:
                    pool.wait_ge(s_ro.sem, s_ro.at((p, n - 2)))
                elif p > 0:
                    pool.wait_ge(s_ro.sem, s_ro.at((p - 1, QB)))
                a, b, w = (n * P, n * P, P) if n < QB else (SEQ, LAST, NS)
                dq, dk = (D_Q, D_K) if n < QB else (D_Q9, D_K9)
                nc.gpsimd.tensor_tensor(qd[:, n % 2, :, 0:w], ret_q[:, a:a + w].unsqueeze(1).to_broadcast([P, 2, w]),
                                        decay[:, dq:dq + 2 * w].rearrange("p (h w) -> p h w", h=2), ALU.mult)
                if n == QB:
                    nc.gpsimd.tensor_tensor(qd9, ret_q[:, a:a + w], decay[:, D_BOTH9:D_BOTH9 + NS], ALU.mult)
                nc.gpsimd.tensor_tensor(kd[:, n % 2, :], ret_k[:, b:b + P], decay[:, dk:dk + P], ALU.mult).then_inc(
                    s_dec.sem, s_dec.mark((p, n)))

            weights_lo(0)
            for step in STEPS:
                kind = step[0]
                if kind == "proj":
                    i, c = step[1:]
                    name, j = BLOCKS[i]
                    if c == 0:
                        weights_lo(i + 1)
                    if name in ("rq", "rk"):
                        use = ("rot", name, j, c)
                        n = rot_uses.index(use)
                        if n >= 2:
                            pool.wait_ge(s_rope.sem, s_rope.at(rot_uses[n - 2]))
                        pool.wait_ge(s_copy.sem, s_copy.at(step))
                        nc.gpsimd.tensor_tensor(rot_a[:, n % 2, :], raw_rot[:, n % 2, :], turn[:, 0, cs(c)], ALU.mult).then_inc(
                            s_rota.sem, s_rota.mark(use))
                elif kind == "att":
                    p, n = step[1:]
                    if n == 0:
                        pool.wait_ge(s_decay.sem, s_decay.at(p))
                        pool.wait_ge(s_rope.sem, s_rope.at(("rot", "rk", p, CH - 1)))
                        decays(p, 0)
                    decays(p, n + 1)
                elif kind == "ds9":
                    _, p, g = step
                    pool.wait_ge(s_copy.sem, s_copy.at(("vtok", "rv", p, CH - 1)))
                    if g == 1:
                        pool.wait_ge(s_ds.sem, s_ds.at((p, QB, 0)))
                    elif p > 0:
                        pool.wait_ge(s_ds.sem, s_ds.at((p - 1, QB, 1)))
                    else:
                        pool.wait_ge(s_hlo.sem, s_hlo.at(("norm", CH - 1, KB - 1)))
                    nc.gpsimd.tensor_tensor(v_own[:], ret_v[:, QB, :].unsqueeze(1).to_broadcast([P, 4, P]),
                                            batch9[:, 4 * g:4 * g + 4].unsqueeze(2).to_broadcast([P, 4, P]),
                                            ALU.mult).then_inc(s_own.sem, s_own.mark((p, g)))
                elif kind == "score":
                    p, u = step[1:]
                    n = UNITS[u][2]
                    for h in range(2):
                        s = stop[:, (2 * u + h) % 4, 0:n]
                        pool.wait_ge(s_e.sem, s_e.at((p, u, h)))
                        nc.gpsimd.tensor_scalar(s, s, E_MAX, None, ALU.min).then_inc(s_min.sem, s_min.mark((p, u, h)))
                elif kind == "post":
                    c = step[1]
                    for k in range(KB):
                        m = c * KB + k
                        x = xs[k][:, cs(c)]
                        pool.wait_ge(s_x[m % 2].sem, s_x[m % 2].at(m))
                        pool.wait_ge(s_scaled.sem, s_scaled.at((c, k)))
                        nc.gpsimd.tensor_tensor(x, x, hx[:, m % 2, :], ALU.add).then_inc(s_new.sem, s_new.mark(m))
                elif kind == "sample_z":
                    p = step[1]
                    pool.wait_ge(s_e.sem, s_e.at((p, "sample")))
                    nc.gpsimd.tensor_scalar(stop9[:], stop9[:], E_MAX, None, ALU.min).then_inc(s_min.sem, s_min.mark((p, "sample")))

        layer.close()
        nums = [x.num for x in sems]
        assert sorted(nums) == list(range(min(nums), max(nums) + 1))
        nc.sync.sem_clear(range(min(nums), max(nums) + 1))
        nc.all_engine_barrier()
        loop.close()


def kernel(x_prompt, x_sample, state_ret, cache_k, cache_v, state_conv, page_table,
           norm_pre, w_in, ret_gn_w, sb_bias, conv_dw_w, conv_dw_b, conv_ln_w, conv_ln_b,
           conv_pw_w, w_out, norm_post):
    import concourse.bacc as bacc
    from concourse.bass_utils import run_bass_kernel_spmd

    L, B, D = DEPTH, DEC_BATCH, HEAD_DIM
    (x_prompt, x_sample, state_ret, cache_k, cache_v, state_conv, page_table, norm_pre, w_in, ret_gn_w, sb_bias,
     conv_dw_w, conv_dw_b, conv_ln_w, conv_ln_b, conv_pw_w, w_out, norm_post) = map(np.asarray, (
         x_prompt, x_sample, state_ret, cache_k, cache_v, state_conv, page_table, norm_pre, w_in, ret_gn_w, sb_bias,
         conv_dw_w, conv_dw_b, conv_ln_w, conv_ln_b, conv_pw_w, w_out, norm_post))

    def by_partition(a):
        return a.reshape(L, -1, P).transpose(0, 2, 1)

    x = np.concatenate([x_prompt.reshape(SEQ, D_MODEL), x_sample.reshape(NS, D_MODEL)])
    columns = [FIRST_COLUMN[name] + j for name, j in PROJ]
    w = np.concatenate([w_in.reshape(L, KB, P, -1, P)[:, :, :, columns], w_out.reshape(L, KB, P, KB, P)], 3)
    w = w.transpose(0, 3, 2, 1, 4).reshape(L, len(BLOCKS), P, KB * P)
    states = np.zeros((L, PAIRS, 2, D, B, 2, D), np.float32)
    s = state_ret.reshape(L, B, PAIRS, 2, D, D)
    for h in range(2):
        states[:, :, h, :, :, h, :] = s[:, :, :, h].transpose(0, 2, 3, 1, 4)
    vec = np.concatenate([
        by_partition(norm_pre), by_partition(norm_post), by_partition(ret_gn_w),
        np.broadcast_to(sb_bias[:, None, :], (L, P, HEADS)),
        conv_dw_w.reshape(L, CONV_K, CB, P).transpose(0, 3, 2, 1).reshape(L, P, CB * CONV_K),
        by_partition(conv_dw_b), by_partition(conv_ln_w), by_partition(conv_ln_b),
        conv_pw_w.reshape(L, CB, P, CONV_W).transpose(0, 2, 1, 3).reshape(L, P, CB * CONV_W),
    ], 2)
    const, masks, turn, decay = shape_constants()
    ins = {
        "xT": x.reshape(NT, KB, P).transpose(2, 1, 0),
        "w": w,
        "vec": vec,
        "state_ret": states.reshape(L, PAIRS, P, B, P),
        "state_conv": state_conv.reshape(L, B, HIST, CB, P).transpose(0, 4, 3, 1, 2),
        "cache_k": cache_k.reshape(L, N_POOL, PAGE, PAIRS, P).transpose(0, 1, 3, 4, 2),
        "cache_v": cache_v.reshape(L, N_POOL, PAGE, PAIRS, P).transpose(0, 1, 3, 2, 4),
        "page_table": page_table.reshape(1, B * N_PAGES),
        "const": const, "masks": masks, "turn": turn, "decay": decay,
    }
    ins = {k: np.ascontiguousarray(v) for k, v in ins.items()}
    outs = {
        "yT": (P, KB, NT), "state_p": (L, PAIRS, P, P), "state_s": (L, PAIRS, P, B, P),
        "k_rows": (L, PAIRS, P, NT), "v_rows": (L, PAIRS, P, NT),
        "conv_p": (L, P, CB, HIST), "conv_s": (L, P, CB, B, HIST),
    }

    def assemble(counts):
        nc = bacc.Bacc("TRN2", target_bir_lowering=False, num_devices=1, dynamic_dma_scratch_size=1024)
        io = {k: nc.dram_tensor(f"in_{k}", v.shape, mybir.dt.from_np(v.dtype), kind="ExternalInput").ap() for k, v in ins.items()}
        io |= {k: nc.dram_tensor(f"out_{k}", v, F32, kind="ExternalOutput").ap() for k, v in outs.items()}
        build(nc, io, counts)
        return nc

    counts = {}
    assemble(counts)
    nc = assemble(counts)
    r = run_bass_kernel_spmd(nc, [{f"in_{k}": v for k, v in ins.items()}], core_ids=[0]).results[0]
    got = {k: np.asarray(r[f"out_{k}"]) for k in outs}

    y = got["yT"].transpose(2, 1, 0).reshape(NT, D_MODEL)
    sp = got["state_p"].reshape(L, PAIRS, 2, D, 2, D)
    sp = np.stack([sp[:, :, h, :, h, :] for h in range(2)], 2).reshape(L, 1, HEADS, D, D)
    ss = got["state_s"].reshape(L, PAIRS, 2, D, B, 2, D)
    ss = np.stack([ss[:, :, h, :, :, h, :] for h in range(2)], 2)
    ss = ss.transpose(0, 4, 1, 2, 3, 5).reshape(L, B, HEADS, D, D)

    def rows(a):
        a = a.transpose(0, 3, 1, 2).reshape(L, NT, HEADS, D)
        return a[:, :SEQ].reshape(L, 1, SEQ, HEADS, D), a[:, SEQ:].reshape(L, B, DEC_SEQ, HEADS, D)

    kp, ks = rows(got["k_rows"])
    vp, vs = rows(got["v_rows"])
    cp = got["conv_p"].transpose(0, 3, 2, 1).reshape(L, 1, HIST, CONV_W)
    cv = got["conv_s"].transpose(0, 3, 4, 2, 1).reshape(L, B, HIST, CONV_W)
    return (y[:SEQ].reshape(1, SEQ, D_MODEL), y[SEQ:].reshape(B, DEC_SEQ, D_MODEL), sp, ss, kp, vp, ks, vs, cp, cv)
```

```python
from contextlib import ExitStack

import numpy as np
import concourse.bass as bass
from concourse import mybir

F32 = mybir.dt.float32
F32R = mybir.dt.float32r
BF16 = mybir.dt.bfloat16
I32 = mybir.dt.int32
ALU = mybir.AluOpType
ACT = mybir.ActivationFunctionType

D_MODEL, SEQ, DEPTH = 1024, 1024, 2
DEC_BATCH, DEC_SEQ, PAST_LEN, PAGE = 8, 4, 256, 128
HEAD_DIM, HEADS, CONV_W, CONV_K = 64, 6, 256, 31
N_PAGES = PAST_LEN // PAGE
N_POOL = DEC_BATCH * N_PAGES * 5 // 4
ROPE_BASE, EPS = 10000.0, 1e-6

P = 128
KB = D_MODEL // P
NS = DEC_BATCH * DEC_SEQ
NT = SEQ + NS
CH = 3
CW = NT // CH
QB = SEQ // P
LAST = NT - P
PAIRS = HEADS // 2
CB = CONV_W // P
HIST = CONV_K - 1

FIRST_COLUMN = {"rq": 0, "rk": 3, "rv": 6, "rg": 9, "sq": 12, "sk": 15, "sv": 18, "sg": 21, "ca": 24, "cb": 26, "cg": 28}
MIX_SLOT = {"r": 0, "s": PAIRS, "c": 2 * PAIRS}
GLU_SLOT = [2, 5]

UNITS = []
for kb in range(QB):
    width = SEQ - kb * P
    parts = -(-width // 512)
    for i in range(parts):
        UNITS.append((kb, kb * P + i * (width // parts), width // parts))

NEVER = -(2.0 ** 100)
E_MAX = 2.0 ** 62

EXP_LN = "natural_log_exp_and_others"

C_ID, C_TRI, C_ONE, C_BLK, C_CH, C_ROT, C_CAUSAL, C_CAUSAL9, C_BATCH9, C_EPS = 0, 128, 256, 384, 512, 640, 768, 896, 928, 936
C_NEG = 937
C_ALL = C_NEG + P
D_Q, D_K, D_Q9, D_BOTH9, D_K9, D_STEP, D_STEP9 = 0, 256, 384, 448, 480, 608, 609
D_ALL = 610
V_PRE, V_POST, V_GN, V_BIAS, V_DW, V_DWB, V_LNW, V_LNB, V_PW = 0, 8, 16, 19, 25, 87, 89, 91, 93
V_ALL = 93 + CB * CONV_W


def shape_constants():
    f = np.float32
    c = np.zeros((P, C_ALL), f)
    i = np.arange(P)
    c[:, C_ID:C_ID + P] = np.eye(P)
    c[:, C_TRI:C_TRI + P] = -(i[:, None] >= i[None, :]).astype(f)
    c[:, C_ONE:C_ONE + P] = 1.0
    c[:, C_BLK:C_BLK + P] = (i[:, None] // HEAD_DIM == i[None, :] // HEAD_DIM) / HEAD_DIM
    c[:, C_CH:C_CH + P] = 1.0 / CONV_W
    half = HEAD_DIM // 2
    for m in range(P):
        if m % HEAD_DIM < half:
            c[m + half, C_ROT + m] = -1.0
        else:
            c[m - half, C_ROT + m] = 1.0
    c[:, C_CAUSAL:C_CAUSAL + P] = i[:, None] <= i[None, :]
    row = i - (P - NS)
    col = np.arange(NS)
    own = (row[:, None] >= 0) & (row[:, None] // DEC_SEQ == col[None, :] // DEC_SEQ)
    c[:, C_CAUSAL9:C_CAUSAL9 + NS] = own & (row[:, None] <= col[None, :])
    c[:, C_BATCH9:C_BATCH9 + DEC_BATCH] = (row[:, None] >= 0) & (row[:, None] // DEC_SEQ == np.arange(DEC_BATCH)[None, :])
    c[:, C_EPS] = EPS
    c[:, C_NEG:C_NEG + P] = -1.0

    masks = np.zeros((P, P + 2 * NS), f)
    masks[:, :P] = np.where(i[:, None] < i[None, :], 0.0, NEVER)
    ok = own & (row[:, None] < col[None, :])
    ok = np.repeat(ok.reshape(P, DEC_BATCH, 1, DEC_SEQ), 2, axis=2).reshape(P, 2 * NS)
    masks[:, P:] = np.where(ok, 0.0, NEVER)

    inv = np.power(f(ROPE_BASE), (-2.0 * np.arange(half, dtype=f) / HEAD_DIM).astype(f)).astype(f)
    pos = np.concatenate([np.arange(SEQ), PAST_LEN + np.arange(NS) % DEC_SEQ]).astype(f)
    angle = (inv[i % half][:, None] * pos[None, :]).astype(f).astype(np.float64)
    turn = np.stack([np.cos(angle), np.sin(angle)], 1).astype(f)

    d = np.zeros((PAIRS, P, D_ALL), f)
    for p in range(PAIRS):
        lg = np.log(1.0 - 2.0 ** (-5.0 - (2 * p + i // HEAD_DIM)))[:, None]
        t = np.arange(P)[None, :]
        q = np.exp((t + 1) * lg)
        q9 = np.exp((col[None, :] % DEC_SEQ + 1) * lg)
        for h in range(2):
            mine = i[:, None] // HEAD_DIM == h
            d[p, :, D_Q + h * P:D_Q + (h + 1) * P] = q * mine
            d[p, :, D_Q9 + h * NS:D_Q9 + (h + 1) * NS] = q9 * mine
        d[p, :, D_BOTH9:D_BOTH9 + NS] = q9
        d[p, :, D_K:D_K + P] = np.exp(-(t + 1) * lg) * HEAD_DIM ** -0.5
        d[p, :, D_K9 + P - NS:D_K9 + P] = np.exp(-(col[None, :] % DEC_SEQ + 1) * lg) * HEAD_DIM ** -0.5
        d[p, :, D_STEP] = np.exp(P * lg[:, 0]) * HEAD_DIM
        d[p, :, D_STEP9] = np.exp(DEC_SEQ * lg[:, 0]) * HEAD_DIM
    return c, masks.astype(mybir.dt.np(BF16)), turn, d


class Signal:

    def __init__(self, sem, counts, complete):
        self.sem, self.counts, self.complete, self.n = sem, counts, complete, 0

    def mark(self, event, by=1):
        self.n += by
        self.counts[event] = self.n
        return by

    def alias(self, event):
        self.counts[event] = self.n

    def at(self, event):
        return self.counts[event] if self.complete else 1


def named_schedule():
    def project(name, j):
        return [("proj", (name, j), c) for c in range(CH)]

    def turned(name, p):
        a = project(name, p)
        return [a[0], a[1], ("rot", name, p, 0), a[2], ("rot", name, p, 1), ("rot", name, p, 2)]

    def values(name, p):
        return project(name, p) + [("vtok", name, p, j) for j in range(CH)]

    def retention_blocks(p):
        return turned("rq", p) + turned("rk", p) + values("rv", p)

    def stick_blocks(p):
        return project("sq", p) + project("sk", p) + values("sv", p)

    def retention(p):
        main = [[("att", p, n)] * (n <= QB) + [("ro", p, n - 1)] * (n > 0) for n in range(QB + 2)]
        return main + [[("ds9", p, 0)], [("ds9", p, 1)]]

    def group_norm(p):
        return [("gn_mean", p, 0), ("gn_mean", p, 1), ("gn_var", p, 0), ("gn_mean", p, 2), ("gn_var", p, 1), ("gn_var", p, 2)]

    def cost(step):
        return {"proj": 8, "taps": 2, "glu_rest": 2, "att": 3, "ro": 2, "ds9": 3, "gn_mean": 2, "gn_var": 2}.get(step[0], 2)

    def between(main, filler, weights=None):
        weights = weights or [1] * len(main)
        whole, out, done, spent, passed = sum(map(cost, filler)), [], 0, 0, 0
        for group, weight in zip(main, weights):
            out += group
            passed += weight
            while done < len(filler) and (spent + cost(filler[done]) / 2) * sum(weights) <= whole * passed:
                spent += cost(filler[done])
                out.append(filler[done])
                done += 1
        return out + filler[done:]

    def singly(steps):
        return [[x] for x in steps]

    taps = [("taps", s, b) for s in range(1, CONV_K) for b in range(CB)]
    conv_norm = []
    for c in range(CH):
        conv_norm += [("ln_mean", c), ("ln_var", c)]
    conv_norm += [("ln_act", b) for b in range(CB)] + [("pw", c) for c in range(CH)]
    glu_blocks = project("ca", 0) + project("cb", 0) + project("ca", 1) + project("cb", 1)

    ahead = [[], between(singly(taps[:20]), group_norm(0)), taps[48:]]
    fill = [
        retention_blocks(0) + between(retention(0), glu_blocks) + [("glu_rest",)],
        between(singly(retention_blocks(1)), taps[20:40])
        + between(singly(between(retention(1), project("rg", 0))), taps[40:48])
        + between(singly(project("sg", 0)), group_norm(1)) + project("rg", 1),
        between(singly(retention_blocks(2)), conv_norm)
        + between(retention(2), project("cg", 0) + project("cg", 1))
        + between(singly(project("sg", 1)), group_norm(2)) + project("rg", 2),
    ]
    steps = [("root_x", 0), ("sum_x", 1), ("norm", 0), ("root_x", 1), ("norm", 1)]
    for p in range(PAIRS):
        blocks = stick_blocks(p)
        if p == 0:
            first = [blocks[b * CH + c] for c in range(CH) for b in range(2)]
            steps += [first[0], ("sum_x", 2), ("root_x", 2), ("norm", 2)] + first[1:]
            blocks = blocks[2 * CH:]
        steps += between([[x] for x in blocks], ahead[p])
        main, weights = [[("score", p, 0)]], [2]
        for u, (_, _, width) in enumerate(UNITS):
            main.append([("score", p, u + 1)] if u + 1 < len(UNITS) else [])
            main.append([("stop", p, u)])
            main.append([("weigh", p, u)])
            weights += [2.5 + width / 256, 2 + width / 256, 1 + width / 256]
        n = len(fill[p]) - (6 if p == 0 else 3)
        late = fill[p][n:]
        steps += between(main, fill[p][:n], weights)
        steps += [("sample_z", p)] + late[:2] + [("sample_t", p)] + late[2:3] + [("sample_v", p)] + late[3:]
    for c, step in enumerate(project("sg", PAIRS - 1)):
        steps += [step, ("split", c)]
    for f in range(KB - 2):
        steps += project("out", f)
    x, y = project("out", KB - 2), project("out", KB - 1)
    steps += [x[0], y[0], x[1], ("root_y", 0), y[1], ("post", 0), x[2], ("root_y", 1), y[2], ("post", 1), ("root_y", 2)]
    steps += [("sum_x", 0), ("post", 2)]
    return steps


BLOCKS = list(dict.fromkeys(step[1] for step in named_schedule() if step[0] == "proj"))
PROJ = BLOCKS[:-KB]


def schedule():
    return [("proj", BLOCKS.index(step[1]), step[2]) if step[0] == "proj" else step for step in named_schedule()]


def build(nc, io, counts):
    complete = bool(counts)
    STEPS = schedule()
    ctx = ExitStack()
    with ctx:
        def sb(name, shape, dt=F32):
            return ctx.enter_context(nc.sbuf_tensor(name, shape, dt))

        def bank(name):
            return ctx.enter_context(nc.psum_tensor(name, [P, 512], F32))

        sems = []

        def sig(name):
            sems.append(ctx.enter_context(nc.semaphore(name)))
            return Signal(sems[-1], counts.setdefault(name, {}), complete)

        H_hi = sb("H_hi", [P, KB, NT], F32R)
        H_lo = sb("H_lo", [P, KB, NT], F32R)
        MX = sb("MX", [P, KB, NT])
        w_raw = sb("w_raw", [P, KB * P])
        w_hi = sb("w_hi", [P, 2, KB * P], F32R)
        w_lo = sb("w_lo", [P, 2, KB * P], F32R)
        const = sb("const", [P, C_ALL])
        masks = sb("masks_sb", [P, P + 2 * NS], BF16)
        ident_b = sb("ident_b", [P, P], BF16)
        turn = sb("turn_sb", [P, 2, NT])
        decay = sb("decay_sb", [P, D_ALL])
        vec = sb("vec_sb", [P, V_ALL])
        pages = sb("pages", [1, DEC_BATCH * N_PAGES], I32)
        ret_q = sb("ret_q", [P, NT])
        sb_k = sb("sb_k", [P, NT])
        sb_q = sb("sb_q", [P, 2, NT])
        raw_rot = sb("raw_rot", [P, 2, CW])
        rot_a = sb("rot_a", [P, 2, CW])
        wide = sb("wide", [P, 4, CW])
        squares = wide[:, 2:4, :]
        gate = sb("gate", [P, NT])
        rstd = sb("rstd", [P, 1, CW])
        sumsq = sb_k[:].rearrange("p (c n) -> p c n", c=CH)
        state = sb("state", [P, P])
        state9 = sb("state9", [P, DEC_BATCH, P])
        qd = sb("qd", [P, 2, 2, P])
        kd = sb("kd", [P, 2, P])
        kd_tok = sb("kd_tok", [P, 2, P])
        att = sb("att", [P, 2, 2, P])
        qd9 = att[:, QB % 2, 0, P - NS:P]
        v_own = wide[:, 0:2, :].rearrange("p a n -> p (a n)")[:, 0:512].rearrange("p (b e) -> p b e", b=DEC_BATCH // 2)
        keep = sb("keep", [P, 512])
        stop9 = sb("stop9", [P, 3, 2 * NS])
        weight9 = stop9
        attend = sb("attend", [P, 2 * 4 * 512 + 2 * 512 + 2 * NT + 2 * (QB + 1) * P])
        cuts = [0]

        def part(n, m):
            cuts.append(cuts[-1] + n * m)
            return attend[:, cuts[-2]:cuts[-1]].rearrange("p (n m) -> p n m", n=n)

        page = part(DEC_BATCH * N_PAGES, P)
        stop = part(4, 512)
        weight = part(2, 512)
        ret_k = part(1, NT)[:, 0, :]
        v_rows = part(1, NT)[:, 0, :]
        ret_v = part(QB + 1, P)
        sb_v = part(QB + 1, P)
        first_squares = attend[:, cuts[1]:cuts[1] + KB * CW].rearrange("p (k n) -> p k n", k=KB)
        old_x = attend[:, 0:KB * NT].rearrange("p (k n) -> p k n", k=KB)
        glu9 = sb("glu9", [P, CB, DEC_BATCH, HIST + DEC_SEQ])

        ring = [bank("ring0"), bank("ring1")]
        Z = [bank(f"Z{i}") for i in range(4)]
        TOT, AV = bank("TOT"), bank("AV")
        SUM_X, SUM_Y = [z[:, 0:CW] for z in Z[:3]], [z[:, 0:CW] for z in (Z[3], TOT, AV)]

        def cc(a, n=P):
            return const[:, a:a + n]

        ident, negtri, ones, blk, ch_mean, rotm = (cc(a) for a in (C_ID, C_TRI, C_ONE, C_BLK, C_CH, C_ROT))
        causal, causal9, batch9, eps, negones = cc(C_CAUSAL), cc(C_CAUSAL9, NS), cc(C_BATCH9, DEC_BATCH), cc(C_EPS, 1), cc(C_NEG)

        def vv(a, n=1):
            return vec[:, a:a + n]

        pw = vec[:, V_PW:V_PW + CB * CONV_W].rearrange("p (k n) -> p k n", k=CB)

        def cs(c):
            return slice(c * CW, (c + 1) * CW)

        xs = [MX[:, k, :] for k in range(KB)]
        glu = [xs[k] for k in GLU_SLOT]
        conv = [xs[6 + b] for b in range(CB)]
        stick = [xs[PAIRS + p] for p in range(PAIRS)]
        U, B = len(UNITS), len(BLOCKS)
        z9 = Z[0][:, 0:6 * NS]

        def of_head(a, h):
            return a.rearrange("p (g h t) -> p g h t", h=2, t=DEC_SEQ)[:, :, h, :]

        s_vec = sig("s_vec")
        s_decay = sig("s_decay")
        s_w = sig("s_w")
        s_state9 = sig("s_state9")
        s_pagek = sig("s_pagek")
        s_pagev = sig("s_pagev")
        s_hist = sig("s_hist")
        s_x = [sig(f"s_x{c}") for c in range(CH)]
        s_keep = sig("s_keep")
        s_out = sig("s_out")
        s_stout = sig("s_stout")
        s_vout = sig("s_vout")
        s_whi = sig("s_whi")
        s_wlo = sig("s_wlo")
        s_full = sig("s_full")
        s_sqa = sig("s_sqa")
        s_sqm = sig("s_sqm")
        s_sumy = sig("s_sumy")
        s_ln, s_rstd = sig("s_ln"), sig("s_rstd")
        s_hx = sig("s_hx")
        s_hhi = sig("s_hhi")
        s_lo = {"dve": sig("s_lo_dve"), "pool": sig("s_lo_pool")}
        s_scaled = sig("s_scaled")
        s_new = {"dve": sig("s_new_dve"), "pool": sig("s_new_pool")}
        s_copy = sig("s_copy")
        s_sqo = sig("s_sqo")
        s_q = sig("s_q")
        s_rota = sig("s_rota")
        s_rotb = sig("s_rotb")
        s_rope = sig("s_rope")
        s_sig = sig("s_sig")
        s_glu = sig("s_glu")
        s_tap = sig("s_tap")
        s_mid = sig("s_mid")
        s_mix = sig("s_mix")
        s_gate = sig("s_gate")
        s_dec = sig("s_dec")
        s_att = sig("s_att")
        s_attm = sig("s_attm")
        s_kd = sig("s_kd")
        s_ro = sig("s_ro")
        s_roc = sig("s_roc")
        s_ds = sig("s_ds")
        s_st = sig("s_st")
        s_own = sig("s_own")
        s_z = sig("s_z")
        s_e = sig("s_e")
        s_min = sig("s_min")
        s_l = sig("s_l")
        s_sp = sig("s_sp")
        s_za = sig("s_za")
        s_tot = sig("s_tot")
        s_a = sig("s_a")
        s_keepf = sig("s_keepf")
        s_av = sig("s_av")
        s_kept = sig("s_kept")
        s_o = sig("s_o")

        LO_BY = {"norm": ["pool" if k in (0, 2, 3, 5, 6) else "dve" for k in range(KB)],
                 "split": ["pool" if k in (0, 3, 6) else "dve" for k in range(KB)]}
        NEW_BY = ["dve" if k in (2, 4, 7) else "pool" for k in range(KB)]

        def wait_lo(engine, src, c):
            for name, sg in s_lo.items():
                engine.wait_ge(sg.sem, sg.at((src, c, max(k for k in range(KB) if LO_BY[src][k] == name))))

        def wait_lo_of(engine, src, c, k):
            sg = s_lo[LO_BY[src][k]]
            engine.wait_ge(sg.sem, sg.at((src, c, k)))

        def wait_new(engine, c, k):
            sg = s_new[NEW_BY[k]]
            engine.wait_ge(sg.sem, sg.at((c, k)))

        s_pages, s_masks, s_turn = (ctx.enter_context(nc.semaphore(name)) for name in ("s_pages", "s_masks", "s_turn"))
        s_zero = ctx.enter_context(nc.semaphore("s_zero"))
        s_first_w = [ctx.enter_context(nc.semaphore(f"s_first_w{i}")) for i in range(2)]
        s_first_lo = [ctx.enter_context(nc.semaphore(f"s_first_lo{i}")) for i in range(2)]
        s_first_hi = ctx.enter_context(nc.semaphore("s_first_hi"))
        first_w = [w_raw[:], attend[:, 0:KB * P]]
        s_const = ctx.enter_context(nc.semaphore("s_const"))
        s_chunk = [ctx.enter_context(nc.semaphore(f"s_chunk{c}")) for c in range(CH)]
        s_first_square = ctx.enter_context(nc.semaphore("s_first_square"))
        s_first_sum = ctx.enter_context(nc.semaphore("s_first_sum"))
        with nc.Block() as block:
            @block.sync
            def _(sp):
                sp.dma_start(MX[:, :, cs(0)], io["xT"][:, :, cs(0)]).then_inc(s_chunk[0], 16)
                for i in range(2):
                    sp.dma_start(first_w[i], io["w"][i]).then_inc(s_first_w[i], 16)
                for c in range(1, CH):
                    sp.dma_start(MX[:, :, cs(c)], io["xT"][:, :, cs(c)]).then_inc(s_chunk[c], 16)

            @block.scalar
            def _(act):
                nc.scalar.preload_act_table_set(EXP_LN)
                act.dma_start(const[:], io["const"]).then_inc(s_const, 16)
                act.dma_start(pages[:], io["page_table"]).then_inc(s_pages, 16)
                act.wait_ge(s_chunk[0], 16)
                for k in range(KB):
                    if k >= 4:
                        act.wait_ge(s_first_sum, k - 3)
                    nc.scalar.activation(wide[:, k % 4, :], xs[k][:, cs(0)], ACT.Square).then_inc(s_first_square, 1)
                for i in range(2):
                    act.wait_ge(s_first_w[i], 16)
                    nc.scalar.activation(w_hi[:, i, :], first_w[i], ACT.Copy).then_inc(s_first_hi, 1)
                act.dma_start(masks[:], io["masks"]).then_inc(s_masks, 16)
                act.dma_start(turn[:], io["turn"]).then_inc(s_turn, 16)

            @block.tensor
            def _(pe):
                pe.wait_ge(s_const, 16)
                for k in range(KB):
                    pe.wait_ge(s_first_square, k + 1)
                    nc.tensor.matmul(SUM_X[0], ones, wide[:, k % 4, :], start=(k == 0), stop=(k == KB - 1)).then_inc(s_first_sum, 1)

            @block.gpsimd
            def _(pool):
                pool.wait_ge(s_first_hi, 1)
                nc.gpsimd.tensor_tensor(w_lo[:, 0, :], first_w[0], w_hi[:, 0, :].bitcast(F32), ALU.subtract).then_inc(s_first_lo[0], 1)
                pool.wait_ge(s_first_lo[0], 1)

            @block.vector
            def _(dve):
                nc.vector.memset(sb_q[:], 0.0).then_inc(s_zero, 1)
                dve.wait_ge(s_const, 16)
                nc.vector.tensor_copy(ident_b[:], ident).then_inc(s_zero, 1)
                dve.wait_ge(s_zero, 2)
                dve.wait_ge(s_first_hi, 2)
                nc.vector.tensor_tensor(w_lo[:, 1, :], first_w[1], w_hi[:, 1, :].bitcast(F32), ALU.subtract).then_inc(s_first_lo[1], 1)
                dve.wait_ge(s_first_lo[1], 1)

        loop = ExitStack()
        l = loop.enter_context(nc.Fori(0, DEPTH))

        def of_layer(name, *more):
            a = io[name][bass.ds(l, 1)]
            names = "abcdef"[:len(a.shape) - 1]
            a = a.rearrange(f"z {' '.join(names)} -> (z {names[0]}) {' '.join(names[1:])}")
            for i in more:
                a = a[i]
            return a

        jobs = {}
        for step in STEPS:
            if step[0] in ("proj", "rot", "vtok", "att", "ro", "ds9", "gn_mean", "gn_var", "ln_mean", "ln_var"):
                jobs[step] = len(jobs)
            if step[0] == "pw":
                for b in range(CB):
                    jobs[("pw", b, step[1])] = len(jobs)
        in_order = list(jobs)

        def in_ring(job):
            return ring[jobs[job] % 2][:, 0:CW]

        def bank_of(job):
            return ring[jobs[job] % 2]

        def scores_of(p, n, w):
            return bank_of(("att", p, n))[:, 0:2 * P].rearrange("p (h w) -> p h w", h=2)[:, :, 0:w]

        def turned_keys(p, n):
            return bank_of(("att", p, n))[:, 2 * P:3 * P]

        def outputs_of(p, n):
            return bank_of(("ro", p, n))[:, 0:P]

        def increment(p, n):
            return bank_of(("ro", p, n))[:, P:2 * P]

        def drained(job):
            kind = job[0]
            if kind == "proj":
                name = BLOCKS[job[1]][0]
                s = {"sq": s_q, "rg": s_gate, "sg": s_gate, "cg": s_gate, "out": s_sqo}.get(name, s_copy)
            elif kind == "rot":
                s = s_rotb
            elif kind in ("vtok", "pw"):
                s = s_copy
            elif kind == "att":
                s, job = s_kd, job[1:]
            elif kind == "ro":
                s, job = s_roc, job[1:]
            elif kind == "ds9":
                s, job = s_st, (job[1], QB, job[2], "sum")
            elif kind in ("gn_mean", "ln_mean"):
                s = s_mid
            else:
                s = s_ln
            return s.sem, s.at(job)

        def job_of(name, j, c):
            return ("proj", BLOCKS.index((name, j)), c)

        rot_uses = [s for s in STEPS if s[0] == "rot"]
        sq_uses, root_uses, gate_uses = [], [], []
        for step in STEPS:
            if step[0] == "gn_mean":
                sq_uses += [("gn_var", step[1], step[2])]
            if step[0] == "ln_mean":
                sq_uses += [("ln_var", step[1], b) for b in range(CB)]
            if step[0] in ("gn_var", "ln_var"):
                root_uses.append(step)
            if step[0] == "proj" and BLOCKS[step[1]][0] in ("cb", "rg", "sg", "cg") and step[2] == CH - 1:
                gate_uses.append(BLOCKS[step[1]])
            if step[0] == "ln_act":
                gate_uses.append(step)
        out_uses = [(BLOCKS[s[1]][1], s[2]) for s in STEPS if s[0] == "proj" and s[1] >= len(PROJ)]
        v_uses = [s for s in STEPS if s[0] == "vtok" and s[3] == CH - 1]

        def low_part(engine, ops, src, c, k):
            x = wide[:, k % 4, :] if src == "norm" else xs[k][:, cs(c)]
            sg = s_lo[LO_BY[src][k]]
            engine.wait_ge(s_hhi.sem, s_hhi.at((src, c, k)))
            ops.tensor_tensor(H_lo[:, k, cs(c)], x, H_hi[:, k, cs(c)].bitcast(F32), ALU.subtract).then_inc(sg.sem, sg.mark((src, c, k)))

        def residual(engine, ops, c, k):
            x = xs[k][:, cs(c)]
            sg = s_new[NEW_BY[k]]
            engine.wait_ge(s_x[c].sem, s_x[c].at(c))
            engine.wait_ge(s_scaled.sem, s_scaled.at((c, k)))
            ops.tensor_tensor(x, x, old_x[:, k, cs(c)], ALU.add).then_inc(sg.sem, sg.mark((c, k)))

        def square_of_x(c, k):
            return raw_rot[:, k % 2, :] if c == 0 else first_squares[:, k, :]

        layer = ExitStack()
        block = layer.enter_context(nc.Block())

        @block.sync
        def _(sp):
            def load_pair(p):
                if p > 0:
                    sp.wait_ge(s_st.sem, s_st.at((p - 1, QB, 1)))
                    sp.wait_ge(s_dec.sem, s_dec.at((p - 1, QB)))
                    sp.wait_ge(s_stout.sem, s_stout.at(p - 1))
                sp.dma_start(decay[:], io["decay"][p]).then_inc(s_decay.sem, s_decay.mark(p, 16))
                sp.dma_start(state9[:], of_layer("state_ret", p)).then_inc(s_state9.sem, s_state9.mark(p, 16))

            def load_pages(p, name, s):
                for i in range(DEC_BATCH * N_PAGES):
                    a = io[name][bass.ds(l, 1), bass.ds(page_ids[i], 1), p]
                    sp.dma_start(page[:, i, :], a.rearrange("z y p n -> (z y p) n")).then_inc(s.sem, s.mark(p, 16))

            sp.dma_start(vec[:], of_layer("vec")).then_inc(s_vec.sem, s_vec.mark("vec", 16))
            load_pair(0)
            sp.wait_ge(s_pages, 16)
            page_ids = [sp.value_load(pages[0:1, i:i + 1], min_val=0, max_val=N_POOL - 1) for i in range(DEC_BATCH * N_PAGES)]
            sp.dma_start(glu9[:, :, :, 0:HIST], of_layer("state_conv")).then_inc(s_hist.sem, s_hist.mark("hist", 16))
            load_pages(0, "cache_k", s_pagek)
            for c in range(CH):
                sp.wait_ge(s_chunk[c], 16)
                sp.dma_start(io["yT"][:, :, cs(c)], MX[:, :, cs(c)]).then_inc(s_keep.sem, s_keep.mark("x", 16))
            for step in STEPS:
                kind = step[0]
                if kind == "glu_rest":
                    sp.wait_ge(s_glu.sem, s_glu.at("rest"))
                    sp.wait_ge(s_hist.sem, s_hist.at("hist"))
                    for b in range(CB):
                        sp.dma_start(of_layer("conv_p")[:, b], glu[b][:, SEQ - HIST:SEQ]).then_inc(s_out.sem, s_out.mark("conv", 16))
                    sp.dma_start(of_layer("conv_s"), glu9[:, :, :, DEC_SEQ:]).then_inc(s_out.sem, s_out.mark("conv", 16))
                elif kind == "vtok" and step[1] == "sv" and step[3] == 0:
                    p = step[2]
                    sp.wait_ge(s_copy.sem, s_copy.at(job_of("sv", p, CH - 1)))
                    sp.dma_start(of_layer("k_rows", p), sb_k[:]).then_inc(s_vout.sem, s_vout.mark(p, 16))
                    sp.dma_start(of_layer("v_rows", p), v_rows[:]).then_inc(s_vout.sem, s_vout.mark(p, 16))
                elif kind == "ds9" and step[2] == 1:
                    p = step[1]
                    sp.wait_ge(s_st.sem, s_st.at((p, QB, 1)))
                    sp.dma_start(of_layer("state_p", p), state[:]).then_inc(s_stout.sem, s_stout.mark(p, 16))
                    sp.dma_start(of_layer("state_s", p), state9[:]).then_inc(s_stout.sem, s_stout.mark(p, 16))
                    if p < PAIRS - 1:
                        load_pair(p + 1)
                elif kind == "sample_z":
                    sp.wait_ge(s_z.sem, s_z.at((step[1], "sample")))
                    load_pages(step[1], "cache_v", s_pagev)
                elif kind == "sample_v" and step[1] < PAIRS - 1:
                    sp.wait_ge(s_av.sem, s_av.at((step[1], "sample")))
                    load_pages(step[1] + 1, "cache_k", s_pagek)
                elif kind == "split" and step[1] == 0:
                    sp.wait_ge(s_av.sem, s_av.at((PAIRS - 1, "sample")))
                    sp.wait_ge(s_ds.sem, s_ds.at((PAIRS - 1, QB, 1)))
                    sp.wait_ge(s_vout.sem, s_vout.at(PAIRS - 1))
                    sp.wait_ge(s_keep.sem, s_keep.at("x"))
                    for c in range(CH):
                        sp.dma_start(old_x[:, :, cs(c)], io["yT"][:, :, cs(c)]).then_inc(s_x[c].sem, s_x[c].mark(c, 16))
                elif kind == "post":
                    c = step[1]
                    for k0 in (0, KB // 2):
                        for name, sg in s_new.items():
                            sp.wait_ge(sg.sem, sg.at((c, max(k for k in range(k0, k0 + KB // 2) if NEW_BY[k] == name))))
                        half = slice(k0, k0 + KB // 2)
                        sp.dma_start(io["yT"][:, half, cs(c)], MX[:, half, cs(c)]).then_inc(s_out.sem, s_out.mark("all", 16))
            sp.wait_ge(s_out.sem, s_out.at("all"))
            sp.wait_ge(s_stout.sem, s_stout.at(PAIRS - 1))
            sp.wait_ge(s_vout.sem, s_vout.at(PAIRS - 1))

        @block.tensor
        def _(pe):
            def claim(job):
                if jobs[job] >= 2:
                    pe.wait_ge(*drained(in_order[jobs[job] - 2]))

            for step in STEPS:
                kind = step[0]
                if kind == "root_y":
                    c = step[1]
                    pe.wait_ge(s_mid.sem, s_mid.at(("sum", KB - 1, c)))
                    nc.tensor.matmul(SUM_Y[c], ones, sumsq[:, c, :], start=True, stop=True).then_inc(s_sumy.sem, s_sumy.mark(c))
                elif kind == "proj":
                    i, c = step[1:]
                    claim(step)
                    if c == 0:
                        if i >= 2:
                            pe.wait_ge(s_wlo.sem, s_wlo.at(i))
                    for k in range(KB):
                        if i == 0 or i == len(PROJ):
                            wait_lo_of(pe, "norm" if i == 0 else "split", c, k)
                        a, b = w_hi[:, i % 2, k * P:(k + 1) * P], w_lo[:, i % 2, k * P:(k + 1) * P]
                        x, y = H_hi[:, k, cs(c)], H_lo[:, k, cs(c)]
                        nc.tensor.matmul(in_ring(step), a, x, start=(k == 0), stop=False)
                        nc.tensor.matmul(in_ring(step), a, y, start=False, stop=False)
                        last = nc.tensor.matmul(in_ring(step), b, x, start=False, stop=(k == KB - 1))
                    last.then_inc(s_full.sem, s_full.mark(step))
                elif kind == "rot":
                    _, name, p, c = step
                    claim(step)
                    pe.wait_ge(s_copy.sem, s_copy.at(job_of(name, p, c)))
                    nc.tensor.matmul(in_ring(step), rotm, raw_rot[:, rot_uses.index(step) % 2, :], start=True, stop=True).then_inc(
                        s_full.sem, s_full.mark(step))
                elif kind == "vtok":
                    _, name, p, j = step
                    claim(step)
                    if j == 0:
                        pe.wait_ge(s_copy.sem, s_copy.at(job_of(name, p, CH - 1)))
                    for n in range(3 * j, 3 * j + 3):
                        t0 = n * P if n < QB else LAST
                        last = nc.tensor.transpose(ring[jobs[step] % 2][:, (n - 3 * j) * P:(n - 3 * j + 1) * P],
                                                   v_rows[:, t0:t0 + P], ident)
                    last.then_inc(s_full.sem, s_full.mark(step))
                elif kind == "att":
                    p, n = step[1:]
                    w = P if n < QB else NS
                    claim(step)
                    pe.wait_ge(s_dec.sem, s_dec.at((p, n)))
                    nc.tensor.matmul(scores_of(p, n, w), kd[:, n % 2, :], qd[:, n % 2, :, 0:w], start=True, stop=True,
                                     skip_group_check=True)
                    nc.tensor.transpose(turned_keys(p, n), kd[:, n % 2, :], ident).then_inc(s_att.sem, s_att.mark((p, n)))
                elif kind == "ro":
                    p, n = step[1:]
                    w = P if n < QB else NS
                    claim(step)
                    if n == 0:
                        pe.wait_ge(s_copy.sem, s_copy.at(("vtok", "rv", p, CH - 1)))
                    else:
                        pe.wait_ge(s_st.sem, s_st.at((p, n - 1)))
                    out = outputs_of(p, n)
                    if 0 < n < QB:
                        for h in range(2):
                            nc.tensor.matmul(out, state[:], qd[:, n % 2, h, :], start=(h == 0), stop=False, skip_group_check=True)
                    pe.wait_ge(s_attm.sem, s_attm.at((p, n)))
                    for h in range(2):
                        r = slice(64 * h, 64 * h + 64)
                        last = nc.tensor.matmul(out[r, 0:w], ret_v[:, n, r], att[:, n % 2, h, 0:w],
                                                start=(n == 0 or n == QB), stop=(n < QB), skip_group_check=True)
                    if n == QB:
                        pe.wait_ge(s_state9.sem, s_state9.at(p))
                        for b in range(DEC_BATCH):
                            q = slice(b * DEC_SEQ, (b + 1) * DEC_SEQ)
                            last = nc.tensor.matmul(out[:, q], state9[:, b, :], qd9[:, q], start=False,
                                                    stop=(b == DEC_BATCH - 1), skip_group_check=True)
                    last.then_inc(s_ro.sem, s_ro.mark((p, n)))
                    if n < QB:
                        pe.wait_ge(s_kd.sem, s_kd.at((p, n)))
                        nc.tensor.matmul(increment(p, n), kd_tok[:, n % 2, :], ret_v[:, n, :], start=True, stop=True,
                                         skip_group_check=True).then_inc(s_ds.sem, s_ds.mark((p, n)))
                elif kind == "ds9":
                    _, p, g = step
                    claim(step)
                    pe.wait_ge(s_kd.sem, s_kd.at((p, QB)))
                    pe.wait_ge(s_own.sem, s_own.at((p, g)))
                    nc.tensor.matmul(bank_of(step)[:, :], kd_tok[:, QB % 2, :], v_own[:].rearrange("p b e -> p (b e)"),
                                     start=True, stop=True).then_inc(s_ds.sem, s_ds.mark((p, QB, g)))
                elif kind in ("gn_mean", "gn_var"):
                    _, p, c = step
                    claim(step)
                    if kind == "gn_mean":
                        pe.wait_ge(s_roc.sem, s_roc.at((p, QB)))
                        rhs = xs[p][:, cs(c)]
                    else:
                        pe.wait_ge(s_sqa.sem, s_sqa.at(step))
                        rhs = squares[:, sq_uses.index(step) % 2, :]
                    nc.tensor.matmul(in_ring(step), blk, rhs, start=True, stop=True).then_inc(s_full.sem, s_full.mark(step))
                elif kind in ("ln_mean", "ln_var"):
                    c = step[1]
                    claim(step)
                    for b in range(CB):
                        if kind == "ln_mean":
                            pe.wait_ge(s_tap.sem, s_tap.at(CONV_K - 1))
                            rhs = conv[b][:, cs(c)]
                        else:
                            pe.wait_ge(s_sqa.sem, s_sqa.at(("ln_var", c, b)))
                            rhs = squares[:, sq_uses.index(("ln_var", c, b)) % 2, :]
                        last = nc.tensor.matmul(in_ring(step), ch_mean, rhs, start=(b == 0), stop=(b == CB - 1))
                    last.then_inc(s_full.sem, s_full.mark(step))
                elif kind == "pw":
                    c = step[1]
                    pe.wait_ge(s_mid.sem, s_mid.at(("ln_act", CB - 1)))
                    for b in range(CB):
                        job = ("pw", b, c)
                        claim(job)
                        for k in range(CB):
                            last = nc.tensor.matmul(in_ring(job), pw[:, k, b * P:(b + 1) * P], conv[k][:, cs(c)],
                                                    start=(k == 0), stop=(k == CB - 1))
                        last.then_inc(s_full.sem, s_full.mark(job))
                elif kind == "score":
                    p, u = step[1:]
                    kb, q0, n = UNITS[u]
                    for h in range(2):
                        if u >= 2:
                            pe.wait_ge(s_a.sem, s_a.at((p, u - 2, h)))
                        elif h == 0 and u == 0:
                            if p > 0:
                                pe.wait_ge(s_a.sem, s_a.at((p - 1, "sample")))
                            pe.wait_ge(s_q.sem, s_q.at(job_of("sq", p, CH - 1)))
                            if p == 0:
                                pe.wait_ge(s_masks, 16)
                            pe.wait_ge(s_copy.sem, s_copy.at(job_of("sk", p, CH - 1)))
                        bk = Z[2 * (u % 2) + h]
                        diagonal = q0 == kb * P
                        last = nc.tensor.matmul(bk[:, 0:n], sb_k[:, kb * P:(kb + 1) * P], sb_q[:, h, q0:q0 + n],
                                                start=True, stop=not diagonal, skip_group_check=True)
                        if diagonal:
                            last = nc.tensor.matmul(bk[:, 0:P], ident_b[:], masks[:, 0:P], start=False, stop=True,
                                                    skip_group_check=True)
                        last.then_inc(s_z.sem, s_z.mark((p, u, h)))
                elif kind == "stop":
                    p, u = step[1:]
                    kb, q0, n = UNITS[u]
                    for h in range(2):
                        pe.wait_ge(s_sp.sem, s_sp.at((p, u, h)))
                        nc.tensor.matmul(Z[2 * (u % 2) + h][:, 0:n], negtri, stop[:, (2 * u + h) % 4, 0:n], start=False,
                                         stop=True, skip_group_check=True).then_inc(s_za.sem, s_za.mark((p, u, h)))
                    if kb > 0:
                        if UNITS[u - 1][0] > 0:
                            pe.wait_ge(s_keepf.sem, s_keepf.at((p, u - 1)))
                        elif p > 0:
                            pe.wait_ge(s_keepf.sem, s_keepf.at((p - 1, U - 1)))
                        for h in range(2):
                            last = nc.tensor.matmul(TOT[64 * h:64 * h + 64, 0:n], ones[:, 0:64], stop[:, (2 * u + h) % 4, 0:n],
                                                    start=True, stop=True, skip_group_check=True)
                        last.then_inc(s_tot.sem, s_tot.mark((p, u)))
                elif kind == "weigh":
                    p, u = step[1:]
                    kb, q0, n = UNITS[u]
                    if u == 0:
                        pe.wait_ge(s_copy.sem, s_copy.at(("vtok", "sv", p, CH - 1)))
                        if p > 0:
                            pe.wait_ge(s_o.sem, s_o.at((p - 1, "sample")))
                    else:
                        pe.wait_ge(s_o.sem, s_o.at((p, u - 1)))
                    for h in range(2):
                        pe.wait_ge(s_a.sem, s_a.at((p, u, h)))
                        last = nc.tensor.matmul(AV[64 * h:64 * h + 64, 0:n], sb_v[:, kb, 64 * h:64 * h + 64],
                                                weight[:, h, 0:n], start=True, stop=True, skip_group_check=True)
                    last.then_inc(s_av.sem, s_av.mark((p, u)))
                elif kind == "sample_z":
                    p = step[1]
                    w = 2 * NS
                    zs = z9.rearrange("p (g b n) -> p g b n", g=3, b=DEC_BATCH)
                    q9 = sb_q[:, :, SEQ:NT].rearrange("p h (b t) -> p b h t", b=DEC_BATCH)
                    pe.wait_ge(s_a.sem, s_a.at((p, U - 1, 1)))
                    pe.wait_ge(s_pagek.sem, s_pagek.at(p))
                    nc.tensor.matmul(z9[:, 2 * w:3 * w], sb_k[:, LAST:NT], q9, start=True, stop=False, skip_group_check=True)
                    nc.tensor.matmul(z9[:, 2 * w:3 * w], ident_b[:], masks[:, P:P + w], start=False, stop=False, skip_group_check=True)
                    for b in range(DEC_BATCH):
                        for g in range(N_PAGES):
                            last = nc.tensor.matmul(zs[:, g, b], page[:, b * N_PAGES + g, :], q9[:, b], start=False,
                                                    stop=False, skip_group_check=True)
                    last.then_inc(s_z.sem, s_z.mark((p, "sample")))
                elif kind == "sample_t":
                    p = step[1]
                    w = 2 * NS
                    pe.wait_ge(s_sp.sem, s_sp.at((p, "sample")))
                    s9 = stop9[:].rearrange("p g n -> p (g n)")
                    nc.tensor.matmul(z9, negtri, s9, start=False, stop=False, skip_group_check=True)
                    nc.tensor.matmul(z9[:, 0:2 * w], negones, s9[:, w:3 * w], start=False, stop=False, skip_group_check=True)
                    nc.tensor.matmul(z9[:, 0:w], negones, s9[:, 2 * w:3 * w], start=False, stop=True,
                                     skip_group_check=True).then_inc(s_za.sem, s_za.mark((p, "sample")))
                elif kind == "sample_v":
                    p = step[1]
                    w = 2 * NS
                    pe.wait_ge(s_a.sem, s_a.at((p, "sample")))
                    pe.wait_ge(s_pagev.sem, s_pagev.at(p))
                    pe.wait_ge(s_o.sem, s_o.at((p, U - 1)))
                    nc.tensor.matmul(AV[:, 0:w], sb_v[:, QB, :], weight9[:, 2, :], start=True, stop=False, skip_group_check=True)
                    for b in range(DEC_BATCH):
                        for g in range(N_PAGES):
                            q = slice(b * 2 * DEC_SEQ, (b + 1) * 2 * DEC_SEQ)
                            last = nc.tensor.matmul(AV[:, q], page[:, b * N_PAGES + g, :], weight9[:, g, q],
                                                    start=False, stop=(b == DEC_BATCH - 1 and g == N_PAGES - 1), skip_group_check=True)
                    last.then_inc(s_av.sem, s_av.mark((p, "sample")))
                elif kind == "sum_x":
                    c = step[1]
                    for k in range(KB):
                        pe.wait_ge(s_sqa.sem, s_sqa.at(("x", c, k)))
                        nc.tensor.matmul(SUM_X[c], ones, square_of_x(c, k), start=(k == 0), stop=(k == KB - 1)).then_inc(
                            s_sqm.sem, s_sqm.mark((c, k)))

        @block.scalar
        def _(act):
            def load_weights(i):
                if i > 2:
                    act.wait_ge(s_wlo.sem, s_wlo.at(i - 1))
                a = io["w"][bass.ds(l * len(BLOCKS) + i, 1)]
                act.dma_start(w_raw[:], a.rearrange("z p n -> (z p) n")).then_inc(s_w.sem, s_w.mark(i, 16))

            def weights_hi(i):
                act.wait_ge(s_w.sem, s_w.at(i))
                act.wait_ge(s_full.sem, s_full.at(("proj", i - 2, CH - 1)))
                nc.scalar.activation(w_hi[:, i % 2, :], w_raw[:], ACT.Copy).then_inc(s_whi.sem, s_whi.mark(i))

            def root(src, scale, use):
                n = root_uses.index(use)
                if n >= 1:
                    old = root_uses[n - 1]
                    act.wait_ge(s_mid.sem, s_mid.at(("root", n - 1)))
                nc.scalar.activation(rstd[:, 0, :], src, ACT.Ln, bias=eps, scale=scale).then_inc(s_ln.sem, s_ln.mark(use))
                act.wait_ge(s_ln.sem, s_ln.at(use))
                nc.scalar.activation(rstd[:, 0, :], rstd[:, 0, :], ACT.Exp, scale=-0.5).then_inc(
                    s_rstd.sem, s_rstd.mark(use))

            def root_of_row(sums, use, c):
                nc.scalar.activation(gate[:, cs(c)], sums[c], ACT.Ln, bias=eps, scale=1.0 / D_MODEL).then_inc(s_ln.sem, s_ln.mark((use, c)))
                act.wait_ge(s_ln.sem, s_ln.at((use, c)))
                nc.scalar.activation(gate[:, cs(c)], gate[:, cs(c)], ACT.Exp, scale=-0.5).then_inc(s_rstd.sem, s_rstd.mark((use, c)))

            def square_x(c, k):
                if c == 0:
                    wait_new(act, c, k)
                    if k >= 2:
                        act.wait_ge(s_sqm.sem, s_sqm.at((c, k - 2)))
                    else:
                        act.wait_ge(s_rope.sem, s_rope.at(rot_uses[-1]))
                elif c == 2:
                    act.wait_ge(s_sqm.sem, s_sqm.at((1, k)))
                if c > 0 and k == 0:
                    act.wait_ge(s_chunk[c], 16)
                nc.scalar.activation(square_of_x(c, k), xs[k][:, cs(c)], ACT.Square).then_inc(s_sqa.sem, s_sqa.mark(("x", c, k)))

            def square(src, use):
                n = sq_uses.index(use)
                if n < 2:
                    wait_lo(act, "norm", CH - 1)
                else:
                    old = sq_uses[n - 2]
                    act.wait_ge(s_full.sem, s_full.at(old if old[0] == "gn_var" else old[:2]))
                nc.scalar.activation(squares[:, n % 2, :], src, ACT.Square).then_inc(s_sqa.sem, s_sqa.mark(use))

            def gate_free(use):
                n = gate_uses.index(use)
                if n == 0:
                    act.wait_ge(s_hx.sem, s_hx.at((CH - 1, KB - 1)))
                else:
                    old = gate_uses[n - 1]
                    s = s_mid if old[0] == "ln_act" else (s_glu if old[0] == "cb" else s_mix)
                    act.wait_ge(s.sem, s.at(old))

            def sigmoid(src, use, **affine):
                nc.scalar.activation(gate[:], src, ACT.Sigmoid, **affine).then_inc(s_sig.sem, s_sig.mark(use))
                nc.scalar.preload_act_table_set(EXP_LN)

            def exp_scores(p, u):
                kb, q0, n = UNITS[u]
                if u >= 2:
                    act.wait_ge(s_za.sem, s_za.at((p, u - 2, 1)))
                    if UNITS[u - 2][0] > 0:
                        act.wait_ge(s_tot.sem, s_tot.at((p, u - 2)))
                elif p > 0:
                    act.wait_ge(s_tot.sem, s_tot.at((p - 1, U - 1)))
                for h in range(2):
                    act.wait_ge(s_z.sem, s_z.at((p, u, h)))
                    nc.scalar.activation(stop[:, (2 * u + h) % 4, 0:n], Z[2 * (u % 2) + h][:, 0:n], ACT.Exp,
                                         bias=vv(V_BIAS + 2 * p + h)).then_inc(s_e.sem, s_e.mark((p, u, h)))

            def ln_scores(p, u):
                n = UNITS[u][2]
                for h in range(2):
                    s = stop[:, (2 * u + h) % 4, 0:n]
                    act.wait_ge(s_min.sem, s_min.at((p, u, h)))
                    nc.scalar.activation(s, s, ACT.Ln, bias=1.0).then_inc(s_l.sem, s_l.mark((p, u, h)))

            load_weights(2)
            for step in STEPS:
                kind = step[0]
                if kind == "root_x":
                    c = step[1]
                    if c > 0:
                        act.wait_ge(s_sqm.sem, s_sqm.at((c, KB - 1)))
                    root_of_row(SUM_X, "x", c)
                elif kind == "root_y":
                    c = step[1]
                    if c == 0:
                        nc.scalar.preload_act_table_set(EXP_LN)
                    act.wait_ge(s_sumy.sem, s_sumy.at(c))
                    root_of_row(SUM_Y, "y", c)
                elif kind == "norm":
                    c = step[1]
                    for k in range(KB):
                        act.wait_ge(s_hx.sem, s_hx.at((c, k)))
                        nc.scalar.activation(H_hi[:, k, cs(c)], wide[:, k % 4, :], ACT.Copy).then_inc(
                            s_hhi.sem, s_hhi.mark(("norm", c, k)))
                        if k < KB // 2 and c + 1 < CH:
                            square_x(c + 1, 2 * k)
                            square_x(c + 1, 2 * k + 1)
                    if c == 0:
                        act.wait_ge(s_vec.sem, s_vec.at("vec"))
                elif kind == "proj":
                    i, c = step[1:]
                    name, j = BLOCKS[i]
                    if c == 0 and 2 <= i < B - 1:
                        weights_hi(i + 1)
                    if (i, c) in [(i, 2)] * (1 <= i < B - 2) + [(B - 2, 1)]:
                        load_weights(i + 2)
                    act.wait_ge(s_full.sem, s_full.at(step))
                    src = in_ring(step)
                    if name in ("rq", "rk"):
                        n = rot_uses.index(("rot", name, j, c))
                        if n >= 2:
                            act.wait_ge(s_rope.sem, s_rope.at(rot_uses[n - 2]))
                        nc.scalar.activation(raw_rot[:, n % 2, :], src, ACT.Copy).then_inc(s_copy.sem, s_copy.mark(step))
                    elif name in ("rv", "sv"):
                        n = v_uses.index(("vtok", name, j, CH - 1))
                        if c == 0 and n > 0:
                            act.wait_ge(s_full.sem, s_full.at(v_uses[n - 1]))
                            if name == "rv":
                                act.wait_ge(s_vout.sem, s_vout.at(j))
                        nc.scalar.activation(v_rows[:, cs(c)], src, ACT.Copy).then_inc(s_copy.sem, s_copy.mark(step))
                    elif name == "sk":
                        if j > 0 and c == 0:
                            act.wait_ge(s_z.sem, s_z.at((j - 1, "sample")))
                            act.wait_ge(s_vout.sem, s_vout.at(j - 1))
                        nc.scalar.activation(sb_k[:, cs(c)], src, ACT.Copy).then_inc(s_copy.sem, s_copy.mark(step))
                    elif name == "ca":
                        act.wait_ge(s_hx.sem, s_hx.at((CH - 1, KB - 1)))
                        act.wait_ge(s_keep.sem, s_keep.at("x"))
                        nc.scalar.activation(glu[j][:, cs(c)], src, ACT.Copy).then_inc(s_copy.sem, s_copy.mark(step))
                    elif (name, j) == ("sg", PAIRS - 1):
                        if c == 0:
                            gate_free((name, j))
                        nc.scalar.activation(gate[:, cs(c)], src, ACT.Sigmoid).then_inc(s_sig.sem, s_sig.mark(step))
                    elif name in ("cb", "rg", "sg", "cg"):
                        if c == 0:
                            gate_free((name, j))
                        nc.scalar.activation(gate[:, cs(c)], src, ACT.Copy).then_inc(s_copy.sem, s_copy.mark(step))
                        if c == CH - 1:
                            act.wait_ge(s_copy.sem, s_copy.at(step))
                            sigmoid(gate[:], (name, j))
                    elif name == "out":
                        nc.scalar.activation(xs[j][:, cs(c)], src, ACT.Copy).then_inc(s_copy.sem, s_copy.mark(step))
                        n = out_uses.index((j, c))
                        if n >= 2:
                            act.wait_ge(s_mid.sem, s_mid.at(("sum", *out_uses[n - 2])))
                        else:
                            act.wait_ge(s_full.sem, s_full.at(("gn_var", PAIRS - 1, CH - 1)))
                        nc.scalar.activation(squares[:, n % 2, :], src, ACT.Square).then_inc(
                            s_sqo.sem, s_sqo.mark(step))
                    if (i, c) in ((0, 2), (B - 2, 2)):
                        weights_hi(i + 2)
                    if (i, c) == (B - 1, 2):
                        load_weights(B + 1)
                elif kind == "vtok":
                    _, name, p, j = step
                    if p > 0 and j == 0:
                        if name == "rv":
                            act.wait_ge(s_ds.sem, s_ds.at((p - 1, QB, 1)))
                        else:
                            act.wait_ge(s_av.sem, s_av.at((p - 1, "sample")))
                    to = ret_v if name == "rv" else sb_v
                    act.wait_ge(s_full.sem, s_full.at(step))
                    nc.scalar.activation(to[:, 3 * j:3 * j + 3, :],
                                         ring[jobs[step] % 2][:, 0:3 * P].rearrange("p (n e) -> p n e", n=3),
                                         ACT.Copy).then_inc(s_copy.sem, s_copy.mark(step))
                elif kind == "att":
                    p, n = step[1:]
                    act.wait_ge(s_attm.sem, s_attm.at((p, n)))
                    if n >= 2:
                        act.wait_ge(s_ds.sem, s_ds.at((p, n - 2)))
                    elif p > 0:
                        act.wait_ge(s_ds.sem, s_ds.at((p - 1, QB, 1)))
                    nc.scalar.activation(kd_tok[:, n % 2, :], turned_keys(p, n), ACT.Copy).then_inc(s_kd.sem, s_kd.mark((p, n)))
                elif kind == "ro":
                    p, n = step[1:]
                    t0, w = (n * P, P) if n < QB else (SEQ, NS)
                    if p == GLU_SLOT[0]:
                        act.wait_ge(s_tap.sem, s_tap.at(CONV_K - 1))
                        act.wait_ge(s_out.sem, s_out.at("conv"))
                    act.wait_ge(s_hx.sem, s_hx.at((CH - 1, KB - 1)))
                    if n < QB:
                        act.wait_ge(s_st.sem, s_st.at((p, n, "sum")))
                    act.wait_ge(s_ro.sem, s_ro.at((p, n)))
                    nc.scalar.activation(xs[p][:, t0:t0 + w], outputs_of(p, n)[:, 0:w], ACT.Copy).then_inc(s_roc.sem, s_roc.mark((p, n)))
                elif kind == "gn_mean":
                    act.wait_ge(s_mid.sem, s_mid.at(step))
                    square(xs[step[1]][:, cs(step[2])], ("gn_var", step[1], step[2]))
                elif kind == "gn_var":
                    act.wait_ge(s_full.sem, s_full.at(step))
                    root(in_ring(step), 1.0, step)
                elif kind == "ln_mean":
                    for b in range(CB):
                        act.wait_ge(s_mid.sem, s_mid.at(step))
                        square(conv[b][:, cs(step[1])], ("ln_var", step[1], b))
                elif kind == "ln_var":
                    act.wait_ge(s_full.sem, s_full.at(step))
                    root(in_ring(step), 1.0, step)
                elif kind == "ln_act":
                    b = step[1]
                    gate_free(step)
                    act.wait_ge(s_mid.sem, s_mid.at(("ln_n", CH - 1, CB - 1)))
                    sigmoid(conv[b], step, scale=vv(V_LNW + b), bias=vv(V_LNB + b))
                elif kind == "pw":
                    c = step[1]
                    act.wait_ge(s_full.sem, s_full.at(("pw", CB - 1, c)))
                    for b in range(CB):
                        nc.scalar.activation(conv[b][:, cs(c)], in_ring(("pw", b, c)), ACT.Copy).then_inc(
                            s_copy.sem, s_copy.mark(("pw", b, c)))
                elif kind == "score":
                    p, u = step[1:]
                    exp_scores(p, u)
                    if u == 0:
                        ln_scores(p, u)
                elif kind == "stop":
                    p, u = step[1:]
                    kb, q0, n = UNITS[u]
                    if u >= 1:
                        act.wait_ge(s_av.sem, s_av.at((p, u - 1)))
                    elif p > 0:
                        act.wait_ge(s_av.sem, s_av.at((p - 1, U - 1)))
                    for h in range(2):
                        act.wait_ge(s_za.sem, s_za.at((p, u, h)))
                        nc.scalar.activation(weight[:, h, 0:n], Z[2 * (u % 2) + h][:, 0:n], ACT.Exp,
                                             bias=vv(V_BIAS + 2 * p + h)).then_inc(s_a.sem, s_a.mark((p, u, h)))
                    if kb > 0:
                        act.wait_ge(s_tot.sem, s_tot.at((p, u)))
                        act.wait_ge(s_o.sem, s_o.at((p, u - 1)))
                        nc.scalar.activation(keep[:, 0:n], TOT[:, 0:n], ACT.Exp, scale=-1.0).then_inc(
                            s_keepf.sem, s_keepf.mark((p, u)))
                elif kind == "weigh":
                    p, u = step[1:]
                    if u + 1 < U:
                        ln_scores(p, u + 1)
                elif kind in ("sample_z", "sample_t"):
                    p = step[1]
                    name, to, ready, done = ("e", stop9, s_z, s_e) if kind == "sample_z" else ("a", weight9, s_za, s_a)
                    act.wait_ge(ready.sem, ready.at((p, "sample")))
                    if p > 0 and name == "e":
                        act.wait_ge(s_av.sem, s_av.at((p - 1, "sample")))
                    for h in range(2):
                        last = nc.scalar.activation(of_head(to[:].rearrange("p g n -> p (g n)"), h), of_head(z9, h), ACT.Exp,
                                                    bias=vv(V_BIAS + 2 * p + h))
                    last.then_inc(done.sem, done.mark((p, "sample")))
                    if name == "e":
                        act.wait_ge(s_min.sem, s_min.at((p, "sample")))
                        nc.scalar.activation(stop9[:], stop9[:], ACT.Ln, bias=1.0).then_inc(s_l.sem, s_l.mark((p, "sample")))
                elif kind == "split":
                    c = step[1]
                    act.wait_ge(s_full.sem, s_full.at(job_of("sg", PAIRS - 1, c)))
                    for k in range(KB):
                        if k == 2 * PAIRS - 1:
                            act.wait_ge(s_mix.sem, s_mix.at(job_of("sg", PAIRS - 1, c)))
                        else:
                            act.wait_ge(s_mix.sem, s_mix.at(("rg", k) if k < PAIRS else ("sg", k - PAIRS) if k < 2 * PAIRS else ("cg", k - 2 * PAIRS)))
                        nc.scalar.activation(H_hi[:, k, cs(c)], xs[k][:, cs(c)], ACT.Copy).then_inc(
                            s_hhi.sem, s_hhi.mark(("split", c, k)))
                elif kind == "sum_x" and step[1] == 0:
                    for k in range(KB):
                        square_x(0, k)
                    weights_hi(B + 1)

        @block.vector
        def _(dve):
            def softplus(p, u):
                n = UNITS[u][2]
                for h in range(2):
                    s = stop[:, (2 * u + h) % 4, 0:n]
                    dve.wait_ge(s_l.sem, s_l.at((p, u, h)))
                    nc.vector.scalar_tensor_tensor(out=s, in0=Z[2 * (u % 2) + h][:, 0:n], scalar=vv(V_BIAS + 2 * p + h), in1=s,
                                                   op0=ALU.add, op1=ALU.max).then_inc(s_sp.sem, s_sp.mark((p, u, h)))

            dve.wait_ge(s_vec.sem, s_vec.at("vec"))
            for step in STEPS:
                kind = step[0]
                if kind == "norm":
                    c = step[1]
                    if c > 0:
                        dve.wait_ge(s_chunk[c], 16)
                    dve.wait_ge(s_rstd.sem, s_rstd.at(("x", c)))
                    for k in range(KB + 2):
                        if k < KB:
                            if k >= 4:
                                wait_lo_of(dve, "norm", c, k - 4)
                            elif c > 0:
                                wait_lo_of(dve, "norm", c - 1, k + KB - 4)
                            nc.vector.scalar_tensor_tensor(out=wide[:, k % 4, :], in0=xs[k][:, cs(c)], scalar=vv(V_PRE + k),
                                                           in1=gate[:, cs(c)], op0=ALU.mult, op1=ALU.mult).then_inc(
                                s_hx.sem, s_hx.mark((c, k)))
                        if k >= 2 and LO_BY["norm"][k - 2] == "dve":
                            low_part(dve, nc.vector, "norm", c, k - 2)
                elif kind == "proj":
                    i, c = step[1:]
                    name, j = BLOCKS[i]
                    src = in_ring(step)
                    if name == "sq":
                        if j > 0 and c == 0:
                            dve.wait_ge(s_z.sem, s_z.at((j - 1, "sample")))
                        dve.wait_ge(s_full.sem, s_full.at(step))
                        for h in range(2):
                            r = slice(64 * h, 64 * h + 64)
                            last = nc.vector.tensor_scalar(sb_q[r, h, cs(c)], src[r], HEAD_DIM ** -0.5, None, ALU.mult)
                        last.then_inc(s_q.sem, s_q.mark(step))
                    elif name == "cb" and c == CH - 1:
                        dve.wait_ge(s_sig.sem, s_sig.at((name, j)))
                        nc.vector.tensor_tensor(glu[j], glu[j], gate[:], ALU.mult).then_inc(s_glu.sem, s_glu.mark((name, j)))
                    elif name in ("rg", "sg", "cg"):
                        k = j + {"rg": 0, "sg": PAIRS, "cg": 2 * PAIRS}[name]
                        x = xs[k][:, cs(c)]
                        if name == "rg":
                            dve.wait_ge(s_mid.sem, s_mid.at(("gn_n", j, c)))
                        elif name == "sg":
                            dve.wait_ge(s_o.sem, s_o.at((j, "sample")))
                        else:
                            dve.wait_ge(s_copy.sem, s_copy.at(("pw", j, c)))
                        final = (name, j) == ("sg", PAIRS - 1)
                        left = s_sig if final else s_copy
                        dve.wait_ge(left.sem, left.at(step))
                        if name == "rg":
                            last = nc.vector.scalar_tensor_tensor(out=x, in0=x, scalar=vv(V_GN + j), in1=src, op0=ALU.mult, op1=ALU.mult)
                        else:
                            last = nc.vector.tensor_tensor(x, x, src, ALU.mult)
                        last.then_inc(s_gate.sem, s_gate.mark(step))
                        if final:
                            dve.wait_ge(s_gate.sem, s_gate.at(step))
                            nc.vector.tensor_tensor(x, x, gate[:, cs(c)], ALU.mult).then_inc(s_mix.sem, s_mix.mark(step))
                        elif c == CH - 1:
                            dve.wait_ge(s_gate.sem, s_gate.at(step))
                            dve.wait_ge(s_sig.sem, s_sig.at((name, j)))
                            nc.vector.tensor_tensor(xs[k], xs[k], gate[:], ALU.mult).then_inc(s_mix.sem, s_mix.mark((name, j)))
                    elif name == "out":
                        dve.wait_ge(s_sqo.sem, s_sqo.at(step))
                        s = squares[:, out_uses.index((j, c)) % 2, :]
                        if j == 0:
                            dve.wait_ge(s_z.sem, s_z.at((PAIRS - 1, "sample")))
                            dve.wait_ge(s_vout.sem, s_vout.at(PAIRS - 1))
                            nc.vector.tensor_copy(sumsq[:, c, :], s).then_inc(s_mid.sem, s_mid.mark(("sum", j, c)))
                        else:
                            dve.wait_ge(s_mid.sem, s_mid.at(("sum", j - 1, c)))
                            nc.vector.tensor_tensor(sumsq[:, c, :], sumsq[:, c, :], s, ALU.add).then_inc(
                                s_mid.sem, s_mid.mark(("sum", j, c)))
                elif kind == "rot":
                    _, name, p, c = step
                    n = rot_uses.index(step)
                    dve.wait_ge(s_full.sem, s_full.at(step))
                    dve.wait_ge(s_rota.sem, s_rota.at(step))
                    if n == 0:
                        dve.wait_ge(s_turn, 16)
                    nc.vector.tensor_tensor(raw_rot[:, n % 2, :], in_ring(step), turn[:, 1, cs(c)], ALU.mult).then_inc(
                        s_rotb.sem, s_rotb.mark(step))
                    dve.wait_ge(s_rotb.sem, s_rotb.at(step))
                    if p > 0 and c == 0:
                        dve.wait_ge(s_dec.sem, s_dec.at((p - 1, QB)))
                    to = ret_q if name == "rq" else ret_k
                    nc.vector.tensor_tensor(to[:, cs(c)], rot_a[:, n % 2, :], raw_rot[:, n % 2, :], ALU.add).then_inc(
                        s_rope.sem, s_rope.mark(step))
                elif kind == "glu_rest":
                    dve.wait_ge(s_glu.sem, s_glu.at(("cb", CB - 1)))
                    for b in range(CB):
                        last = nc.vector.tensor_copy(glu9[:, b, :, HIST:], glu[b][:, SEQ:NT].rearrange("p (b t) -> p b t", b=DEC_BATCH))
                    last.then_inc(s_glu.sem, s_glu.mark("rest"))
                    dve.wait_ge(s_glu.sem, s_glu.at("rest"))
                    for b in range(CB):
                        w = vv(V_DW + b * CONV_K + CONV_K - 1)
                        nc.vector.tensor_scalar(conv[b][:, 0:SEQ], glu[b][:, 0:SEQ], w, vv(V_DWB + b), ALU.mult, ALU.add)
                        last = nc.vector.tensor_scalar(conv[b][:, SEQ:NT].rearrange("p (b t) -> p b t", b=DEC_BATCH),
                                                       glu9[:, b, :, HIST:], w, vv(V_DWB + b), ALU.mult, ALU.add)
                        last.then_inc(s_tap.sem, s_tap.mark((0, b)))
                    dve.wait_ge(s_hist.sem, s_hist.at("hist"))
                elif kind == "taps":
                    _, s, b = step
                    w = vv(V_DW + b * CONV_K + CONV_K - 1 - s)
                    dve.wait_ge(s_tap.sem, s_tap.at((s - 1, b)))
                    y, y9 = conv[b][:, s:SEQ], conv[b][:, SEQ:NT].rearrange("p (b t) -> p b t", b=DEC_BATCH)
                    nc.vector.scalar_tensor_tensor(out=y, in0=glu[b][:, 0:SEQ - s], scalar=w, in1=y, op0=ALU.mult, op1=ALU.add)
                    last = nc.vector.scalar_tensor_tensor(out=y9, in0=glu9[:, b, :, HIST - s:HIST - s + DEC_SEQ], scalar=w,
                                                          in1=y9, op0=ALU.mult, op1=ALU.add)
                    last.then_inc(s_tap.sem, s_tap.mark((s, b)))
                    if (s, b) == (CONV_K - 1, CB - 1):
                        s_tap.alias(CONV_K - 1)
                elif kind == "att":
                    p, n = step[1:]
                    w = P if n < QB else NS
                    dve.wait_ge(s_att.sem, s_att.at((p, n)))
                    if n >= 2:
                        dve.wait_ge(s_ro.sem, s_ro.at((p, n - 2)))
                    elif p > 0:
                        dve.wait_ge(s_ro.sem, s_ro.at((p - 1, QB)))
                    ok = (causal if n < QB else causal9).unsqueeze(1).to_broadcast([P, 2, w])
                    last = nc.vector.tensor_tensor(att[:, n % 2, :, 0:w], scores_of(p, n, w), ok, ALU.mult)
                    last.then_inc(s_attm.sem, s_attm.mark((p, n)))
                elif kind == "ro" and step[2] < QB:
                    p, n = step[1:]
                    if n == 0:
                        dve.wait_ge(s_decay.sem, s_decay.at(p))
                        if p > 0:
                            dve.wait_ge(s_stout.sem, s_stout.at(p - 1))
                        dve.wait_ge(s_ds.sem, s_ds.at((p, n)))
                        nc.vector.scalar_tensor_tensor(out=state[:], in0=increment(p, n), scalar=decay[:, D_STEP:D_STEP + 1], in1=blk,
                                                       op0=ALU.mult, op1=ALU.mult).then_inc(
                            s_st.sem, s_st.mark((p, n)))
                        s_st.alias((p, n, "sum"))
                    else:
                        dve.wait_ge(s_ds.sem, s_ds.at((p, n)))
                        dve.wait_ge(s_st.sem, s_st.at((p, n - 1)))
                        nc.vector.tensor_tensor(state[:], state[:], increment(p, n), ALU.add).then_inc(s_st.sem, s_st.mark((p, n, "sum")))
                        dve.wait_ge(s_st.sem, s_st.at((p, n, "sum")))
                        nc.vector.scalar_tensor_tensor(out=state[:], in0=state[:], scalar=decay[:, D_STEP:D_STEP + 1], in1=blk,
                                                       op0=ALU.mult, op1=ALU.mult).then_inc(
                            s_st.sem, s_st.mark((p, n)))
                elif kind == "ds9":
                    _, p, g = step
                    x = state9[:, 4 * g:4 * g + 4, :]
                    dve.wait_ge(s_ro.sem, s_ro.at((p, QB)))
                    dve.wait_ge(s_ds.sem, s_ds.at((p, QB, g)))
                    nc.vector.tensor_tensor(x, x, bank_of(step)[:, :].rearrange("p (b e) -> p b e", b=4), ALU.add).then_inc(
                        s_st.sem, s_st.mark((p, QB, g, "sum")))
                    dve.wait_ge(s_st.sem, s_st.at((p, QB, g, "sum")))
                    nc.vector.scalar_tensor_tensor(out=x, in0=x, scalar=decay[:, D_STEP9:D_STEP9 + 1], in1=blk.unsqueeze(1).to_broadcast([P, 4, P]),
                                                   op0=ALU.mult, op1=ALU.mult).then_inc(s_st.sem, s_st.mark((p, QB, g)))
                elif kind == "gn_mean":
                    _, p, c = step
                    dve.wait_ge(s_full.sem, s_full.at(step))
                    nc.vector.tensor_tensor(xs[p][:, cs(c)], xs[p][:, cs(c)], in_ring(step), ALU.subtract).then_inc(
                        s_mid.sem, s_mid.mark(step))
                elif kind == "gn_var":
                    _, p, c = step
                    n = root_uses.index(step)
                    dve.wait_ge(s_rstd.sem, s_rstd.at(step))
                    dve.wait_ge(s_mid.sem, s_mid.at(("gn_mean", p, c)))
                    nc.vector.tensor_tensor(xs[p][:, cs(c)], xs[p][:, cs(c)], rstd[:, 0, :], ALU.mult).then_inc(
                        s_mid.sem, s_mid.mark(("gn_n", p, c)))
                    s_mid.alias(("root", n))
                elif kind == "ln_mean":
                    c = step[1]
                    dve.wait_ge(s_full.sem, s_full.at(step))
                    for b in range(CB):
                        last = nc.vector.tensor_tensor(conv[b][:, cs(c)], conv[b][:, cs(c)], in_ring(step), ALU.subtract)
                    last.then_inc(s_mid.sem, s_mid.mark(step))
                elif kind == "ln_var":
                    c = step[1]
                    n = root_uses.index(step)
                    dve.wait_ge(s_rstd.sem, s_rstd.at(step))
                    dve.wait_ge(s_mid.sem, s_mid.at(("ln_mean", c)))
                    for b in range(CB):
                        nc.vector.tensor_tensor(conv[b][:, cs(c)], conv[b][:, cs(c)], rstd[:, 0, :], ALU.mult).then_inc(
                            s_mid.sem, s_mid.mark(("ln_n", c, b)))
                    s_mid.alias(("root", n))
                elif kind == "ln_act":
                    b = step[1]
                    dve.wait_ge(s_sig.sem, s_sig.at(step))
                    nc.vector.tensor_scalar(conv[b], conv[b], vv(V_LNW + b), vv(V_LNB + b), ALU.mult, ALU.add).then_inc(
                        s_mid.sem, s_mid.mark(("ln_l", b)))
                    dve.wait_ge(s_mid.sem, s_mid.at(("ln_l", b)))
                    nc.vector.tensor_tensor(conv[b], conv[b], gate[:], ALU.mult).then_inc(s_mid.sem, s_mid.mark(step))
                elif kind == "score":
                    if step[2] == 0:
                        softplus(*step[1:])
                elif kind == "weigh":
                    p, u = step[1:]
                    kb, q0, n = UNITS[u]
                    if u + 1 < U:
                        softplus(p, u + 1)
                    o = stick[p][:, q0:q0 + n]
                    dve.wait_ge(s_av.sem, s_av.at((p, u)))
                    if kb == 0:
                        if p == 0:
                            dve.wait_ge(s_keep.sem, s_keep.at("x"))
                        if p == 2:
                            dve.wait_ge(s_tap.sem, s_tap.at(CONV_K - 1))
                            dve.wait_ge(s_out.sem, s_out.at("conv"))
                        nc.vector.tensor_copy(o, AV[:, 0:n]).then_inc(s_o.sem, s_o.mark((p, u)))
                    else:
                        dve.wait_ge(s_keepf.sem, s_keepf.at((p, u)))
                        dve.wait_ge(s_o.sem, s_o.at((p, u - 1)))
                        nc.vector.tensor_tensor(o, o, keep[:, 0:n], ALU.mult).then_inc(s_kept.sem, s_kept.mark((p, u)))
                        dve.wait_ge(s_kept.sem, s_kept.at((p, u)))
                        nc.vector.tensor_tensor(o, o, AV[:, 0:n], ALU.add).then_inc(s_o.sem, s_o.mark((p, u)))
                elif kind == "sample_z":
                    p = step[1]
                    dve.wait_ge(s_l.sem, s_l.at((p, "sample")))
                    s9 = stop9[:].rearrange("p g n -> p (g n)")
                    for h in range(2):
                        last = nc.vector.scalar_tensor_tensor(out=of_head(s9, h), in0=of_head(z9, h), scalar=vv(V_BIAS + 2 * p + h),
                                                              in1=of_head(s9, h), op0=ALU.add, op1=ALU.max)
                    last.then_inc(s_sp.sem, s_sp.mark((p, "sample")))
                elif kind == "sample_v":
                    p = step[1]
                    dve.wait_ge(s_av.sem, s_av.at((p, "sample")))
                    for h in range(2):
                        r = slice(64 * h, 64 * h + 64)
                        last = nc.vector.tensor_copy(stick[p][r, SEQ:NT].rearrange("p (b t) -> p b t", b=DEC_BATCH),
                                                     of_head(AV[r, 0:2 * NS], h))
                    last.then_inc(s_o.sem, s_o.mark((p, "sample")))
                elif kind == "split":
                    c = step[1]
                    for k in range(KB):
                        if LO_BY["split"][k] == "dve":
                            low_part(dve, nc.vector, "split", c, k)
                elif kind == "post":
                    c = step[1]
                    dve.wait_ge(s_rstd.sem, s_rstd.at(("y", c)))
                    for k in range(KB):
                        x = xs[k][:, cs(c)]
                        nc.vector.scalar_tensor_tensor(out=x, in0=x, scalar=vv(V_POST + k), in1=gate[:, cs(c)], op0=ALU.mult,
                                                       op1=ALU.mult).then_inc(s_scaled.sem, s_scaled.mark((c, k)))
                        if NEW_BY[k] == "dve":
                            residual(dve, nc.vector, c, k)

        @block.gpsimd
        def _(pool):
            def weights_lo(i):
                pool.wait_ge(s_whi.sem, s_whi.at(i))
                pool.wait_ge(s_full.sem, s_full.at(("proj", i - 2, CH - 1)))
                nc.gpsimd.tensor_tensor(w_lo[:, i % 2, :], w_raw[:], w_hi[:, i % 2, :].bitcast(F32), ALU.subtract).then_inc(
                    s_wlo.sem, s_wlo.mark(i))

            def decays(p, n):
                if n > QB:
                    return
                if n >= 2:
                    pool.wait_ge(s_ro.sem, s_ro.at((p, n - 2)))
                elif p > 0:
                    pool.wait_ge(s_ro.sem, s_ro.at((p - 1, QB)))
                a, b, w = (n * P, n * P, P) if n < QB else (SEQ, LAST, NS)
                dq, dk = (D_Q, D_K) if n < QB else (D_Q9, D_K9)
                nc.gpsimd.tensor_tensor(qd[:, n % 2, :, 0:w], ret_q[:, a:a + w].unsqueeze(1).to_broadcast([P, 2, w]),
                                        decay[:, dq:dq + 2 * w].rearrange("p (h w) -> p h w", h=2), ALU.mult)
                if n == QB:
                    nc.gpsimd.tensor_tensor(qd9, ret_q[:, a:a + w], decay[:, D_BOTH9:D_BOTH9 + NS], ALU.mult)
                nc.gpsimd.tensor_tensor(kd[:, n % 2, :], ret_k[:, b:b + P], decay[:, dk:dk + P], ALU.mult).then_inc(
                    s_dec.sem, s_dec.mark((p, n)))

            for step in STEPS:
                kind = step[0]
                if kind == "proj":
                    i, c = step[1:]
                    name, j = BLOCKS[i]
                    if c == 0 and 2 <= i < B - 1:
                        weights_lo(i + 1)
                    if (i, c) in ((0, 2), (B - 2, 2)):
                        weights_lo(i + 2)
                    if name in ("rq", "rk"):
                        use = ("rot", name, j, c)
                        n = rot_uses.index(use)
                        if n >= 2:
                            pool.wait_ge(s_rope.sem, s_rope.at(rot_uses[n - 2]))
                        if n == 0:
                            pool.wait_ge(s_turn, 16)
                        pool.wait_ge(s_copy.sem, s_copy.at(step))
                        nc.gpsimd.tensor_tensor(rot_a[:, n % 2, :], raw_rot[:, n % 2, :], turn[:, 0, cs(c)], ALU.mult).then_inc(
                            s_rota.sem, s_rota.mark(use))
                elif kind == "att":
                    p, n = step[1:]
                    if n == 0:
                        pool.wait_ge(s_decay.sem, s_decay.at(p))
                        pool.wait_ge(s_rope.sem, s_rope.at(("rot", "rk", p, CH - 1)))
                        decays(p, 0)
                    decays(p, n + 1)
                elif kind == "ds9":
                    _, p, g = step
                    pool.wait_ge(s_copy.sem, s_copy.at(("vtok", "rv", p, CH - 1)))
                    if g == 1:
                        pool.wait_ge(s_ds.sem, s_ds.at((p, QB, 0)))
                    elif p > 0:
                        pool.wait_ge(s_ds.sem, s_ds.at((p - 1, QB, 1)))
                    else:
                        wait_lo(pool, "norm", CH - 1)
                    nc.gpsimd.tensor_tensor(v_own[:], ret_v[:, QB, :].unsqueeze(1).to_broadcast([P, 4, P]),
                                            batch9[:, 4 * g:4 * g + 4].unsqueeze(2).to_broadcast([P, 4, P]),
                                            ALU.mult).then_inc(s_own.sem, s_own.mark((p, g)))
                elif kind == "score":
                    p, u = step[1:]
                    n = UNITS[u][2]
                    for h in range(2):
                        s = stop[:, (2 * u + h) % 4, 0:n]
                        pool.wait_ge(s_e.sem, s_e.at((p, u, h)))
                        nc.gpsimd.tensor_scalar(s, s, E_MAX, None, ALU.min).then_inc(s_min.sem, s_min.mark((p, u, h)))
                elif kind == "post":
                    c = step[1]
                    for k in range(KB):
                        if NEW_BY[k] == "pool":
                            residual(pool, nc.gpsimd, c, k)
                    if c == CH - 1:
                        weights_lo(B + 1)
                elif kind in ("norm", "split"):
                    for k in range(KB):
                        if LO_BY[kind][k] == "pool":
                            low_part(pool, nc.gpsimd, kind, step[1], k)
                elif kind == "sample_z":
                    p = step[1]
                    pool.wait_ge(s_e.sem, s_e.at((p, "sample")))
                    nc.gpsimd.tensor_scalar(stop9[:], stop9[:], E_MAX, None, ALU.min).then_inc(s_min.sem, s_min.mark((p, "sample")))

        layer.close()
        nums = [x.num for x in sems]
        assert sorted(nums) == list(range(min(nums), max(nums) + 1))
        nc.sync.sem_clear(range(min(nums), max(nums) + 1))
        nc.all_engine_barrier()
        loop.close()


def kernel(x_prompt, x_sample, state_ret, cache_k, cache_v, state_conv, page_table,
           norm_pre, w_in, ret_gn_w, sb_bias, conv_dw_w, conv_dw_b, conv_ln_w, conv_ln_b,
           conv_pw_w, w_out, norm_post):
    import concourse.bacc as bacc
    from concourse.bass_utils import run_bass_kernel_spmd

    L, B, D = DEPTH, DEC_BATCH, HEAD_DIM
    (x_prompt, x_sample, state_ret, cache_k, cache_v, state_conv, page_table, norm_pre, w_in, ret_gn_w, sb_bias,
     conv_dw_w, conv_dw_b, conv_ln_w, conv_ln_b, conv_pw_w, w_out, norm_post) = map(np.asarray, (
         x_prompt, x_sample, state_ret, cache_k, cache_v, state_conv, page_table, norm_pre, w_in, ret_gn_w, sb_bias,
         conv_dw_w, conv_dw_b, conv_ln_w, conv_ln_b, conv_pw_w, w_out, norm_post))

    def by_partition(a):
        return a.reshape(L, -1, P).transpose(0, 2, 1)

    x = np.concatenate([x_prompt.reshape(SEQ, D_MODEL), x_sample.reshape(NS, D_MODEL)])
    columns = [FIRST_COLUMN[name] + j for name, j in PROJ]
    w = np.concatenate([w_in.reshape(L, KB, P, -1, P)[:, :, :, columns], w_out.reshape(L, KB, P, KB, P)], 3)
    w = w.transpose(0, 3, 2, 1, 4).reshape(L * len(BLOCKS), P, KB * P)
    w = np.concatenate([w, np.zeros_like(w[:2])])
    states = np.zeros((L, PAIRS, 2, D, B, 2, D), np.float32)
    s = state_ret.reshape(L, B, PAIRS, 2, D, D)
    for h in range(2):
        states[:, :, h, :, :, h, :] = s[:, :, :, h].transpose(0, 2, 3, 1, 4)
    vec = np.concatenate([
        by_partition(norm_pre), by_partition(norm_post), by_partition(ret_gn_w),
        np.broadcast_to(sb_bias[:, None, :], (L, P, HEADS)),
        conv_dw_w.reshape(L, CONV_K, CB, P).transpose(0, 3, 2, 1).reshape(L, P, CB * CONV_K),
        by_partition(conv_dw_b), by_partition(conv_ln_w), by_partition(conv_ln_b),
        conv_pw_w.reshape(L, CB, P, CONV_W).transpose(0, 2, 1, 3).reshape(L, P, CB * CONV_W),
    ], 2)
    const, masks, turn, decay = shape_constants()
    ins = {
        "xT": x.reshape(NT, KB, P).transpose(2, 1, 0),
        "w": w,
        "vec": vec,
        "state_ret": states.reshape(L, PAIRS, P, B, P),
        "state_conv": state_conv.reshape(L, B, HIST, CB, P).transpose(0, 4, 3, 1, 2),
        "cache_k": cache_k.reshape(L, N_POOL, PAGE, PAIRS, P).transpose(0, 1, 3, 4, 2),
        "cache_v": cache_v.reshape(L, N_POOL, PAGE, PAIRS, P).transpose(0, 1, 3, 2, 4),
        "page_table": page_table.reshape(1, B * N_PAGES),
        "const": const, "masks": masks, "turn": turn, "decay": decay,
    }
    ins = {k: np.ascontiguousarray(v) for k, v in ins.items()}
    outs = {
        "yT": (P, KB, NT), "state_p": (L, PAIRS, P, P), "state_s": (L, PAIRS, P, B, P),
        "k_rows": (L, PAIRS, P, NT), "v_rows": (L, PAIRS, P, NT),
        "conv_p": (L, P, CB, HIST), "conv_s": (L, P, CB, B, HIST),
    }

    def assemble(counts):
        nc = bacc.Bacc("TRN2", target_bir_lowering=False, num_devices=1, dynamic_dma_scratch_size=1024)
        io = {k: nc.dram_tensor(f"in_{k}", v.shape, mybir.dt.from_np(v.dtype), kind="ExternalInput").ap() for k, v in ins.items()}
        io |= {k: nc.dram_tensor(f"out_{k}", v, F32, kind="ExternalOutput").ap() for k, v in outs.items()}
        build(nc, io, counts)
        return nc

    counts = {}
    assemble(counts)
    nc = assemble(counts)
    r = run_bass_kernel_spmd(nc, [{f"in_{k}": v for k, v in ins.items()}], core_ids=[0]).results[0]
    got = {k: np.asarray(r[f"out_{k}"]) for k in outs}

    y = got["yT"].transpose(2, 1, 0).reshape(NT, D_MODEL)
    sp = got["state_p"].reshape(L, PAIRS, 2, D, 2, D)
    sp = np.stack([sp[:, :, h, :, h, :] for h in range(2)], 2).reshape(L, 1, HEADS, D, D)
    ss = got["state_s"].reshape(L, PAIRS, 2, D, B, 2, D)
    ss = np.stack([ss[:, :, h, :, :, h, :] for h in range(2)], 2)
    ss = ss.transpose(0, 4, 1, 2, 3, 5).reshape(L, B, HEADS, D, D)

    def rows(a):
        a = a.transpose(0, 3, 1, 2).reshape(L, NT, HEADS, D)
        return a[:, :SEQ].reshape(L, 1, SEQ, HEADS, D), a[:, SEQ:].reshape(L, B, DEC_SEQ, HEADS, D)

    kp, ks = rows(got["k_rows"])
    vp, vs = rows(got["v_rows"])
    cp = got["conv_p"].transpose(0, 3, 2, 1).reshape(L, 1, HIST, CONV_W)
    cv = got["conv_s"].transpose(0, 3, 4, 2, 1).reshape(L, B, HIST, CONV_W)
    return (y[:SEQ].reshape(1, SEQ, D_MODEL), y[SEQ:].reshape(B, DEC_SEQ, D_MODEL), sp, ss, kp, vp, ks, vs, cp, cv)
```
